# Optimizing a Trainium2 kernel written in Bass

```python
import math
import jax, jax.numpy as jnp
from jax import lax
import numpy as np

D_MODEL = 1024
BATCH = 1
SEQ = 256
DEPTH = 2

CHUNK = 64
N_MIXERS = 2
D_FF = 2816
PLE_DIM = 256
S5_GROUP = 16
S5_GROUPS = D_MODEL // S5_GROUP
S5_STATE = 64
SB_HEAD_DIM = 64
SB_HEADS = D_MODEL // SB_HEAD_DIM
Q_BLOCK = 128
N_A = (DEPTH + 1) // 2
N_B = DEPTH // 2
EPS = 1e-6
DT_MIN = 1e-3
DT_MAX = 1e-1

kernel_name = 'hybrid_s5_stickbreaking_macaron'

def rmsnorm(x, g):
    xf = x.astype(jnp.float32)
    y = xf * lax.rsqrt(jnp.mean(xf * xf, axis=-1, keepdims=True) + EPS)
    return (y * g.astype(jnp.float32)).astype(x.dtype)

def swiglu(x, w1, w3, w2):
    return (jax.nn.silu(x @ w1) * (x @ w3)) @ w2

def _cmul(ar, ai, br, bi):
    return ar * br - ai * bi, ar * bi + ai * br

def _s5_combine(e1, e2):
    a1r, a1i, b1r, b1i = e1
    a2r, a2i, b2r, b2i = e2
    ar, ai = _cmul(a2r, a2i, a1r, a1i)
    cr, ci = _cmul(a2r, a2i, b1r, b1i)
    return ar, ai, cr + b2r, ci + b2i

def s5_mixer(h, w_in, a_re, a_im, log_dt, b_re, b_im, c_re, c_im, d_skip, w_glu):
    bsz, seq_len, _ = h.shape
    f32 = jnp.float32
    u = h @ w_in
    ug = u.astype(f32).reshape(bsz, seq_len, S5_GROUPS, S5_GROUP)
    lam_re = jnp.minimum(a_re.astype(f32), -1e-4)
    lam_im = a_im.astype(f32)
    dt = jnp.exp(log_dt.astype(f32))[:, None]
    mag = jnp.exp(lam_re * dt)
    abar_re = mag * jnp.cos(lam_im * dt)
    abar_im = mag * jnp.sin(lam_im * dt)
    den = lam_re * lam_re + lam_im * lam_im
    nr = abar_re - 1.0
    ni = abar_im
    fr = (nr * lam_re + ni * lam_im) / den
    fi = (ni * lam_re - nr * lam_im) / den
    bre = b_re.astype(f32)
    bim = b_im.astype(f32)
    bbar_re = fr[..., None] * bre - fi[..., None] * bim
    bbar_im = fr[..., None] * bim + fi[..., None] * bre
    bu_re = jnp.einsum('blgh,gph->blgp', ug, bbar_re)
    bu_im = jnp.einsum('blgh,gph->blgp', ug, bbar_im)
    a_seq_re = jnp.broadcast_to(abar_re, (1, seq_len, S5_GROUPS, S5_STATE))
    a_seq_im = jnp.broadcast_to(abar_im, (1, seq_len, S5_GROUPS, S5_STATE))
    _, _, s_re, s_im = lax.associative_scan(
        _s5_combine, (a_seq_re, a_seq_im, bu_re, bu_im), axis=1)
    y = (jnp.einsum('blgp,ghp->blgh', s_re, c_re.astype(f32))
         - jnp.einsum('blgp,ghp->blgh', s_im, c_im.astype(f32)))
    y = y.reshape(bsz, seq_len, D_MODEL) + d_skip.astype(f32) * u.astype(f32)
    z = jax.nn.gelu(y).astype(h.dtype)
    z_out, z_gate = jnp.split(z @ w_glu, 2, axis=-1)
    return z_out * jax.nn.sigmoid(z_gate)

def stick_breaking_mixer(h, w_qkv, w_o):
    bsz, seq_len, _ = h.shape
    qkv = (h @ w_qkv).reshape(bsz, seq_len, 3, SB_HEADS, SB_HEAD_DIM)
    q = qkv[:, :, 0].transpose(0, 2, 1, 3)
    k = qkv[:, :, 1].transpose(0, 2, 1, 3)
    v = qkv[:, :, 2].transpose(0, 2, 1, 3)
    scale = SB_HEAD_DIM ** -0.5
    outs = []
    for blk in range(seq_len // Q_BLOCK):
        start = blk * Q_BLOCK
        end = start + Q_BLOCK
        qb = q[:, :, start:end]
        kb = k[:, :, :end]
        vb = v[:, :, :end]
        z = jnp.einsum('bhqd,bhkd->bhqk', qb, kb).astype(jnp.float32) * scale
        t_pos = start + jnp.arange(Q_BLOCK)[:, None]
        s_pos = jnp.arange(end)[None, :]
        strict = s_pos < t_pos
        log_keep = jnp.where(strict, jax.nn.log_sigmoid(-z), 0.0)
        later = lax.cumsum(log_keep, axis=3, reverse=True) - log_keep
        att = jnp.where(strict, jnp.exp(jax.nn.log_sigmoid(z) + later), 0.0)
        outs.append(jnp.einsum('bhqk,bhkd->bhqd', att.astype(vb.dtype), vb))
    o = jnp.concatenate(outs, axis=2).transpose(0, 2, 1, 3).reshape(bsz, seq_len, D_MODEL)
    return o @ w_o

def setup_inputs(seed: int = 0) -> dict:
    key = jax.random.key(seed)
    ks = jax.random.split(key, 32)
    f32 = jnp.float32
    nrm = lambda k, shape, s: jax.random.normal(k, shape, f32) * s
    gain = lambda k, shape: 1.0 + 0.02 * jax.random.normal(k, shape, f32)
    d_in = D_MODEL ** -0.5
    a_im0 = math.pi * jnp.arange(S5_STATE, dtype=f32)
    return {
        'x': jax.random.normal(ks[0], (BATCH, SEQ, D_MODEL), f32),
        'p': jax.random.normal(ks[1], (DEPTH, BATCH, SEQ, PLE_DIM), f32),
        'ffn1_norm': gain(ks[2], (DEPTH, D_MODEL)),
        'ffn1_w1': nrm(ks[3], (DEPTH, D_MODEL, D_FF), d_in),
        'ffn1_w3': nrm(ks[4], (DEPTH, D_MODEL, D_FF), d_in),
        'ffn1_w2': nrm(ks[5], (DEPTH, D_FF, D_MODEL), D_FF ** -0.5),
        'mix_norm': gain(ks[6], (DEPTH, D_MODEL)),
        'ffn2_norm': gain(ks[7], (DEPTH, D_MODEL)),
        'ffn2_w1': nrm(ks[8], (DEPTH, D_MODEL, D_FF), d_in),
        'ffn2_w3': nrm(ks[9], (DEPTH, D_MODEL, D_FF), d_in),
        'ffn2_w2': nrm(ks[10], (DEPTH, D_FF, D_MODEL), D_FF ** -0.5),
        'ple_norm': gain(ks[11], (DEPTH, D_MODEL)),
        'ple_proj': nrm(ks[12], (DEPTH, PLE_DIM, D_MODEL), PLE_DIM ** -0.5),
        'ple_gate': nrm(ks[13], (DEPTH, D_MODEL, D_MODEL), d_in),
        's5_w_in': nrm(ks[14], (N_A, D_MODEL, D_MODEL), d_in),
        's5_a_re': -0.5 + 0.01 * jax.random.normal(ks[15], (N_A, S5_GROUPS, S5_STATE), f32),
        's5_a_im': a_im0 + 0.01 * jax.random.normal(ks[16], (N_A, S5_GROUPS, S5_STATE), f32),
        's5_log_dt': jax.random.uniform(ks[17], (N_A, S5_GROUPS), f32,
                                        math.log(DT_MIN), math.log(DT_MAX)),
        's5_b_re': nrm(ks[18], (N_A, S5_GROUPS, S5_STATE, S5_GROUP), (2 * S5_GROUP) ** -0.5),
        's5_b_im': nrm(ks[19], (N_A, S5_GROUPS, S5_STATE, S5_GROUP), (2 * S5_GROUP) ** -0.5),
        's5_c_re': nrm(ks[20], (N_A, S5_GROUPS, S5_GROUP, S5_STATE), S5_STATE ** -0.5),
        's5_c_im': nrm(ks[21], (N_A, S5_GROUPS, S5_GROUP, S5_STATE), S5_STATE ** -0.5),
        's5_d': jax.random.normal(ks[22], (N_A, D_MODEL), f32),
        's5_w_glu': nrm(ks[23], (N_A, D_MODEL, 2 * D_MODEL), d_in),
        'sb_w_qkv': nrm(ks[24], (N_B, D_MODEL, 3 * D_MODEL), d_in),
        'sb_w_o': nrm(ks[25], (N_B, D_MODEL, D_MODEL), d_in),
        'final_norm': gain(ks[26], (D_MODEL,)),
    }

def reference(x, p, ffn1_norm, ffn1_w1, ffn1_w3, ffn1_w2, mix_norm, ffn2_norm,
              ffn2_w1, ffn2_w3, ffn2_w2, ple_norm, ple_proj, ple_gate,
              s5_w_in, s5_a_re, s5_a_im, s5_log_dt, s5_b_re, s5_b_im,
              s5_c_re, s5_c_im, s5_d, s5_w_glu, sb_w_qkv, sb_w_o, final_norm):
    h = x
    for i in range(DEPTH):
        h = h + 0.5 * swiglu(rmsnorm(h, ffn1_norm[i]), ffn1_w1[i], ffn1_w3[i], ffn1_w2[i])
        hn = rmsnorm(h, mix_norm[i])
        j = i // N_MIXERS
        if i % N_MIXERS == 0:
            m = s5_mixer(hn, s5_w_in[j], s5_a_re[j], s5_a_im[j], s5_log_dt[j],
                         s5_b_re[j], s5_b_im[j], s5_c_re[j], s5_c_im[j],
                         s5_d[j], s5_w_glu[j])
        else:
            m = stick_breaking_mixer(hn, sb_w_qkv[j], sb_w_o[j])
        h = h + m
        h = h + 0.5 * swiglu(rmsnorm(h, ffn2_norm[i]), ffn2_w1[i], ffn2_w3[i], ffn2_w2[i])
        gate = jax.nn.sigmoid(rmsnorm(h, ple_norm[i]) @ ple_gate[i])
        h = h + (p[i].astype(h.dtype) @ ple_proj[i]) * gate
    return rmsnorm(h, final_norm)


_drawn_inputs = setup_inputs


def setup_inputs(seed=0):
    import zlib

    import numpy as np

    out = dict(_drawn_inputs(seed))
    spreads = {}
    factors = {'ffn1_norm': 5.244,
     'mix_norm': 12.838,
     'ffn2_norm': 6.251,
     'ple_norm': 64.0,
     's5_a_re': 64.0,
     's5_b_re': 3.119,
     's5_b_im': 3.188,
     's5_c_re': 3.149,
     's5_c_im': 3.158,
     'final_norm': 7.837}
    for name, (base, spread) in spreads.items():
        noise = np.random.default_rng([zlib.crc32(name.encode()), seed]).standard_normal(out[name].shape)
        drawn = base * np.exp(spread * noise) if base else spread * noise
        out[name] = __import__('jax').numpy.asarray(drawn.astype(out[name].dtype))
    for name, factor in factors.items():
        out[name] = (out[name] * factor).astype(out[name].dtype)
    return out
```

```python
from contextlib import ExitStack

import concourse.bass as bass
from concourse import mybir

F32 = mybir.dt.float32
F32R = mybir.dt.float32r
BF16 = mybir.dt.bfloat16
ALU = mybir.AluOpType
ACT = mybir.ActivationFunctionType

P = 128
EPS = 1e-6
HALF = [0, 1, 1, 0, 1, 0, 1, 0, 1, 0]
TURN = 6.28125, 0.0019354820251464844, -1.7484556e-07
ROUND = 12582912.0


class Stage:

    def __init__(self, kind, layer, index, first_chunk, operand, ffn, gates, ples):
        self.kind, self.layer = kind, layer
        self.v = index
        self.n0 = first_chunk
        self.u = operand
        self.f = ffn
        self.e = gates
        self.q = ples


CHUNKS = {"ffn1": 66, "ffn2": 66, "s5": 24, "attn": 32, "ple": 10, "final": 0}
SETS = {"ffn1": 1, "ffn2": 1, "s5": 2, "attn": 2, "ple": 1, "final": 0}
KINDS = [("ffn1", 0), ("s5", 0), ("ffn2", 0), ("ple", 0), ("ffn1", 1), ("attn", 1), ("ffn2", 1), ("ple", 1), ("final", 1)]


def plan(kinds):
    stages, n, u, f, e, q = [], 0, 0, 0, 0, 0
    for index, (kind, layer) in enumerate(kinds):
        stages.append(Stage(kind, layer, index, n, u, f, e, q))
        e, q = e + 4 * (kind in ("s5", "ple")), q + (kind == "ple")
        n, u, f = n + CHUNKS[kind], u + SETS[kind], f + (kind[:3] == "ffn")
    return stages, n


def hybrid_trunk(nc, x, p, ffn1_norm, ffn1_w1, ffn1_w3, ffn1_w2, mix_norm, ffn2_norm, ffn2_w1, ffn2_w3, ffn2_w2,
                 ple_norm, ple_proj, ple_gate, s5_w_in, s5_a_re, s5_a_im, s5_log_dt, s5_b_re, s5_b_im,
                 s5_c_re, s5_c_im, s5_d, s5_w_glu, sb_w_qkv, sb_w_o, final_norm, out, kinds=KINDS):
    _, T, D = x.shape
    DFF = ffn1_w1.shape[2]
    KD = D // P
    TB = T // P
    NG = DFF // 256
    NB = KD // 2
    RING = 3
    stages, n_chunks = plan(kinds)
    NH, DH = 16, 64
    SCALE = DH ** -0.5
    MASKED = -1e30
    H, S = s5_b_re.shape[3], s5_b_re.shape[2]
    NQ = D // (2 * H)
    TAU, NC = 4, T // 4
    QG = 8
    STEPS = NH + 2
    norm_rows = {"ffn1": ffn1_norm, "ffn2": ffn2_norm, "s5": mix_norm, "attn": mix_norm, "ple": ple_norm}
    ffn_weights = {"ffn1": (ffn1_w1, ffn1_w3, ffn1_w2), "ffn2": (ffn2_w1, ffn2_w3, ffn2_w2)}

    with ExitStack() as ctx:
        top = [-(-nc.sbuf_base // 32) * 32]
        spot = {}

        def sb(name, shape, dt=F32, at=None):
            size = 2 if dt == BF16 else 4
            for d in shape[1:]:
                size *= d
            if at is None:
                at = top[0]
                top[0] += -(-size // 32) * 32
            spot[name] = at
            return nc.alloc_sbuf_tensor_at(name, shape, dt, offset=at)

        def sem(name):
            return ctx.enter_context(nc.semaphore(name))

        raw = sb("raw", [P, RING, 1024])
        w_hi = sb("w_hi", [P, RING, 1024], F32R)
        w_lo = sb("w_lo", [P, RING, 1024], F32R)
        xT = sb("xT", [P, KD, T])
        op_hi = sb("op_hi", [P, 2, KD, T], F32R)
        op_lo = sb("op_lo", [P, 2, KD, T], F32R)
        squares = sb("squares", [P, 2, 2, T])
        square_sum = sb("square_sum", [P, 2, T])
        mean_sq = sb("mean_sq", [P, TB])
        r_col = sb("r_col", [P, TB])
        minus_half = sb("minus_half", [P, TB])
        r_diag = sb("r_diag", [P, TB, P])
        r_row = sb("r_row", [P, T])
        gain_rows = sb("gain_rows", [9 * KD, P])
        gain = sb("gain", [P, 9 * KD])
        a_n = sb("a_n", [P, 2, T])
        b_n = sb("b_n", [P, 2, T])
        silu = sb("silu", [P, 2, T])
        prod = sb("prod", [P, 2, T])
        g_hi = sb("g_hi", [P, 2, 2, T], F32R)
        g_lo = sb("g_lo", [P, 2, 2, T], F32R)
        rows_in = sb("rows_in", [P, TB, D], at=spot["g_hi"])
        p_rows = sb("p_rows", [P, TB, T])
        s5_rows = sb("s5_rows", [NQ, 4, P])
        skip = sb("skip", [2 * H, NQ, 2 * H], at=spot["p_rows"])
        p_hi = sb("p_hi", [P, 2, T], F32R)
        p_lo = sb("p_lo", [P, 2, T], F32R)
        minus_tri = sb("minus_tri", [P, P])
        minus_ones = sb("minus_ones", [P, P])
        ident_b = sb("ident_b", [P, P], BF16)
        masked_b = sb("masked_b", [P, P], BF16)
        ident = sb("ident", [P, P])
        ones = sb("ones", [P, P])
        half_pi = sb("half_pi", [P, 1])
        zeros_b = sb("zeros_b", [P, P], BF16)

        half_1 = spot["op_hi"] + KD * T * 4, spot["op_lo"] + KD * T * 4
        mixer = top[0]
        w_in_state = sb("w_in_state", [P, 2, NQ, TAU, 2, H])
        w_state_out = sb("w_state_out", [P, 2, NQ, TAU + 1, 2, H])
        turn_cos = sb("turn_cos", [P, NQ, NC])
        turn_sin = sb("turn_sin", [P, NQ, NC])
        decay = sb("decay", [P, NQ, NC])
        within = [sb(f"within{i}", [P, NQ // 2, P], at=spot[o]) for i, o in enumerate(("op_hi", "op_lo"))]
        u_steps = sb("u_steps", [P, NQ, NC], at=spot["g_hi"])
        b_in = sb("b_in", [P, 2, NQ, H], at=half_1[0])
        c_in = sb("c_in", [P, 2, NQ, H], at=half_1[0] + 2 * NQ * H * 4)
        c_rows = sb("c_rows", [P, 2, KD, S], at=half_1[1])
        tmp = sb("tmp", [P, 2, NQ * 32], at=half_1[1])
        small = sb("small", [P, 32, NQ], at=spot["p_hi"])
        scratch = sb("scratch", [P, 2, 512], at=spot["p_hi"])
        dt_rows = sb("dt_rows", [NQ, 2])

        kT = sb("kT", [P, KD, T], at=mixer)
        qT = sb("qT", [P, KD, T], at=mixer + 4 * KD * T)
        val = sb("val", [P, TB, D], at=mixer + 8 * KD * T)
        HW = T + P
        z_abs, z_exp, z_log, drop, att = (sb(name, [P, 2, HW], at=mixer + 12 * KD * T + 8 * HW * i)
                                           for i, name in enumerate(("z_abs", "z_exp", "z_log", "drop", "att")))
        assert top[0] <= nc.sbuf_usable_end

        acc = [ctx.enter_context(nc.psum_tensor(f"acc{b}", [P, 2, T], F32)) for b in range(NB)]
        bank = [ctx.enter_context(nc.psum_tensor(f"bank{b}", [P, 2, T], F32)) for b in range(2)]
        stat = ctx.enter_context(nc.psum_tensor("stat", [P, 512], F32))
        misc = ctx.enter_context(nc.psum_tensor("misc", [P, 512], F32))

        raw_landed = [sem(f"raw_landed{s}") for s in range(RING)]
        hi_done, lo_done, pe_done = sem("hi_done"), sem("lo_done"), sem("pe_done")
        rows_landed = sem("rows_landed")
        gains_landed = sem("gains_landed")
        consts_ready = sem("consts_ready")
        ident_zeroed = sem("ident_zeroed")
        x_turned = sem("x_turned")
        p_landed = sem("p_landed")
        p_turned = sem("p_turned")
        p_hi_done, p_lo_done = sem("p_hi_done"), sem("p_lo_done")
        gate_taken, gate_ready, gated = sem("gate_taken"), sem("gate_ready"), sem("gated")
        masks_made = sem("masks_made")
        s5_landed, rows_spread, s5_turned, small_ready = (sem(n) for n in ("s5_landed", "rows_spread", "s5_turned", "small_ready"))
        c_turned, c_ready = sem("c_turned"), sem("c_ready")
        angles_ready, phasors_ready = sem("angles_ready"), sem("phasors_ready")
        pool_step = sem("pool_step")
        weights_ready = sem("weights_ready")
        within_zeroed = sem("within_zeroed")
        block_done, block_skip, block_first, block_taken = (sem(n) for n in ("block_done", "block_skip", "block_first", "block_taken"))
        turned_done, turned_taken = sem("turned_done"), sem("turned_taken")
        u_scaled, u_placed = sem("u_scaled"), sem("u_placed")
        s_in_done, y_done = sem("s_in_done"), sem("y_done")
        dve_step = sem("dve_step")
        scanned, state_re, state_im = sem("scanned"), sem("state_re"), sem("state_im")
        imag_step = sem("imag_step")
        gelu_done = sem("gelu_done")
        bank_taken = sem("bank_taken")
        z_done, abs_done, exp_done, log_done = sem("z_done"), sem("abs_done"), sem("exp_done"), sem("log_done")
        drop_done, drop_masked = sem("drop_done"), sem("drop_masked")
        exponent_done, att_done, o_done = sem("exponent_done"), sem("att_done"), sem("o_done")
        gain_turned = sem("gain_turned")
        gain_ready = sem("gain_ready")
        acc_done = sem("acc_done")
        x_new = sem("x_new")
        op_hi_done, op_lo_done = sem("op_hi_done"), sem("op_lo_done")
        squared = sem("squared")
        squares_used = sem("squares_used")
        sum_ready = sem("sum_ready")
        sum_col = sem("sum_col")
        mean_ready = sem("mean_ready")
        r_ready = sem("r_ready")
        diag_ready = sem("diag_ready")
        r_spread = sem("r_spread")
        r_row_ready = sem("r_row_ready")
        a_taken, b_taken = sem("a_taken"), sem("b_taken")
        silu_done, prod_done = sem("silu_done"), sem("prod_done")
        g_hi_done, g_lo_done = sem("g_hi_done"), sem("g_lo_done")
        out_turned = sem("out_turned")
        out_rows = sem("out_rows")
        stored = sem("stored")
        scaled = sem("scaled")

        def a_chunk(w, half, col):
            return w[half * 512:(half + 1) * 512, col].rearrange("(k p) c -> p k c", p=P)

        def slot_a(buf, n):
            return buf[:, n % RING, :].rearrange("p (k c) -> p k c", k=4)

        OUT_ORDER = [(0, 0), (1, 0), (0, 1), (1, 1), (2, 0), (2, 1), (3, 0), (3, 1)]

        def step_chunk(st, s):
            return st.n0 + 12 + s if s < 14 else None

        block = ctx.enter_context(nc.Block())

        @block.sync
        def _(sp):
            def load(n, slot, src, shape_k):
                if not isinstance(n, int) or n >= RING:
                    sp.wait_ge(lo_done, n - (RING - 1))
                dst = raw[:, slot, :]
                if shape_k:
                    dst = dst.rearrange("p (k c) -> p k c", k=4)
                sp.dma_start(dst, src).then_inc(raw_landed[slot], 16)

            def load_ffn(st):
                w1, w3, w2 = (w[st.layer] for w in ffn_weights[st.kind])

                def pair(w, n, s, g):
                    for half in range(2):
                        load(n + half, (s + half) % RING, a_chunk(w, half, bass.ds(g * 256, 256)), True)

                def down(n, s, g):
                    for j in range(2):
                        load(n + j, (s + j) % RING, w2[bass.ds(g * 256 + j * P, P), :], False)
                pair(w1, st.n0, st.n0, 0)
                pair(w3, st.n0 + 2, st.n0 + 2, 0)
                with sp.Fori(1, NG) as g:
                    n, s = g * 6 + (st.n0 - 2), st.n0 + 4
                    pair(w1, n, s, g)
                    pair(w3, n + 2, s + 2, g)
                    down(n + 4, s + 4, g - 1)
                down(st.n0 + 6 * NG - 2, st.n0 + 6 * NG - 2, NG - 1)

            def load_group(n, w, col):
                for half in range(2):
                    load(n + half, (n + half) % RING, a_chunk(w, half, slice(col, col + 256)), True)

            def load_ple(st):
                for kt in range(2):
                    load(st.n0 + kt, (st.n0 + kt) % RING, ple_proj[st.layer, kt * P:(kt + 1) * P, :], False)
                for j in range(NB):
                    load_group(st.n0 + 2 + 2 * j, ple_gate[st.layer], 256 * j)

            def load_s5(st):
                for j in range(NB):
                    load_group(st.n0 + 2 * j, s5_w_in[0], 256 * j)
                for j in range(NB):
                    load_group(st.n0 + 8 + 4 * j, s5_w_glu[0], D + 256 * j)
                    load_group(st.n0 + 10 + 4 * j, s5_w_glu[0], 256 * j)

            def load_attn(st):
                w = sb_w_qkv[0]
                for j in range(NB):
                    load_group(st.n0 + 2 * j, w, 2 * D + 256 * j)
                for j in range(NB):
                    load_group(st.n0 + 8 + 4 * j, w, D + 256 * j)
                    load_group(st.n0 + 10 + 4 * j, w, 256 * j)
                for i, (j, half) in enumerate(OUT_ORDER):
                    n = st.n0 + 24 + i
                    load(n, n % RING, a_chunk(sb_w_o[0], half, slice(256 * j, 256 * j + 256)), True)

            for st, nxt in zip(stages, stages[1:] + [None]):
                if nxt is not None and nxt.kind == "ple":
                    if any(o.kind == "s5" for o in stages):
                        sp.wait_ge(block_skip, 8)
                    if nxt.q:
                        sp.wait_ge(p_turned, nxt.q)
                    sp.dma_start(p_rows[:, :, :],
                                 p[nxt.layer, 0].rearrange("(b p) c -> p b c", p=P)).then_inc(p_landed, 16)
                if st.kind[:3] == "ffn":
                    load_ffn(st)
                if st.kind == "s5":
                    load_s5(st)
                if st.kind == "ple":
                    load_ple(st)
                if st.kind == "attn":
                    load_attn(st)
                if st.kind == "final":
                    for tb in range(TB):
                        sp.wait_ge(out_rows, 2 * (tb + 1))
                        sp.dma_start(out[0, tb * P:(tb + 1) * P, :], rows_in[:, tb, :]).then_inc(stored, 16)
                    sp.wait_ge(stored, 16 * TB)

        @block.gpsimd
        def _(pool):
            pool.memset(ident[:, :], 0.0).then_inc(ident_zeroed, 1)
            pool.memset(ones[:, :], 1.0).then_inc(consts_ready, 1)
            pool.memset(minus_half[:, :], -0.5).then_inc(consts_ready, 1)
            pool.memset(zeros_b[:, :], 0.0).then_inc(consts_ready, 1)
            pool.memset(half_pi[:, :], 1.5707963267948966).then_inc(consts_ready, 1)
            pool.wait_ge(ident_zeroed, 1)
            pool.affine_select(out=ident[:, :], in_=ident[:, :], compare_op=ALU.not_equal, fill=1.0, base=0,
                               pattern=[[-1, P]], channel_multiplier=1).then_inc(consts_ready, 1)

            def norm(v):
                sq = squares_used
                pool.wait_ge(squared, 4 * v + 2)
                if v:
                    pool.wait_ge(sum_col, v)
                pool.tensor_tensor(square_sum[:, :, :], squares[:, 0], squares[:, 1], ALU.add).then_inc(sq, 2)
                for b in (2, 3):
                    pool.wait_ge(sq, 4 * v + b)
                    pool.wait_ge(squared, 4 * v + b + 1)
                    pool.tensor_tensor(square_sum[:, :, :], square_sum[:, :, :], squares[:, b % 2], ALU.add)\
                        .then_inc(sq, 1)
                pool.wait_ge(sq, 4 * v + 4)
                pool.tensor_tensor(square_sum[:, 0], square_sum[:, 0], square_sum[:, 1], ALU.add).then_inc(sum_ready, 1)
                pool.wait_ge(mean_ready, v + 1)
                pool.tensor_tensor(r_col[:, :], mean_sq[:, :], minus_half[:, :], ALU.pow).then_inc(r_ready, 1)
            pool.wait_ge(consts_ready, 5)
            pool.memset(minus_tri[:, :], -1.0).then_inc(masks_made, 1)
            pool.memset(minus_ones[:, :], -1.0).then_inc(masks_made, 1)
            pool.memset(ident_b[:, :], 0.0).then_inc(masks_made, 1)
            pool.memset(masked_b[:, :], 0.0).then_inc(masks_made, 1)
            pool.wait_ge(masks_made, 4)
            pool.affine_select(out=minus_tri[:, :], in_=minus_tri[:, :], compare_op=ALU.is_ge, fill=0.0, base=0,
                               pattern=[[-1, P]], channel_multiplier=1).then_inc(masks_made, 1)
            pool.affine_select(out=ident_b[:, :], in_=ident_b[:, :], compare_op=ALU.not_equal, fill=1.0, base=0,
                               pattern=[[-1, P]], channel_multiplier=1).then_inc(masks_made, 1)
            pool.affine_select(out=masked_b[:, :], in_=masked_b[:, :], compare_op=ALU.is_gt, fill=MASKED, base=0,
                               pattern=[[1, P]], channel_multiplier=-1).then_inc(masks_made, 1)

            def attention():
                for h in range(NH):
                    pool.wait_ge(drop_done, h + 1)
                    for c in (0, T):
                        d = drop[:, h % 2, c:c + P]
                        pool.affine_select(out=d, in_=d, compare_op=ALU.is_gt, fill=0.0, base=0,
                                           pattern=[[1, P]], channel_multiplier=-1).then_inc(drop_masked, 1)

            links = [0]

            def link(ins):
                links[0] += 1
                ins.then_inc(pool_step, 1)
                pool.wait_ge(pool_step, links[0])

            def tt(o, a, b, op=ALU.mult):
                link(pool.tensor_tensor(o, a, b, op))

            def ts(o, a, m, b):
                link(pool.tensor_scalar(o, a, m, b, ALU.mult, ALU.add))

            def sm(i):
                return small[:, i, :]

            def s5_parameters():
                lam_re, lam_im, dt, skip_col, decay_log, angle, mag, cos, sin, fr, fi, t0, t1, t2 = range(14)
                A, F, E, M4 = 14, 22, 30, mag
                link(pool.memset(w_in_state[:, :, :, :, :, :], 0.0))
                link(pool.memset(w_state_out[:, :, :, :, :, :], 0.0))
                pool.wait_ge(small_ready, 4)
                pool.wait_ge(c_ready, 2)
                tt(skip[:, :, :], ident[0:32, 0:32].unsqueeze(1).broadcast_to([32, NQ, 32]),
                   sm(skip_col)[0:32].unsqueeze(2).broadcast_to([32, NQ, 32]))
                link(pool.tensor_scalar(sm(lam_re), sm(lam_re), -1e-4, None, ALU.min))
                tt(sm(decay_log), sm(lam_re), sm(dt))
                tt(sm(angle), sm(lam_im), sm(dt))
                ts(sm(t0), sm(angle), 1.0 / (2 * 3.141592653589793), ROUND)
                link(pool.tensor_scalar(sm(t0), sm(t0), -ROUND, None, ALU.add))
                for part in TURN:
                    link(pool.tensor_scalar(sm(t1), sm(t0), -part, None, ALU.mult))
                    tt(sm(angle), sm(angle), sm(t1), ALU.add)
                pool.tensor_scalar(sm(angle), sm(angle), 3.1415925, -3.1415925, ALU.min, ALU.max).then_inc(angles_ready, 1)
                tt(sm(t0), sm(lam_re), sm(lam_re))
                tt(sm(t1), sm(lam_im), sm(lam_im))
                tt(sm(t0), sm(t0), sm(t1), ALU.add)
                link(pool.memset(sm(t1), -1.0))
                tt(sm(t2), sm(t0), sm(t1), ALU.pow)
                pool.wait_ge(phasors_ready, 3)

                def product(o_re, o_im, a_re, a_im, b_re, b_im, x, y):
                    tt(x, a_re, b_re)
                    tt(y, a_im, b_im)
                    tt(o_re, x, y, ALU.subtract)
                    tt(x, a_re, b_im)
                    tt(y, a_im, b_re)
                    tt(o_im, x, y, ALU.add)

                a_re = [None] + [sm(A + j) for j in range(4)]
                a_im = [None] + [sm(A + 4 + j) for j in range(4)]
                tt(a_re[1], sm(mag), sm(cos))
                tt(a_im[1], sm(mag), sm(sin))
                link(pool.tensor_scalar(sm(decay_log), a_re[1], -1.0, None, ALU.add))
                tt(sm(t0), sm(decay_log), sm(lam_re))
                tt(sm(t1), a_im[1], sm(lam_im))
                tt(sm(fr), sm(t0), sm(t1), ALU.add)
                tt(sm(t0), a_im[1], sm(lam_re))
                tt(sm(t1), sm(decay_log), sm(lam_im))
                tt(sm(fi), sm(t0), sm(t1), ALU.subtract)
                tt(sm(F + 3), sm(fr), sm(t2))
                tt(sm(F + 7), sm(fi), sm(t2))
                for j in (2, 3, 4):
                    product(a_re[j], a_im[j], a_re[j - 1], a_im[j - 1], a_re[1], a_im[1], sm(t0), sm(t1))
                for tau in range(TAU - 1):
                    j = TAU - 1 - tau
                    product(sm(F + tau), sm(F + 4 + tau), a_re[j], a_im[j], sm(F + 3), sm(F + 7), sm(t0), sm(t1))
                for _ in range(2):
                    tt(sm(mag), sm(mag), sm(mag))

                def over(x, n):
                    return x.unsqueeze(2).broadcast_to([P, NQ, n])
                xy = [tmp[:, i, 0:NQ * H].rearrange("p (q h) -> p q h", h=H) for i in range(2)]

                def both(o, part, j, op):
                    for e in range(2):
                        r = slice(64 * e, 64 * e + 64)
                        tt(o[r, part, :, j, e, :], xy[0][r], xy[1][r], op)
                for tau in range(TAU):
                    f_re, f_im = over(sm(F + tau), H), over(sm(F + 4 + tau), H)
                    tt(xy[0], f_re, b_in[:, 0])
                    tt(xy[1], f_im, b_in[:, 1])
                    both(w_in_state, 0, tau, ALU.subtract)
                    tt(xy[0], f_re, b_in[:, 1])
                    tt(xy[1], f_im, b_in[:, 0])
                    both(w_in_state, 1, tau, ALU.add)
                for e in range(2):
                    r = slice(64 * e, 64 * e + 64)
                    for part in range(2):
                        link(pool.tensor_copy(w_state_out[r, part, :, 0, e, :], c_in[r, part]))
                for j in range(1, TAU + 1):
                    p_re, p_im = over(a_re[j], H), over(a_im[j], H)
                    tt(xy[0], c_in[:, 0], p_re)
                    tt(xy[1], c_in[:, 1], p_im)
                    both(w_state_out, 0, j, ALU.add)
                    tt(xy[0], c_in[:, 1], p_re)
                    tt(xy[1], c_in[:, 0], p_im)
                    both(w_state_out, 1, j, ALU.subtract)
                e_re, e_im = sm(E), sm(E + 1)
                product(e_re, e_im, sm(cos), sm(sin), sm(cos), sm(sin), sm(t0), sm(t1))
                product(sm(fr), sm(fi), e_re, e_im, e_re, e_im, sm(t0), sm(t1))
                link(pool.memset(turn_cos[:, :, 0:1], 1.0))
                link(pool.memset(turn_sin[:, :, 0:1], 0.0))
                n, cur, new = 1, (sm(fr), sm(fi)), (e_re, e_im)
                while n < NC:
                    xn = [tmp[:, i, 0:NQ * n].rearrange("p (q c) -> p q c", c=n) for i in range(2)]
                    product(turn_cos[:, :, n:2 * n], turn_sin[:, :, n:2 * n], turn_cos[:, :, 0:n], turn_sin[:, :, 0:n],
                            over(cur[0], n), over(cur[1], n), *xn)
                    product(*new, *cur, *cur, sm(t0), sm(t1))
                    cur, new, n = new, cur, 2 * n
                ts(decay[:, :, :], over(sm(mag), NC), 1.0, 0.0)
                pool.memset(decay[:, :, 0:1], 0.0).then_inc(weights_ready, 1)

            def s5_mix():
                for g in range(NQ // QG):
                    cos, sin = (t[:, QG * g:QG * g + QG, :].rearrange("p q c -> p (q c)") for t in (turn_cos, turn_sin))
                    pool.wait_ge(scanned, 2 * g + 2)
                    if g:
                        pool.wait_ge(y_done, g)
                    pool.tensor_tensor(scratch[:, 0, :], b_n.rearrange("p a t -> p (a t)"), sin, ALU.mult).then_inc(imag_step, 1)
                    pool.tensor_tensor(scratch[:, 1, :], prod.rearrange("p a t -> p (a t)"), cos, ALU.mult).then_inc(imag_step, 1)
                    pool.wait_ge(imag_step, 2 * g + 2)
                    pool.tensor_tensor(squares[:, 1].rearrange("p a t -> p (a t)"), scratch[:, 0, :], scratch[:, 1, :], ALU.add)\
                        .then_inc(state_im, 1)

            for st in stages:
                if st.kind == "s5":
                    pool.wait_ge(acc_done, NB * (st.f - 1) + 1)
                    for i in range(2):
                        pool.memset(within[i][:, :, :], 0.0).then_inc(within_zeroed, 1)
                norm(st.v)
                if st.v == 0 and any(o.kind == "s5" for o in stages):
                    s5_parameters()
                if st.kind == "s5":
                    s5_mix()
                if st.kind == "attn":
                    attention()

        @block.scalar
        def _(act):
            act.dma_start(rows_in[:, :, :], x[0].rearrange("(b p) d -> p b d", p=P)).then_inc(rows_landed, 16)
            for i, st in enumerate(stages):
                src = final_norm if st.kind == "final" else norm_rows[st.kind][st.layer]
                act.dma_start(gain_rows[i * KD:(i + 1) * KD, :], src.rearrange("(k p) -> k p", p=P))\
                    .then_inc(gains_landed, 16)

            act.dma_start(s5_rows[:, 0, :], s5_a_re[0].rearrange("(q e) p -> q (e p)", e=2)).then_inc(s5_landed, 16)
            act.dma_start(s5_rows[:, 1, :], s5_a_im[0].rearrange("(q e) p -> q (e p)", e=2)).then_inc(s5_landed, 16)
            act.dma_start(dt_rows[:, :], s5_log_dt[0].rearrange("(q e) -> q e", e=2)).then_inc(s5_landed, 16)
            for tau in range(TAU):
                act.dma_start(s5_rows[:, 3, 32 * tau:32 * tau + 32], s5_d[0].rearrange("(q c) -> q c", q=NQ))\
                    .then_inc(s5_landed, 16)
            for i, (b, c) in enumerate(((s5_b_re, s5_c_re), (s5_b_im, s5_c_im))):
                act.dma_start(c_rows[:, i], c[0].rearrange("(k g) h p -> (g h) k p", k=KD)).then_inc(s5_landed, 16)
                act.dma_start(b_in[:, i], b[0].rearrange("(q e) p h -> (e p) q h", e=2)).then_inc(s5_landed, 16)

            def split_hi(n, slot, uses):
                act.wait_ge(raw_landed[slot], uses * 16)
                if not isinstance(n, int) or n >= RING:
                    act.wait_ge(pe_done, n - (RING - 1))
                act.activation(w_hi[:, slot, :], raw[:, slot, :], ACT.Copy).then_inc(hi_done, 1)

            def split(n):
                if n < n_chunks:
                    split_hi(n, n % RING, n // RING + 1)

            def prep(v, u, banks=range(NB)):
                for b in banks:
                    act.wait_ge(x_new, 4 * v + b + 1)
                    if u is not None:
                        for k in (2 * b, 2 * b + 1):
                            act.activation(op_hi[:, HALF[u], k, :], xT[:, k, :], ACT.Copy,
                                           scale=gain[:, v * KD + k:v * KD + k + 1]).then_inc(op_hi_done, 1)
                    if b >= 2 or v > 0:
                        act.wait_ge(squares_used, 4 * v + 2 * (b >= 2))
                    act.activation(squares[:, b % 2], xT[:, 2 * b:2 * b + 2, :], ACT.Square).then_inc(squared, 1)

            def ffn(st, nxt):
                n0, base = st.n0, NG * st.f

                def do_silu(g):
                    act.wait_ge(a_taken, base + g + 1)
                    if st.f or not isinstance(g, int) or g:
                        act.wait_ge(prod_done, base + g)
                    act.activation(silu[:, :, :], a_n[:, :, :], ACT.Silu).then_inc(silu_done, 1)

                def do_g_hi(g, half):
                    act.wait_ge(prod_done, base + g + 1)
                    act.activation(g_hi[:, half], prod[:, :, :], ACT.Copy).then_inc(g_hi_done, 1)
                split(n0 + 2)
                split(n0 + 3)
                split(n0 + 4)
                split(n0 + 5)
                do_silu(0)
                if nxt.kind == "ple":
                    p_high(nxt.q)
                if nxt.kind == "s5":
                    s5_phasors()
                with act.Fori(1, NG - 1) as g:
                    n = g * 6 + (n0 - 2)
                    s = n0 + 4

                    def sp_(j):
                        m = s + j - 6
                        split_hi(n + j, (s + j) % RING, g * 2 + (m // RING + 1))
                    sp_(2)
                    do_g_hi(g - 1, 0)
                    sp_(3)
                    sp_(4)
                    sp_(5)
                    do_silu(g)
                    sp_(6)
                    sp_(7)
                n = n0 + 6 * (NG - 1) - 2
                split(n + 2)
                do_g_hi(NG - 2, 0)
                split(n + 3)
                split(n + 4)
                split(n + 5)
                do_silu(NG - 1)
                split(n + 6)
                do_g_hi(NG - 1, 1)
                split(n + 7)
                split(n + 8)
                if nxt.kind == "s5":
                    act.wait_ge(weights_ready, 1)
                prep(nxt.v, nxt.u if nxt.kind != "final" else None)
                split(n + 9)

            def p_high(q):
                act.wait_ge(p_turned, q + 1)
                act.activation(p_hi[:, :, :], misc[:, :].rearrange("p (k t) -> p k t", k=2), ACT.Copy).then_inc(p_hi_done, 1)

            def ple(st, nxt):
                split(st.n0 + 2)
                split(st.n0 + 3)
                for j in range(NB):
                    split(st.n0 + 4 + 2 * j)
                    if j < NB - 1:
                        split(st.n0 + 5 + 2 * j)
                    act.wait_ge(gate_taken, 4 * st.q + j + 1)
                    if st.e or j:
                        act.wait_ge(gated, st.e + j)
                    act.activation(silu[:, :, :], a_n[:, :, :], ACT.Sigmoid).then_inc(gate_ready, 1)
                    prep(nxt.v, nxt.u if nxt.kind != "final" else None, [j])
                split(st.n0 + 11)

            def s5_in():
                act.wait_ge(s5_landed, 16 * 11)
                act.activation(s5_rows[:, 2, :].rearrange("q (e p) -> q e p", e=2),
                               dt_rows[:, :].unsqueeze(2).broadcast_to([NQ, 2, S]), ACT.Copy).then_inc(rows_spread, 1)
                act.wait_ge(s5_turned, 1)
                for i, to in ((0, 0), (1, 1), (3, 3)):
                    act.activation(small[:, to, :], misc[:, 128 + NQ * i:128 + NQ * (i + 1)], ACT.Copy).then_inc(small_ready, 1)
                act.activation(small[:, 2, :], misc[:, 128 + NQ * 2:128 + NQ * 3], ACT.Exp).then_inc(small_ready, 1)

            def s5_phasors():
                act.wait_ge(angles_ready, 1)
                act.activation(small[:, 6, :], small[:, 4, :], ACT.Exp).then_inc(phasors_ready, 1)
                act.activation(small[:, 8, :], small[:, 5, :], ACT.Sin).then_inc(phasors_ready, 1)
                act.activation(small[:, 7, :], small[:, 5, :], ACT.Abs).then_inc(rows_spread, 1)
                act.wait_ge(rows_spread, 2)
                act.activation(small[:, 7, :], small[:, 7, :], ACT.Sin, scale=-1.0, bias=half_pi[:, 0:1]).then_inc(phasors_ready, 1)

            def s5(st, nxt):
                n0, z_set = st.n0, st.u + 1
                scaled_u = (a_n, b_n)

                def blocks(i):
                    act.wait_ge(block_first, i + 1)
                    o = within[i // 4][:, 4 * (i % 4):4 * (i % 4) + 4, :]
                    for quad in (2, 3):
                        r = slice(32 * quad, 32 * quad + 32)
                        act.activation(o[r, :, 32 * quad:P], o[0:32, :, 0:P - 32 * quad], ACT.Copy).then_inc(block_taken, 1)
                    act.wait_ge(turned_done, 2 * i + 1)
                    act.activation(w_in_state[:, 0, 4 * i:4 * i + 4].rearrange("p q t e h -> p (q t e h)"),
                                   acc[1].rearrange("p a t -> p (a t)"), ACT.Copy).then_inc(turned_taken, 1)

                def place(j):
                    act.wait_ge(u_scaled, j + 1)
                    for quad in (2, 3):
                        for tau in range(TAU):
                            src = scaled_u[j % 2][32 * quad:32 * quad + 32].rearrange("p k (c t) -> p k c t", t=TAU)[:, :, :, tau]
                            dst = u_steps[32 * tau:32 * tau + 32, 8 * j:8 * j + 8, :].rearrange("p (k j) c -> p k j c", k=2)[:, :, quad, :]
                            act.activation(dst, src, ACT.Copy).then_inc(u_placed, 1)
                for i in range(8):
                    split(n0 + i + 2)
                    blocks(i)
                    if i and i % 2 == 0:
                        place(i // 2 - 1)
                place(3)
                zf = square_sum
                for g in range(NB):
                    act.wait_ge(y_done, g + 1)
                    if g:
                        act.wait_ge(op_lo_done, KD * z_set + 2 * g)
                    y = bank[g % 2].rearrange("p a t -> p (a t)").rearrange("p (k j c) -> p k j c", k=2, c=NC)
                    for quad in range(4):
                        for tau in range(TAU):
                            dst = zf[32 * quad:32 * quad + 32].rearrange("p k (c t) -> p k c t", t=TAU)[:, :, :, tau]
                            act.activation(dst, y[32 * tau:32 * tau + 32, :, quad, :], ACT.Gelu_apprx_tanh).then_inc(gelu_done, 1)
                    act.wait_ge(gelu_done, 16 * g + 16)
                    act.activation(op_hi[:, HALF[z_set], 2 * g:2 * g + 2, :], zf[:, :, :], ACT.Copy).then_inc(op_hi_done, 2)
                for j in range(NB):
                    n = n0 + 8 + 4 * j
                    split(n + 2)
                    split(n + 3)
                    act.wait_ge(pe_done, n + 2)
                    if st.e or j:
                        act.wait_ge(gated, st.e + j)
                    act.activation(silu[:, :, :], bank[j % 2][:, :, :], ACT.Sigmoid).then_inc(gate_ready, 1)
                    split(n + 4)
                    if j < NB - 1:
                        split(n + 5)
                    prep(nxt.v, nxt.u, [j])
                split(n0 + 25)

            def attention(st, nxt):
                n0, o_set = st.n0, st.u + 1
                act.wait_ge(gated, st.e)
                act.preload_act_table_set("natural_log_exp_and_others")
                split(n0 + 2)
                split(n0 + 3)
                for j in range(NB):
                    act.wait_ge(r_ready, st.v + 1)
                    act.wait_ge(pe_done, n0 + 2 * j + 2)
                    for tb in range(TB):
                        act.activation(val[:, tb, 256 * j:256 * j + 256], bank[j % 2][:, tb, :], ACT.Copy,
                                       scale=r_col[:, tb:tb + 1]).then_inc(bank_taken, 1)
                    split(n0 + 4 + 2 * j)
                    split(n0 + 5 + 2 * j)
                for n in (n0 + 12, n0 + 13):
                    split(n)
                for s in range(STEPS):
                    h = s
                    if h < NH:
                        act.wait_ge(z_done, h + 1)
                        act.activation(z_abs[:, h % 2], acc[h % 2].rearrange("p a t -> p (a t)")[:, 0:HW], ACT.Abs)\
                            .then_inc(abs_done, 1)
                        act.wait_ge(abs_done, h + 1)
                        act.activation(z_exp[:, h % 2], z_abs[:, h % 2], ACT.Exp, scale=-1.0).then_inc(exp_done, 1)
                        act.wait_ge(exp_done, h + 1)
                        if h >= 2:
                            act.wait_ge(drop_done, h - 1)
                        act.activation(z_log[:, h % 2], z_exp[:, h % 2], ACT.Ln, bias=1.0).then_inc(log_done, 1)
                    h = s - 1
                    if 0 <= h < NH:
                        act.wait_ge(exponent_done, h + 1)
                        if h >= 2:
                            act.wait_ge(o_done, h - 1)
                        act.activation(att[:, h % 2], acc[h % 2].rearrange("p a t -> p (a t)")[:, 0:HW], ACT.Exp)\
                            .then_inc(att_done, 1)
                    h = s - 2
                    if 0 <= h and h % 2:
                        act.wait_ge(o_done, h + 1)
                        act.activation(op_hi[:, HALF[o_set], h // 2, :], acc[2 + h // 2 % 2][:, 0, :], ACT.Copy)\
                            .then_inc(op_hi_done, 1)
                    if step_chunk(st, s) is not None:
                        split(step_chunk(st, s) + 2)
                split(n0 + 28)
                split(n0 + 29)
                prep(nxt.v, nxt.u, [0])
                split(n0 + 30)
                split(n0 + 31)
                prep(nxt.v, nxt.u, [1])
                prep(nxt.v, nxt.u, [2])
                split(n0 + 32)
                prep(nxt.v, nxt.u, [3])
                split(n0 + 33)

            split(0)
            split(1)
            act.wait_ge(gain_turned, 1)
            act.activation(gain[:, 0:KD * len(stages)], misc[:, 0:KD * len(stages)], ACT.Copy).then_inc(gain_ready, 1)
            act.wait_ge(gain_ready, 1)
            prep(0, 0)
            if any(o.kind == "s5" for o in stages):
                s5_in()
            for st, nxt in zip(stages, stages[1:] + [None]):
                if st.kind[:3] == "ffn":
                    ffn(st, nxt)
                if st.kind == "s5":
                    s5(st, nxt)
                if st.kind == "ple":
                    ple(st, nxt)
                if st.kind == "attn":
                    attention(st, nxt)

        @block.vector
        def _(dve):
            def split_lo(n, slot):
                dve.wait_ge(hi_done, n + 1)
                dve.tensor_tensor(w_lo[:, slot, :], raw[:, slot, :], w_hi[:, slot, :].bitcast(F32), ALU.subtract)\
                    .then_inc(lo_done, 1)

            def split(n):
                if n < n_chunks:
                    split_lo(n, n % RING)

            def op_low(v, u, b):
                if u is None:
                    return
                for k in (2 * b, 2 * b + 1):
                    dve.wait_ge(op_hi_done, KD * u + k + 1)
                    dve.scalar_tensor_tensor(out=op_lo[:, HALF[u], k, :], in0=xT[:, k, :],
                                             scalar=gain[:, v * KD + k:v * KD + k + 1],
                                             in1=op_hi[:, HALF[u], k, :].bitcast(F32), op0=ALU.mult, op1=ALU.subtract)\
                        .then_inc(op_lo_done, 1)

            def stat_mean(v):
                dve.wait_ge(sum_col, v + 1)
                dve.tensor_scalar(mean_sq[:, :], stat[:, 0:TB], 1.0 / D, EPS, ALU.mult, ALU.add).then_inc(mean_ready, 1)

            def stat_diag(v):
                dve.wait_ge(r_ready, v + 1)
                for tb in range(TB):
                    dve.tensor_scalar(r_diag[:, tb, :], ident[:, :], r_col[:, tb:tb + 1], None, ALU.mult)\
                        .then_inc(diag_ready, 1)

            def stat_row(v):
                dve.wait_ge(r_spread, v + 1)
                dve.tensor_copy(r_row[:, :], stat[:, 256:256 + T]).then_inc(r_row_ready, 1)

            def residual_from_acc(v, u, f):
                dve.wait_ge(x_new, 4 * v)
                for b in range(NB):
                    dve.wait_ge(acc_done, NB * f + b + 1)
                    dve.scalar_tensor_tensor(out=xT[:, 2 * b:2 * b + 2, :], in0=acc[b][:, :, :], scalar=0.5,
                                             in1=xT[:, 2 * b:2 * b + 2, :], op0=ALU.mult, op1=ALU.add).then_inc(x_new, 1)
                    if b:
                        op_low(v, u, b - 1)
                op_low(v, u, NB - 1)

            r_bc = r_row[:, :].unsqueeze(1).broadcast_to([P, 2, T])

            def ffn(st, nxt):
                n0, base, v = st.n0, NG * st.f, st.v

                def take_a(n, g):
                    dve.wait_ge(pe_done, n + 1)
                    if st.f or not isinstance(g, int) or g:
                        dve.wait_ge(silu_done, base + g)
                    dve.tensor_tensor(a_n[:, :, :], bank[0][:, :, :], r_bc, ALU.mult).then_inc(a_taken, 1)

                def take_b(n, g):
                    dve.wait_ge(pe_done, n + 1)
                    dve.tensor_tensor(b_n[:, :, :], bank[1][:, :, :], r_bc, ALU.mult).then_inc(b_taken, 1)
                    dve.wait_ge(silu_done, base + g + 1)
                    dve.wait_ge(b_taken, base + g + 1)
                    if st.f or not isinstance(g, int) or g:
                        dve.wait_ge(g_hi_done, base + g)
                    dve.tensor_tensor(prod[:, :, :], silu[:, :, :], b_n[:, :, :], ALU.mult).then_inc(prod_done, 1)

                def do_g_lo(g, half):
                    dve.wait_ge(g_hi_done, base + g + 1)
                    dve.tensor_tensor(g_lo[:, half], prod[:, :, :], g_hi[:, half].bitcast(F32), ALU.subtract)\
                        .then_inc(g_lo_done, 1)
                split(n0 + 2)
                split(n0 + 3)
                stat_mean(v)
                split(n0 + 4)
                stat_diag(v)
                split(n0 + 5)
                stat_row(v)
                dve.wait_ge(r_row_ready, v + 1)
                take_a(n0 + 1, 0)
                take_b(n0 + 3, 0)
                if nxt.kind == "ple":
                    dve.wait_ge(p_hi_done, nxt.q + 1)
                    dve.tensor_tensor(p_lo[:, :, :], misc[:, :].rearrange("p (k t) -> p k t", k=2), p_hi[:, :, :].bitcast(F32),
                                      ALU.subtract).then_inc(p_lo_done, 1)
                with dve.Fori(1, NG - 1) as g:
                    n, s = g * 6 + (n0 - 2), n0 + 4
                    split_lo(n + 2, (s + 2) % RING)
                    do_g_lo(g - 1, 0)
                    split_lo(n + 3, (s + 3) % RING)
                    split_lo(n + 4, (s + 4) % RING)
                    take_a(n + 1, g)
                    split_lo(n + 5, (s + 5) % RING)
                    split_lo(n + 6, (s + 6) % RING)
                    take_b(n + 3, g)
                    split_lo(n + 7, (s + 7) % RING)
                n = n0 + 6 * (NG - 1) - 2
                split(n + 2)
                do_g_lo(NG - 2, 0)
                split(n + 3)
                split(n + 4)
                take_a(n + 1, NG - 1)
                split(n + 5)
                split(n + 6)
                take_b(n + 3, NG - 1)
                do_g_lo(NG - 1, 1)
                split(n + 7)
                split(n + 8)
                if nxt.kind == "s5":
                    dve.wait_ge(weights_ready, 1)
                residual_from_acc(nxt.v, nxt.u if nxt.kind != "final" else None, st.f)
                split(n + 9)

            def ple(st, nxt):
                n0, v = st.n0, nxt.v
                u = nxt.u if nxt.kind != "final" else None
                split(n0 + 2)
                stat_mean(st.v)
                split(n0 + 3)
                stat_diag(st.v)
                stat_row(st.v)
                for j in range(NB):
                    split(n0 + 4 + 2 * j)
                    if j < NB - 1:
                        split(n0 + 5 + 2 * j)
                    dve.wait_ge(pe_done, n0 + 4 + 2 * j)
                    dve.wait_ge(r_row_ready, st.v + 1)
                    if st.e or j:
                        dve.wait_ge(gate_ready, st.e + j)
                    dve.tensor_tensor(a_n[:, :, :], bank[j % 2][:, :, :], r_bc, ALU.mult).then_inc(gate_taken, 1)
                    if j:
                        op_low(v, u, j - 1)
                    dve.wait_ge(gate_ready, st.e + j + 1)
                    dve.tensor_tensor(b_n[:, :, :], acc[j][:, :, :], silu[:, :, :], ALU.mult).then_inc(gated, 1)
                    dve.wait_ge(gated, st.e + j + 1)
                    dve.wait_ge(x_new, 4 * v)
                    xj = xT[:, 2 * j:2 * j + 2, :]
                    dve.tensor_tensor(xj, xj, b_n[:, :, :], ALU.add).then_inc(x_new, 1)
                op_low(v, u, NB - 1)
                split(n0 + 11)

            def s5(st, nxt):
                n0, z_set, v, u = st.n0, st.u + 1, nxt.v, nxt.u
                scaled_u = (a_n, b_n)

                def blocks(i):
                    o = within[i // 4][:, 4 * (i % 4):4 * (i % 4) + 4, :]
                    kk = acc[0].rearrange("p a t -> p (a t)").rearrange("p (q c) -> p q c", q=4)
                    dve.wait_ge(block_done, i + 1)
                    dve.tensor_tensor(kk[0:32, :, 0:32], kk[0:32, :, 0:32], skip[:, 4 * i:4 * i + 4, :], ALU.add).then_inc(block_skip, 1)
                    dve.wait_ge(block_skip, i + 1)
                    dve.wait_ge(within_zeroed, 2)
                    dve.tensor_copy(o[0:32], kk[0:32]).then_inc(block_first, 1)
                    dve.tensor_copy(o[32:64, :, 32:P], kk[0:32, :, 0:P - 32]).then_inc(block_taken, 2)
                    dve.wait_ge(turned_done, 2 * i + 2)
                    dve.tensor_copy(w_in_state[:, 1, 4 * i:4 * i + 4].rearrange("p q t e h -> p (q t e h)"),
                                    acc[2].rearrange("p a t -> p (a t)")).then_inc(turned_taken, 1)

                def place(j):
                    dve.wait_ge(pe_done, n0 + 2 * j + 2)
                    if j >= 2:
                        dve.wait_ge(u_placed, 16 * (j - 1))
                    dve.tensor_tensor(scaled_u[j % 2][:, :, :], bank[j % 2][:, :, :], r_bc, ALU.mult).then_inc(u_scaled, 1)
                    dve.wait_ge(u_scaled, j + 1)
                    for quad in (0, 1):
                        for tau in range(TAU):
                            src = scaled_u[j % 2][32 * quad:32 * quad + 32].rearrange("p k (c t) -> p k c t", t=TAU)[:, :, :, tau]
                            dst = u_steps[32 * tau:32 * tau + 32, 8 * j:8 * j + 8, :].rearrange("p (k j) c -> p k j c", k=2)[:, :, quad, :]
                            dve.tensor_copy(dst, src).then_inc(u_placed, 1)
                for i in range(8):
                    split(n0 + i + 2)
                    blocks(i)
                    if i == 0:
                        stat_mean(st.v)
                        stat_diag(st.v)
                        stat_row(st.v)
                        dve.wait_ge(r_row_ready, st.v + 1)
                    if i and i % 2 == 0:
                        place(i // 2 - 1)
                place(3)
                links = [0]

                def link(ins):
                    links[0] += 1
                    ins.then_inc(dve_step, 1)
                    dve.wait_ge(dve_step, links[0])
                A, B, C, E = (t.rearrange("p a t -> p (a t)") for t in (a_n, b_n, silu, prod))
                s_re = squares[:, 0].rearrange("p a t -> p (a t)")
                zf = square_sum

                def z_low(g):
                    dve.wait_ge(op_hi_done, KD * z_set + 2 * g + 2)
                    dve.tensor_tensor(op_lo[:, HALF[z_set], 2 * g:2 * g + 2, :], zf[:, :, :],
                                      op_hi[:, HALF[z_set], 2 * g:2 * g + 2, :].bitcast(F32), ALU.subtract).then_inc(op_lo_done, 2)
                dve.wait_ge(u_placed, 64)
                for g in range(NB):
                    cos, sin, fall = (t[:, QG * g:QG * g + QG, :].rearrange("p q c -> p (q c)")
                                      for t in (turn_cos, turn_sin, decay))
                    x_re, x_im = (acc[2 * (g % 2) + i].rearrange("p a t -> p (a t)") for i in range(2))
                    dve.wait_ge(s_in_done, g + 1)
                    if g:
                        dve.wait_ge(state_im, g)
                        dve.wait_ge(state_re, g)
                    dve.tensor_tensor(A, x_re, cos, ALU.mult).then_inc(dve_step, 1)
                    dve.tensor_tensor(B, x_im, sin, ALU.mult).then_inc(dve_step, 1)
                    dve.tensor_tensor(C, x_im, cos, ALU.mult).then_inc(dve_step, 1)
                    dve.tensor_tensor(E, x_re, sin, ALU.mult).then_inc(dve_step, 1)
                    links[0] += 4
                    dve.wait_ge(dve_step, links[0])
                    dve.tensor_tensor(A, A, B, ALU.add).then_inc(dve_step, 1)
                    dve.tensor_tensor(C, C, E, ALU.subtract).then_inc(dve_step, 1)
                    links[0] += 2
                    dve.wait_ge(dve_step, links[0])
                    dve.tensor_tensor_scan(B, fall, A, 0.0, ALU.mult, ALU.add).then_inc(scanned, 1)
                    dve.tensor_tensor_scan(E, fall, C, 0.0, ALU.mult, ALU.add).then_inc(scanned, 1)
                    dve.wait_ge(scanned, 2 * g + 2)
                    dve.tensor_tensor(A, B, cos, ALU.mult).then_inc(dve_step, 1)
                    dve.tensor_tensor(C, E, sin, ALU.mult).then_inc(dve_step, 1)
                    links[0] += 2
                    dve.wait_ge(dve_step, links[0])
                    if g:
                        dve.wait_ge(y_done, g)
                    dve.tensor_tensor(s_re, A, C, ALU.subtract).then_inc(state_re, 1)
                    if g:
                        z_low(g - 1)
                z_low(NB - 1)
                for j in range(NB):
                    n = n0 + 8 + 4 * j
                    split(n + 2)
                    split(n + 3)
                    if j:
                        op_low(v, u, j - 1)
                    split(n + 4)
                    if j < NB - 1:
                        split(n + 5)
                    dve.wait_ge(pe_done, n + 4)
                    dve.wait_ge(gate_ready, st.e + j + 1)
                    dve.tensor_tensor(b_n[:, :, :], acc[j][:, :, :], silu[:, :, :], ALU.mult).then_inc(gated, 1)
                    dve.wait_ge(gated, st.e + j + 1)
                    dve.wait_ge(x_new, 4 * v)
                    xj = xT[:, 2 * j:2 * j + 2, :]
                    dve.tensor_tensor(xj, xj, b_n[:, :, :], ALU.add).then_inc(x_new, 1)
                op_low(v, u, NB - 1)
                split(n0 + 25)

            def attention(st, nxt):
                n0, o_set = st.n0, st.u + 1

                def take_kq(j, which):
                    dve.wait_ge(pe_done, n0 + 10 + 4 * j + 2 * which)
                    dst = (kT, qT)[which][:, 2 * j:2 * j + 2, :]
                    if which:
                        op = dve.scalar_tensor_tensor(out=dst, in0=bank[1][:, :, :], scalar=SCALE, in1=r_bc,
                                                      op0=ALU.mult, op1=ALU.mult)
                    else:
                        op = dve.tensor_tensor(dst, bank[0][:, :, :], r_bc, ALU.mult)
                    op.then_inc(bank_taken, 2)

                def take_out(j):
                    xj = xT[:, 2 * j:2 * j + 2, :]
                    dve.wait_ge(x_new, 4 * nxt.v)
                    dve.tensor_tensor(xj, xj, bank[j % 2][:, :, :], ALU.add).then_inc(x_new, 1)

                split(n0 + 2)
                split(n0 + 3)
                stat_mean(st.v)
                split(n0 + 4)
                stat_diag(st.v)
                split(n0 + 5)
                stat_row(st.v)
                for n in range(n0 + 6, n0 + 12):
                    split(n)
                dve.wait_ge(r_row_ready, st.v + 1)
                dve.wait_ge(bank_taken, 8)
                take_kq(0, 0)
                split(n0 + 12)
                split(n0 + 13)
                take_kq(0, 1)
                for s in range(STEPS):
                    h = s
                    if h < NH:
                        zb = acc[h % 2].rearrange("p a t -> p (a t)")[:, 0:HW]
                        dve.wait_ge(z_done, h + 1)
                    if step_chunk(st, s) is not None:
                        split(step_chunk(st, s) + 2)
                    if h < NH:
                        dve.wait_ge(log_done, h + 1)
                        if h >= 2:
                            dve.wait_ge(exponent_done, h - 1)
                        dve.scalar_tensor_tensor(out=drop[:, h % 2], in0=zb, scalar=0.0, in1=z_log[:, h % 2],
                                                 op0=ALU.max, op1=ALU.add).then_inc(drop_done, 1)
                    h = s - 2
                    if 0 <= h and h % 2:
                        dve.wait_ge(op_hi_done, KD * o_set + h // 2 + 1)
                        dve.tensor_tensor(op_lo[:, HALF[o_set], h // 2, :], acc[2 + h // 2 % 2][:, 0, :],
                                          op_hi[:, HALF[o_set], h // 2, :].bitcast(F32), ALU.subtract).then_inc(op_lo_done, 1)
                    if s < 12 and s % 2:
                        take_kq(s // 4 + 1, s // 2 % 2)
                split(n0 + 28)
                dve.wait_ge(pe_done, n0 + 27)
                take_out(0)
                split(n0 + 29)
                op_low(nxt.v, nxt.u, 0)
                split(n0 + 30)
                dve.wait_ge(pe_done, n0 + 28)
                take_out(1)
                split(n0 + 31)
                op_low(nxt.v, nxt.u, 1)
                dve.wait_ge(pe_done, n0 + 30)
                take_out(2)
                op_low(nxt.v, nxt.u, 2)
                split(n0 + 32)
                dve.wait_ge(pe_done, n0 + 32)
                take_out(3)
                op_low(nxt.v, nxt.u, 3)
                split(n0 + 33)

            def c_take():
                for i in range(2):
                    dve.wait_ge(c_turned, i + 1)
                    dve.tensor_scalar(c_in[:, i].rearrange("p q h -> p (q h)"), acc[i].rearrange("p a t -> p (a t)"),
                                      1.0 - 2 * i, None, ALU.mult).then_inc(c_ready, 1)

            split(0)
            split(1)
            for b in range(NB):
                dve.wait_ge(x_turned, b + 1)
                dve.tensor_copy(xT[:, 2 * b:2 * b + 2, :], acc[b][:, :, :]).then_inc(x_new, 1)
            dve.wait_ge(gain_ready, 1)
            for b in range(NB):
                op_low(0, 0, b)
            if any(o.kind == "s5" for o in stages):
                c_take()
            for st, nxt in zip(stages, stages[1:] + [None]):
                if st.kind[:3] == "ffn":
                    ffn(st, nxt)
                if st.kind == "s5":
                    s5(st, nxt)
                if st.kind == "ple":
                    ple(st, nxt)
                if st.kind == "attn":
                    attention(st, nxt)
                if st.kind == "final":
                    stat_mean(st.v)
                    dve.wait_ge(squared, 4 * st.v + 4)
                    dve.wait_ge(x_new, 4 * st.v + 4)
                    for k in range(KD):
                        dve.tensor_scalar(xT[:, k, :], xT[:, k, :], gain[:, st.v * KD + k:st.v * KD + k + 1], None,
                                          ALU.mult).then_inc(scaled, 1)
                    dve.wait_ge(r_ready, st.v + 1)
                    for tb in range(TB):
                        for h in range(2):
                            dve.wait_ge(out_turned, 2 * tb + h + 1)
                            dve.tensor_scalar(rows_in[:, tb, h * 512:(h + 1) * 512], acc[2 * (tb % 2) + h][:, :, :]
                                              .rearrange("p a t -> p (a t)"), r_col[:, tb:tb + 1], None, ALU.mult)\
                                .then_inc(out_rows, 1)

        @block.tensor
        def _(pe):
            def products(o, wh, wl, xh, xl, start, stop):
                pe.matmul(o, wh, xh, start=start, stop=False, skip_group_check=True)
                pe.matmul(o, wl, xh, start=False, stop=False, skip_group_check=True)
                return pe.matmul(o, wh, xl, start=False, stop=stop, skip_group_check=True)

            def stat_sum(v):
                pe.wait_ge(sum_ready, v + 1)
                for tb in range(TB):
                    mm = pe.matmul(stat[:, tb:tb + 1], square_sum[:, 0, tb * P:(tb + 1) * P], ones[:, 0:1],
                                   start=True, stop=True)
                mm.then_inc(sum_col, 1)

            def stat_spread(v):
                for tb in range(TB):
                    pe.wait_ge(diag_ready, TB * v + tb + 1)
                    mm = pe.matmul(stat[:, 256 + tb * P:256 + (tb + 1) * P], ones[:, :], r_diag[:, tb, :],
                                   start=True, stop=True)
                mm.then_inc(r_spread, 1)

            def chunk_a(n, slot, half, o, u, ready=True, hooks={}):
                pe.wait_ge(lo_done, n + 1)
                for kk in range(4):
                    k = 4 * half + kk
                    if not ready:
                        pe.wait_ge(op_lo_done, KD * u + k + 1)
                    for m in range(2):
                        wh, wl = (w[:, slot, (kk * 2 + m) * P:(kk * 2 + m + 1) * P] for w in (w_hi, w_lo))
                        mm = products(o[:, m, :], wh, wl, op_hi[:, HALF[u], k, :], op_lo[:, HALF[u], k, :],
                                      k == 0 and m == 0, k == KD - 1)
                    if kk == 3:
                        mm.then_inc(pe_done, 1)
                    if k in hooks:
                        hooks[k]()

            def open_acc():
                for b in range(NB):
                    pe.matmul(acc[b][:, 0, 0:2], zeros_b[:, :], zeros_b[:, 0:2], start=True, stop=True,
                              skip_group_check=True)

            def group(n, o, u, **kw):
                for half in range(2):
                    chunk_a(n + half, (n + half) % RING, half, o, u, **kw)

            def ple(st):
                n0, u = st.n0, st.u
                pe.wait_ge(p_lo_done, st.q + 1)
                for kt in range(2):
                    pe.wait_ge(lo_done, n0 + kt + 1)
                    for m in range(KD):
                        if kt == 0 and m % 2 == 0:
                            pe.wait_ge(x_new, 4 * st.v + m // 2 + 1)
                        wh, wl = (w[:, (n0 + kt) % RING, m * P:(m + 1) * P] for w in (w_hi, w_lo))
                        mm = products(acc[m // 2][:, m % 2, :], wh, wl, p_hi[:, kt, :], p_lo[:, kt, :],
                                      kt == 0 and m % 2 == 0, kt == 1)
                    mm.then_inc(pe_done, 1)
                    if kt == 0:
                        pass
                stat_sum(st.v)
                group(n0 + 2, bank[0], u, ready=False, hooks={3: lambda: stat_spread(st.v)})
                group(n0 + 4, bank[1], u)
                for j in (2, 3):
                    pe.wait_ge(gate_taken, 4 * st.q + j - 1)
                    group(n0 + 2 + 2 * j, bank[j % 2], u)

            def s5_turn():
                pe.wait_ge(s5_landed, 16 * 11)
                pe.wait_ge(rows_spread, 1)
                for i in range(4):
                    mm = pe.transpose(misc[:, 128 + NQ * i:128 + NQ * (i + 1)], s5_rows[:, i, :], ident[0:NQ, 0:NQ])
                mm.then_inc(s5_turned, 1)
                by_group = ident[:, :].rearrange("p (q e h) -> p q e h", e=2, h=H)
                for i in range(2):
                    pe.wait_ge(x_new, i + 1)
                    for e in range(2):
                        for k in range(KD):
                            mm = pe.matmul(acc[i].rearrange("p a t -> p (a t)")[S * e:S * e + S, 64 * k:64 * k + 64],
                                           c_rows[:, i, k, :], by_group[:, :, e, :], start=True, stop=True,
                                           skip_group_check=True)
                    mm.then_inc(c_turned, 1)

            def s5(st):
                n0, u = st.n0, st.u

                def blocks(i):
                    flat = [a.rearrange("p a t -> p (a t)") for a in acc]
                    if i == 0:
                        pe.wait_ge(weights_ready, 1)
                        pe.wait_ge(x_new, 4 * st.v + 4)
                    else:
                        pe.wait_ge(block_taken, 4 * i)
                        pe.wait_ge(turned_taken, 2 * i)
                    for q in range(4):
                        for part in range(2):
                            lhs = w_in_state[:, part, 4 * i + q, TAU - 1, :, :].rearrange("p e h -> p (e h)")
                            rhs = w_state_out[:, part, 4 * i + q, 0:TAU].rearrange("p t e h -> p (t e h)")
                            mm = pe.matmul(flat[0][0:32, P * q:P * q + P], lhs, rhs, start=part == 0, stop=part == 1)
                    mm.then_inc(block_done, 1)
                    for part in range(2):
                        for q in range(4):
                            mm = pe.transpose(flat[1 + part][:, P * q:P * q + P],
                                              w_in_state[:, part, 4 * i + q].rearrange("p t e h -> p (t e h)"), ident[:, :])
                        mm.then_inc(turned_done, 1)
                for i in range(8):
                    if i >= 4 and i % 2 == 0:
                        pe.wait_ge(u_scaled, i // 2 - 1)
                    chunk_a(n0 + i, (n0 + i) % RING, i % 2, bank[i // 2 % 2], u, ready=i >= 2,
                            hooks={6: lambda: (stat_sum(st.v), stat_spread(st.v))} if i == 1 else {})
                    blocks(i)
                pe.wait_ge(block_taken, 32)
                pe.wait_ge(turned_taken, 16)
                pe.wait_ge(u_placed, 64)

                def state_in(g):
                    if g >= 2:
                        pe.wait_ge(scanned, 2 * g - 2)
                    for part in range(2):
                        o = acc[2 * (g % 2) + part].rearrange("p a t -> p (a t)")
                        for q in range(QG):
                            w = w_in_state[:, part, QG * g + q].rearrange("p t e h -> p (t e h)")
                            mm = pe.matmul(o[:, NC * q:NC * q + NC], w, u_steps[:, QG * g + q, :], start=True, stop=True)
                    mm.then_inc(s_in_done, 1)

                def state_out(g):
                    y = bank[g % 2].rearrange("p a t -> p (a t)")
                    if g >= 2:
                        pe.wait_ge(gelu_done, 16 * (g - 1))
                    for q in range(QG):
                        qq = QG * g + q
                        pe.matmul(y[:, NC * q:NC * q + NC], within[qq // 16][:, qq % 16, :], u_steps[:, qq, :],
                                  start=q == 0, stop=False, skip_group_check=True)
                    pe.wait_ge(state_re, g + 1)
                    for part in range(2):
                        if part:
                            pe.wait_ge(state_im, g + 1)
                        states = squares[:, part].rearrange("p a t -> p (a t)")
                        for q in range(QG):
                            w = w_state_out[:, part, QG * g + q, 1:TAU + 1].rearrange("p t e h -> p (t e h)")
                            mm = pe.matmul(y[:, NC * q + 1:NC * q + NC], w, states[:, NC * q:NC * q + NC - 1], start=False,
                                           stop=part == 1, skip_group_check=True)
                    mm.then_inc(y_done, 1)
                state_in(0)
                for g in range(NB):
                    if g + 1 < NB:
                        state_in(g + 1)
                    state_out(g)
                for j in range(NB):
                    n = n0 + 8 + 4 * j
                    if j == 0:
                        pe.wait_ge(op_lo_done, KD * (u + 2))
                    if j >= 2:
                        pe.wait_ge(gate_ready, st.e + j - 1)
                    group(n, bank[j % 2], u + 1)
                    group(n + 2, acc[j], u + 1)

            def head_step(s):
                h = s
                if h < NH:
                    j, q0 = h // 2, DH * (h % 2)
                    zb = acc[h % 2].rearrange("p a t -> p (a t)")
                    pe.wait_ge(bank_taken, 8 + 4 * (h // 4 + 1))
                    if h >= 2:
                        pe.wait_ge(att_done, h - 1)
                    pe.matmul(zb[:, 0:T], kT[q0:q0 + DH, j, 0:P], qT[q0:q0 + DH, j, :], start=True, stop=True,
                              skip_group_check=True)
                    pe.matmul(zb[:, T:HW], kT[q0:q0 + DH, j, P:T], qT[q0:q0 + DH, j, P:T], start=False, stop=True,
                              skip_group_check=True).then_inc(z_done, 1)
                h = s - 1
                if 0 <= h < NH:
                    zb = acc[h % 2].rearrange("p a t -> p (a t)")
                    pe.wait_ge(drop_masked, 2 * h + 2)
                    d = drop[:, h % 2]

                    def add(o, a, b):
                        return pe.matmul(o, a, b, start=False, stop=True, skip_group_check=True)
                    add(zb[:, 0:T], minus_tri[:, :], d[:, 0:T])
                    add(zb[:, P:T], minus_ones[:, :], d[:, T:HW])
                    add(zb[:, T:HW], minus_tri[:, :], d[:, T:HW])
                    add(zb[:, 0:P], ident_b[:, :], masked_b[:, :])
                    add(zb[:, T:HW], ident_b[:, :], masked_b[:, :]).then_inc(exponent_done, 1)
                h = s - 2
                if 0 <= h:
                    j, q0 = h // 2, DH * (h % 2)
                    o = acc[2 + j % 2][q0:q0 + DH, 0, :]
                    pe.wait_ge(att_done, h + 1)
                    if j >= 2 and h % 2 == 0:
                        pe.wait_ge(op_lo_done, KD * o_set[0] + j - 1)
                    pe.matmul(o, val[:, 0, h * DH:(h + 1) * DH], att[:, h % 2, 0:T], start=True, stop=True,
                              skip_group_check=True)
                    pe.matmul(o[:, P:T], val[:, 1, h * DH:(h + 1) * DH], att[:, h % 2, T:HW], start=False, stop=True,
                              skip_group_check=True).then_inc(o_done, 1)

            o_set = [0]

            def attention(st):
                n0, u = st.n0, st.u
                o_set[0] = u + 1
                for j in range(NB):
                    if j >= 2:
                        pe.wait_ge(bank_taken, 2 * j - 2)
                    for half in range(2):
                        n = n0 + 2 * j + half
                        pe.wait_ge(lo_done, n + 1)
                        for kk in range(4):
                            k = 4 * half + kk
                            if j == 0:
                                pe.wait_ge(op_lo_done, KD * u + k + 1)
                            wh, wl = (w[:, n % RING, kk * 256:(kk + 1) * 256] for w in (w_hi, w_lo))
                            for tb in range(TB):
                                xh, xl = (o[:, HALF[u], k, tb * P:(tb + 1) * P] for o in (op_hi, op_lo))
                                start = k == 0 and tb == 0
                                pe.matmul(bank[j % 2][:, tb, :], xh, wh, start=start, stop=False, skip_group_check=True)
                                pe.matmul(bank[j % 2][:, tb, :], xh, wl, start=False, stop=False, skip_group_check=True)
                                mm = pe.matmul(bank[j % 2][:, tb, :], xl, wh, start=False, stop=k == KD - 1,
                                               skip_group_check=True)
                            if kk == 3:
                                mm.then_inc(pe_done, 1)
                            if j == 0 and k == 6:
                                stat_sum(st.v)
                            if j == 1 and k == 3:
                                stat_spread(st.v)
                pe.wait_ge(bank_taken, 6)
                group(n0 + 8, bank[0], u)
                pe.wait_ge(bank_taken, 8)
                group(n0 + 10, bank[1], u)
                for s in range(STEPS):
                    if s < 12:
                        if s % 2 == 0:
                            pe.wait_ge(bank_taken, 8 + 4 * (s // 4) + 2 + 2 * (s // 2 % 2))
                        n = n0 + 12 + s
                        chunk_a(n, n % RING, s % 2, bank[s // 2 % 2], u)
                    elif s < 14:
                        n = n0 + 12 + s
                        if s == 12:
                            pe.wait_ge(bank_taken, 24)
                            pe.wait_ge(op_lo_done, KD * (u + 1) + 4)
                        chunk_a(n, n % RING, 0, bank[s % 2], u + 1)
                    head_step(s)
                for i, (j, half) in enumerate(OUT_ORDER[2:]):
                    if half == 0:
                        pe.wait_ge(x_new, 4 * (st.v + 1) + j - 1)
                    n = n0 + 26 + i
                    chunk_a(n, n % RING, half, bank[j % 2], u + 1, ready=False)

            def ffn(st, nxt):
                n0, base, v, u = st.n0, NG * st.f, st.v, st.u

                def up(n, s, which, **kw):
                    for half in range(2):
                        chunk_a(n + half, (s + half) % RING, half, bank[which], u, **kw)

                def down_tile(s, m, j, half):
                    wh, wl = (w[:, (s + j) % RING, m * P:(m + 1) * P] for w in (w_hi, w_lo))
                    return products(acc[m // 2][:, m % 2, :], wh, wl, g_hi[:, half, j, :], g_lo[:, half, j, :], False, False)

                def down(n, s, half):
                    for j in range(2):
                        pe.wait_ge(lo_done, n + j + 1)
                        for m in range(KD):
                            mm = down_tile(s, m, j, half)
                        mm.then_inc(pe_done, 1)
                if st.v:
                    pe.wait_ge(x_new, 4 * v)
                    pe.wait_ge(gate_taken, 4 * st.q)
                if st.e:
                    pe.wait_ge(gate_ready, st.e - 1)
                up(n0, n0, 0, ready=False, hooks={6: lambda: stat_sum(v)})
                pe.wait_ge(x_new, 4 * v + 4)
                if nxt.kind == "s5":
                    pe.wait_ge(c_ready, 2)
                open_acc()
                if nxt.kind == "ple":
                    pe.wait_ge(p_landed, 16 * (nxt.q + 1))
                    pe.wait_ge(gain_ready, 1)
                    for kt in range(2):
                        for tb in range(TB):
                            mm = pe.transpose(misc[:, kt * T + tb * P:kt * T + (tb + 1) * P],
                                              p_rows[:, tb, kt * P:(kt + 1) * P], ident[:, :])
                    mm.then_inc(p_turned, 1)
                if st.f:
                    pe.wait_ge(b_taken, base)
                if st.e:
                    pe.wait_ge(gate_ready, st.e)
                up(n0 + 2, n0 + 2, 1, hooks={3: lambda: stat_spread(v)})
                with pe.Fori(1, NG - 1) as g:
                    n, s = g * 6 + (n0 - 2), n0 + 4
                    pe.wait_ge(a_taken, g + base)
                    up(n, s, 0)
                    pe.wait_ge(b_taken, g + base)
                    up(n + 2, s + 2, 1)
                    pe.wait_ge(g_lo_done, g + base)
                    down(n + 4, s + 4, 0)
                n = n0 + 6 * (NG - 1) - 2
                pe.wait_ge(a_taken, base + NG - 1)
                up(n, n, 0)
                pe.wait_ge(b_taken, base + NG - 1)
                up(n + 2, n + 2, 1)
                pe.wait_ge(g_lo_done, base + NG - 1)
                down(n + 4, n + 4, 0)
                pe.wait_ge(g_lo_done, base + NG)
                pe.wait_ge(lo_done, n + 8)
                for m in range(KD):
                    for j in range(2):
                        mm = down_tile(n + 6, m, j, 1)
                    if m % 2:
                        mm.then_inc(acc_done, 1)
                if nxt.kind == "ple":
                    pe.wait_ge(p_lo_done, nxt.q + 1)
                pe.matmul(misc[:, 0:2], zeros_b[:, :], zeros_b[:, 0:2], start=True, stop=True).then_inc(pe_done, 2)

            pe.wait_ge(consts_ready, 5)
            pe.wait_ge(rows_landed, 16)
            for k in range(KD):
                for tb in range(TB):
                    mm = pe.transpose(acc[k // 2][:, k % 2, tb * P:(tb + 1) * P], rows_in[:, tb, k * P:(k + 1) * P],
                                      ident[:, :])
                if k % 2:
                    mm.then_inc(x_turned, 1)
            pe.wait_ge(gains_landed, 16 * len(stages))
            R = KD * len(stages)
            pe.transpose(misc[:, 0:R], gain_rows[0:R, :], ident[0:R, 0:R]).then_inc(gain_turned, 1)
            if any(o.kind == "s5" for o in stages):
                s5_turn()
            pe.wait_ge(masks_made, 7)
            for st, nxt in zip(stages, stages[1:] + [None]):
                if st.kind[:3] == "ffn":
                    ffn(st, nxt)
                if st.kind == "s5":
                    s5(st)
                if st.kind == "ple":
                    ple(st)
                if st.kind == "attn":
                    attention(st)
                if st.kind == "final":
                    stat_sum(st.v)
                    for tb in range(TB):
                        for k in range(KD):
                            if tb == 0:
                                pe.wait_ge(scaled, k + 1)
                            mm = pe.transpose(acc[2 * (tb % 2) + k // 4][:, :, :].rearrange("p a t -> p (a t)")
                                              [:, (k % 4) * P:(k % 4 + 1) * P], xT[:, k, tb * P:(tb + 1) * P], ident[:, :])
                            if k % 4 == 3:
                                mm.then_inc(out_turned, 1)


_INS = ['x', 'p', 'ffn1_norm', 'ffn1_w1', 'ffn1_w3', 'ffn1_w2', 'mix_norm', 'ffn2_norm', 'ffn2_w1', 'ffn2_w3',
        'ffn2_w2', 'ple_norm', 'ple_proj', 'ple_gate', 's5_w_in', 's5_a_re', 's5_a_im', 's5_log_dt', 's5_b_re',
        's5_b_im', 's5_c_re', 's5_c_im', 's5_d', 's5_w_glu', 'sb_w_qkv', 'sb_w_o', 'final_norm']
_OUTS = [((1, 256, 1024), 'float32')]


def kernel(**inputs):
    import numpy as _np
    import concourse.bacc as _bacc
    from concourse import mybir as _mybir
    from concourse.bass_utils import run_bass_kernel_spmd as _run

    nc = _bacc.Bacc("TRN2", target_bir_lowering=False, num_devices=1)
    arrays, args = {}, []
    for name in _INS:
        a = _np.ascontiguousarray(inputs[name])
        arrays[f"in_{name}_dram"] = a
        args.append(nc.dram_tensor(f"in_{name}_dram", a.shape, _mybir.dt.from_np(a.dtype), kind="ExternalInput").ap())
    for i, (shape, dtype) in enumerate(_OUTS):
        dt = _mybir.dt.from_np(_np.dtype(dtype))
        args.append(nc.dram_tensor(f"out_{i}_dram", shape, dt, kind="ExternalOutput").ap())
    hybrid_trunk(nc, *args)
    r = _run(nc, [arrays], core_ids=[0])
    got = tuple(r.results[0][f"out_{i}_dram"] for i in range(len(_OUTS)))
    return got[0]
```

```python
from contextlib import ExitStack

import concourse.bass as bass
from concourse import mybir

F32 = mybir.dt.float32
F32R = mybir.dt.float32r
BF16 = mybir.dt.bfloat16
ALU = mybir.AluOpType
ACT = mybir.ActivationFunctionType

P = 128
EPS = 1e-6
HALF = [0, 0, 1, 0, 1, 0, 1, 0, 1, 0]
TURN = 6.28125, 0.0019354820251464844, -1.7484556e-07
ROUND = 12582912.0


class Stage:

    def __init__(self, kind, layer, index, first_chunk, operand, ffn, gates, ples):
        self.kind, self.layer = kind, layer
        self.v = index
        self.n0 = first_chunk
        self.u = operand
        self.f = ffn
        self.e = gates
        self.q = ples


CHUNKS = {"ffn1": 66, "ffn2": 66, "s5": 24, "attn": 32, "ple": 10, "final": 0}
SETS = {"ffn1": 1, "ffn2": 1, "s5": 2, "attn": 2, "ple": 1, "final": 0}
KINDS = [("ffn1", 0), ("s5", 0), ("ffn2", 0), ("ple", 0), ("ffn1", 1), ("attn", 1), ("ffn2", 1), ("ple", 1), ("final", 1)]


def plan(kinds):
    stages, n, u, f, e, q = [], 0, 0, 0, 0, 0
    for index, (kind, layer) in enumerate(kinds):
        stages.append(Stage(kind, layer, index, n, u, f, e, q))
        e, q = e + 4 * (kind in ("s5", "ple")), q + (kind == "ple")
        n, u, f = n + CHUNKS[kind], u + SETS[kind], f + (kind[:3] == "ffn")
    return stages, n


def hybrid_trunk(nc, x, p, ffn1_norm, ffn1_w1, ffn1_w3, ffn1_w2, mix_norm, ffn2_norm, ffn2_w1, ffn2_w3, ffn2_w2,
                 ple_norm, ple_proj, ple_gate, s5_w_in, s5_a_re, s5_a_im, s5_log_dt, s5_b_re, s5_b_im,
                 s5_c_re, s5_c_im, s5_d, s5_w_glu, sb_w_qkv, sb_w_o, final_norm, out, kinds=KINDS):
    _, T, D = x.shape
    DFF = ffn1_w1.shape[2]
    KD = D // P
    TB = T // P
    NG = DFF // 256
    NB = KD // 2
    RING = 3
    stages, n_chunks = plan(kinds)
    NH, DH = 16, 64
    SCALE = DH ** -0.5
    MASKED = -1e30
    H, S = s5_b_re.shape[3], s5_b_re.shape[2]
    NQ = D // (2 * H)
    TAU, NC = 4, T // 4
    QG = 8
    STEPS = NH + 3
    DEPTH = 3
    norms = [ffn1_norm, mix_norm, ffn2_norm, ple_norm]
    norm_of = {"ffn1": 0, "s5": 1, "attn": 1, "ffn2": 2, "ple": 3}
    ffn_weights = {"ffn1": (ffn1_w1, ffn1_w3, ffn1_w2), "ffn2": (ffn2_w1, ffn2_w3, ffn2_w2)}

    with ExitStack() as ctx:
        top = [-(-nc.sbuf_base // 32) * 32]
        spot = {}

        def sb(name, shape, dt=F32, at=None):
            size = 2 if dt == BF16 else 4
            for d in shape[1:]:
                size *= d
            if at is None:
                at = top[0]
                top[0] += -(-size // 32) * 32
            spot[name] = at
            return nc.alloc_sbuf_tensor_at(name, shape, dt, offset=at)

        def sem(name):
            return ctx.enter_context(nc.semaphore(name))

        raw = sb("raw", [P, RING, 1024])
        w_hi = sb("w_hi", [P, RING, 1024], F32R)
        w_lo = sb("w_lo", [P, RING, 1024], F32R)
        xT = sb("xT", [P, KD, T])
        op_hi = sb("op_hi", [P, 2, KD, T], F32R)
        op_lo = sb("op_lo", [P, 2, KD, T], F32R)
        squares = sb("squares", [P, 2, 2, T])
        square_sum = sb("square_sum", [P, 2, T])
        mean_sq = sb("mean_sq", [P, TB])
        r_col = sb("r_col", [P, TB])
        minus_half = sb("minus_half", [P, TB])
        r_diag = sb("r_diag", [P, TB, P])
        r_row = sb("r_row", [P, T])
        gain_rows = sb("gain_rows", [9 * KD, P])
        gain = sb("gain", [P, 9 * KD])
        a_n = sb("a_n", [P, 2, T])
        b_n = sb("b_n", [P, 2, T])
        silu = sb("silu", [P, 2, T])
        prod = sb("prod", [P, 2, T])
        g_hi = sb("g_hi", [P, 2, 2, T], F32R)
        g_lo = sb("g_lo", [P, 2, 2, T], F32R)
        rows_in = sb("rows_in", [P, TB, D], at=spot["g_hi"])
        p_rows = sb("p_rows", [P, TB, T])
        s5_rows = sb("s5_rows", [NQ, 4, P])
        skip = sb("skip", [2 * H, NQ, 2 * H], at=spot["p_rows"])
        p_hi = sb("p_hi", [P, 2, T], F32R)
        p_lo = sb("p_lo", [P, 2, T], F32R)
        minus_tri = sb("minus_tri", [P, P])
        minus_ones = sb("minus_ones", [P, P])
        ident_b = sb("ident_b", [P, P], BF16)
        masked_b = sb("masked_b", [P, P], BF16)
        ident = sb("ident", [P, P])
        ones = sb("ones", [P, P])
        half_pi = sb("half_pi", [P, 1])
        zeros_b = sb("zeros_b", [P, P], BF16)

        half_1 = spot["op_hi"] + KD * T * 4, spot["op_lo"] + KD * T * 4
        mixer = top[0]
        w_in_state = sb("w_in_state", [P, 2, NQ, TAU, 2, H])
        w_state_out = sb("w_state_out", [P, 2, NQ, TAU + 1, 2, H])
        z_ops = sb("z_ops", [P, 2, NB, 4, T], F32R, at=spot["w_in_state"])
        turn_cos = sb("turn_cos", [P, NQ, NC])
        turn_sin = sb("turn_sin", [P, NQ, NC])
        decay = sb("decay", [P, NQ, NC])
        within = [sb(f"within{i}", [P, NQ // 2, P], at=half_1[i]) for i in range(2)]
        u_steps = sb("u_steps", [P, NQ, NC], at=spot["g_hi"])
        b_in = sb("b_in", [P, 2, NQ, H], at=half_1[0])
        c_in = sb("c_in", [P, 2, NQ, H], at=half_1[0] + 2 * NQ * H * 4)
        c_rows = sb("c_rows", [P, KD, 2, S], at=half_1[1])
        tmp = sb("tmp", [P, 2, NQ * 32], at=spot["decay"])
        small = sb("small", [P, 32, NQ], at=spot["p_hi"])
        scratch = sb("scratch", [P, 2, 512], at=spot["p_hi"])
        dt_rows = sb("dt_rows", [NQ, 2])

        kT = sb("kT", [P, KD, T], at=mixer)
        qT = sb("qT", [P, KD, T], at=mixer + 4 * KD * T)
        val = sb("val", [P, TB, D], at=mixer + 8 * KD * T)
        HW = T + P
        z_abs, z_exp, z_log, drop, att = (sb(name, [P, DEPTH, HW], at=mixer + 12 * KD * T + 4 * DEPTH * HW * i)
                                           for i, name in enumerate(("z_abs", "z_exp", "z_log", "drop", "att")))
        assert top[0] <= nc.sbuf_usable_end

        acc = [ctx.enter_context(nc.psum_tensor(f"acc{b}", [P, 2, T], F32)) for b in range(NB)]
        bank = [ctx.enter_context(nc.psum_tensor(f"bank{b}", [P, 2, T], F32)) for b in range(2)]
        stat = ctx.enter_context(nc.psum_tensor("stat", [P, 512], F32))
        misc = ctx.enter_context(nc.psum_tensor("misc", [P, 512], F32))

        raw_landed = [sem(f"raw_landed{s}") for s in range(RING)]
        hi_done, lo_done, pe_done = sem("hi_done"), sem("lo_done"), sem("pe_done")
        rows_landed = sem("rows_landed")
        gains_landed = sem("gains_landed")
        consts_ready = sem("consts_ready")
        ident_zeroed = sem("ident_zeroed")
        x_turned = sem("x_turned")
        p_landed = sem("p_landed")
        p_turned = sem("p_turned")
        p_hi_done, p_lo_done = sem("p_hi_done"), sem("p_lo_done")
        gate_taken, gate_ready, gated = sem("gate_taken"), sem("gate_ready"), sem("gated")
        masks_made = sem("masks_made")
        s5_landed, rows_spread, s5_turned, small_ready = (sem(n) for n in ("s5_landed", "rows_spread", "s5_turned", "small_ready"))
        c_landed, b_landed = sem("c_landed"), sem("b_landed")
        c_turned, c_ready = sem("c_turned"), sem("c_ready")
        angles_ready, phasors_ready = sem("angles_ready"), sem("phasors_ready")
        pool_step = sem("pool_step")
        weights_ready = sem("weights_ready")
        turns_ready = sem("turns_ready")
        block_done, block_skip, block_first, block_taken = (sem(n) for n in ("block_done", "block_skip", "block_first", "block_taken"))
        turned_done, turned_taken = sem("turned_done"), sem("turned_taken")
        u_scaled, u_placed = sem("u_scaled"), sem("u_placed")
        s_in_done, y_done = sem("s_in_done"), sem("y_done")
        dve_step = sem("dve_step")
        scanned, state_re, state_im = sem("scanned"), sem("state_re"), sem("state_im")
        imag_step = sem("imag_step")
        x_back = sem("x_back")
        gelu_done = sem("gelu_done")
        bank_taken = sem("bank_taken")
        z_done, abs_done, exp_done, log_done = sem("z_done"), sem("abs_done"), sem("exp_done"), sem("log_done")
        drop_done, drop_masked = sem("drop_done"), sem("drop_masked")
        exponent_done, att_done, o_done = sem("exponent_done"), sem("att_done"), sem("o_done")
        gain_turned = sem("gain_turned")
        gain_ready = sem("gain_ready")
        acc_done = sem("acc_done")
        x_new = sem("x_new")
        op_hi_done, op_lo_done = sem("op_hi_done"), sem("op_lo_done")
        squared = sem("squared")
        squares_used = sem("squares_used")
        sum_ready = sem("sum_ready")
        sum_col = sem("sum_col")
        mean_ready = sem("mean_ready")
        r_ready = sem("r_ready")
        diag_ready = sem("diag_ready")
        r_spread = sem("r_spread")
        r_row_ready = sem("r_row_ready")
        a_taken, b_taken = sem("a_taken"), sem("b_taken")
        silu_done, prod_done = sem("silu_done"), sem("prod_done")
        g_hi_done, g_lo_done = sem("g_hi_done"), sem("g_lo_done")
        out_turned = sem("out_turned")
        out_rows = sem("out_rows")
        stored = sem("stored")
        scaled = sem("scaled")

        def gain_col(st, k):
            i = (8 if st.kind == "final" else 2 * norm_of[st.kind] + st.layer) * KD + k
            return gain[:, i:i + 1]

        def a_chunk(w, half, col):
            return w[half * 512:(half + 1) * 512, col].rearrange("(k p) c -> p k c", p=P)

        def slot_a(buf, n):
            return buf[:, n % RING, :].rearrange("p (k c) -> p k c", k=4)

        GATE, OUT = 0, 1
        GLU = [(w, j, half) for half in range(2) for j in range(NB) for w in (GATE, OUT) if (w, j) != (OUT, NB - 1)] + \
              [(OUT, NB - 1, half) for half in range(2)]
        glu_bank = [[bank[0], bank[1], acc[2], misc], [acc[0], acc[1], acc[3], stat]]
        BETWEEN = {(2, 3): [("in", 0, 0)],
                   (3, 1): [("in", 0, 1)],
                   (4, 1): [("step", 0)], (4, 3): [("in", 1, 0)],
                   (5, 1): [("in", 1, 1)], (5, 3): [("out", 0, 0)],
                   (6, 1): [("out", 0, 1)], (6, 3): [("step", 1)],
                   (7, 1): [("out", 1, 0)], (7, 3): [("out", 1, 1), ("in", 2, 0), ("in", 2, 1)],
                   (8, 1): [("in", 3, 0)], (8, 3): [("in", 3, 1)],
                   (9, 1): [("step", 2)], (9, 3): [("out", 2, 0)],
                   (10, 1): [("out", 2, 1)],
                   (12, 1): [("step", 3), ("out", 3, 0)], (12, 3): [("out", 3, 1)]}
        DVE_WORK = {0: [("stats",)], 1: [("place", 0)], 3: [("back", 0), ("place", 1), ("scan", 0)],
                    5: [("back", 1), ("place", 2), ("scan", 1)], 6: [("low", 0)],
                    7: [("place", 3), ("low", 1), ("back", 2), ("scan", 2)], 8: [("back", 3), ("scan", 3)],
                    11: [("low", 2)], 13: [("low", 3)]}
        ACT_WORK = {1: [("place", 0)], 3: [("place", 1)], 5: [("place", 2)], 6: [("gelu", 0)],
                    7: [("place", 3), ("gelu", 1)], 10: [("gelu", 2)], 12: [("gelu", 3)]}
        y_bank = [stat, acc[0].rearrange("p a t -> p (a t)"), stat, stat]
        z_set = [o.u + 1 for o in stages if o.kind == "s5"]

        def peeled(nxt):
            return 3 if nxt.kind == "s5" else 1

        def block_at(c):
            i = c - (CHUNKS["ffn1"] - 4 - NQ // 2 + 1)
            return (i // 2, i % 2) if 0 <= i < NQ // 2 else (None, None)

        def operand(u, k):
            if u in z_set:
                return [z_ops[:, i, k // 2, k % 2, :] for i in range(2)]
            return op_hi[:, HALF[u], k, :], op_lo[:, HALF[u], k, :]

        OUT_ORDER = [(0, 0), (1, 0), (2, 0), (0, 1), (1, 1), (2, 1), (3, 0), (3, 1)]
        out_bank = [bank[0], bank[1], stat.rearrange("p (k t) -> p k t", k=2), misc.rearrange("p (k t) -> p k t", k=2)]
        z_bank = [acc[0].rearrange("p a t -> p (a t)"), acc[1].rearrange("p a t -> p (a t)"), misc]

        def step_chunk(st, s):
            return st.n0 + 12 + s if s < 18 else None

        block = ctx.enter_context(nc.Block())

        @block.sync
        def _(sp):
            def load(n, slot, src, shape_k):
                if not isinstance(n, int) or n >= RING:
                    sp.wait_ge(lo_done, n - (RING - 1))
                dst = raw[:, slot, :]
                if shape_k:
                    dst = dst.rearrange("p (k c) -> p k c", k=4)
                sp.dma_start(dst, src).then_inc(raw_landed[slot], 16)

            def load_ffn(st):
                w1, w3, w2 = (w[st.layer] for w in ffn_weights[st.kind])

                def pair(w, n, s, g):
                    for half in range(2):
                        load(n + half, (s + half) % RING, a_chunk(w, half, bass.ds(g * 256, 256)), True)

                def down(n, s, g):
                    for j in range(2):
                        load(n + j, (s + j) % RING, w2[bass.ds(g * 256 + j * P, P), :], False)
                pair(w1, st.n0, st.n0, 0)
                pair(w3, st.n0 + 2, st.n0 + 2, 0)
                with sp.Fori(1, NG) as g:
                    n, s = g * 6 + (st.n0 - 2), st.n0 + 4
                    pair(w1, n, s, g)
                    pair(w3, n + 2, s + 2, g)
                    down(n + 4, s + 4, g - 1)
                down(st.n0 + 6 * NG - 2, st.n0 + 6 * NG - 2, NG - 1)

            def load_group(n, w, col):
                for half in range(2):
                    load(n + half, (n + half) % RING, a_chunk(w, half, slice(col, col + 256)), True)

            def load_ple(st):
                for kt in range(2):
                    load(st.n0 + kt, (st.n0 + kt) % RING, ple_proj[st.layer, kt * P:(kt + 1) * P, :], False)
                for j in range(NB):
                    load_group(st.n0 + 2 + 2 * j, ple_gate[st.layer], 256 * j)

            def load_s5(st):
                for j in range(NB):
                    load_group(st.n0 + 2 * j, s5_w_in[0], 256 * j)
                for i, (which, j, half) in enumerate(GLU):
                    n, col = st.n0 + 8 + i, (D if which == GATE else 0) + 256 * j
                    load(n, n % RING, a_chunk(s5_w_glu[0], half, slice(col, col + 256)), True)

            def load_attn(st):
                w = sb_w_qkv[0]
                for j in range(NB):
                    load_group(st.n0 + 2 * j, w, 2 * D + 256 * j)
                for j in range(NB):
                    load_group(st.n0 + 8 + 4 * j, w, D + 256 * j)
                    load_group(st.n0 + 10 + 4 * j, w, 256 * j)
                for i, (j, half) in enumerate(OUT_ORDER):
                    n = st.n0 + 24 + i
                    load(n, n % RING, a_chunk(sb_w_o[0], half, slice(256 * j, 256 * j + 256)), True)

            sp.dma_start(rows_in[:, 0, :], x[0, 0:P, :]).then_inc(rows_landed, 16)
            for st, nxt in zip(stages, stages[1:] + [None]):
                if nxt is not None and nxt.kind == "ple":
                    if any(o.kind == "s5" for o in stages):
                        sp.wait_ge(block_skip, 8)
                    if nxt.q:
                        sp.wait_ge(p_turned, nxt.q)
                    sp.dma_start(p_rows[:, :, :],
                                 p[nxt.layer, 0].rearrange("(b p) c -> p b c", p=P)).then_inc(p_landed, 16)
                if st.kind[:3] == "ffn":
                    load_ffn(st)
                if st.kind == "s5":
                    load_s5(st)
                if st.kind == "ple":
                    load_ple(st)
                if st.kind == "attn":
                    load_attn(st)
                if st.kind == "final":
                    for tb in range(TB):
                        sp.wait_ge(out_rows, 2 * (tb + 1))
                        sp.dma_start(out[0, tb * P:(tb + 1) * P, :], rows_in[:, tb, :]).then_inc(stored, 16)
                    sp.wait_ge(stored, 16 * TB)

        @block.gpsimd
        def _(pool):
            pool.memset(ident[:, :], 0.0).then_inc(ident_zeroed, 1)
            pool.memset(ones[:, :], 1.0).then_inc(consts_ready, 1)
            pool.memset(minus_half[:, :], -0.5).then_inc(consts_ready, 1)
            pool.memset(zeros_b[:, :], 0.0).then_inc(consts_ready, 1)
            pool.memset(half_pi[:, :], 1.5707963267948966).then_inc(consts_ready, 1)
            pool.wait_ge(ident_zeroed, 1)
            pool.affine_select(out=ident[:, :], in_=ident[:, :], compare_op=ALU.not_equal, fill=1.0, base=0,
                               pattern=[[-1, P]], channel_multiplier=1).then_inc(consts_ready, 1)

            def norm(v):
                sq = squares_used
                pool.wait_ge(squared, 4 * v + 2)
                if v:
                    pool.wait_ge(sum_col, v)
                pool.tensor_tensor(square_sum[:, :, :], squares[:, 0], squares[:, 1], ALU.add).then_inc(sq, 2)
                for b in (2, 3):
                    pool.wait_ge(sq, 4 * v + b)
                    pool.wait_ge(squared, 4 * v + b + 1)
                    pool.tensor_tensor(square_sum[:, :, :], square_sum[:, :, :], squares[:, b % 2], ALU.add)\
                        .then_inc(sq, 1)
                pool.wait_ge(sq, 4 * v + 4)
                pool.tensor_tensor(square_sum[:, 0], square_sum[:, 0], square_sum[:, 1], ALU.add).then_inc(sum_ready, 1)
                pool.wait_ge(mean_ready, v + 1)
                pool.tensor_tensor(r_col[:, :], mean_sq[:, :], minus_half[:, :], ALU.pow).then_inc(r_ready, 1)
            pool.wait_ge(consts_ready, 5)
            pool.memset(minus_tri[:, :], -1.0).then_inc(masks_made, 1)
            pool.memset(minus_ones[:, :], -1.0).then_inc(masks_made, 1)
            pool.memset(ident_b[:, :], 0.0).then_inc(masks_made, 1)
            pool.memset(masked_b[:, :], 0.0).then_inc(masks_made, 1)
            pool.wait_ge(masks_made, 4)
            pool.affine_select(out=minus_tri[:, :], in_=minus_tri[:, :], compare_op=ALU.is_ge, fill=0.0, base=0,
                               pattern=[[-1, P]], channel_multiplier=1).then_inc(masks_made, 1)
            pool.affine_select(out=ident_b[:, :], in_=ident_b[:, :], compare_op=ALU.not_equal, fill=1.0, base=0,
                               pattern=[[-1, P]], channel_multiplier=1).then_inc(masks_made, 1)
            pool.affine_select(out=masked_b[:, :], in_=masked_b[:, :], compare_op=ALU.is_gt, fill=MASKED, base=0,
                               pattern=[[1, P]], channel_multiplier=-1).then_inc(masks_made, 1)

            def attention():
                for h in range(NH):
                    pool.wait_ge(drop_done, h + 1)
                    for c in (0, T):
                        d = drop[:, h % DEPTH, c:c + P]
                        pool.affine_select(out=d, in_=d, compare_op=ALU.is_gt, fill=0.0, base=0,
                                           pattern=[[1, P]], channel_multiplier=-1).then_inc(drop_masked, 1)

            links = [0]

            def link(ins):
                links[0] += 1
                ins.then_inc(pool_step, 1)
                pool.wait_ge(pool_step, links[0])

            def tt(o, a, b, op=ALU.mult):
                link(pool.tensor_tensor(o, a, b, op))

            def ts(o, a, m, b):
                link(pool.tensor_scalar(o, a, m, b, ALU.mult, ALU.add))

            def sm(i):
                return small[:, i, :]

            def s5_parameters():
                lam_re, lam_im, dt, skip_col, decay_log, angle, mag, cos, sin, fr, fi, t0, t1, t2 = range(14)
                A, F, E, M4 = 14, 22, 30, mag
                link(pool.memset(w_in_state[:, :, :, :, :, :], 0.0))
                link(pool.memset(w_state_out[:, :, :, :, :, :], 0.0))
                pool.wait_ge(small_ready, 3)
                pool.wait_ge(angles_ready, 2)
                tt(skip[:, :, :], ident[0:32, 0:32].unsqueeze(1).broadcast_to([32, NQ, 32]),
                   sm(skip_col)[0:32].unsqueeze(2).broadcast_to([32, NQ, 32]))
                pool.wait_ge(phasors_ready, 3)
                pool.wait_ge(b_landed, 16 * 2)
                pool.wait_ge(c_ready, 2)

                def product(o_re, o_im, a_re, a_im, b_re, b_im, x, y):
                    tt(x, a_re, b_re)
                    tt(y, a_im, b_im)
                    tt(o_re, x, y, ALU.subtract)
                    tt(x, a_re, b_im)
                    tt(y, a_im, b_re)
                    tt(o_im, x, y, ALU.add)

                a_re = [None] + [sm(A + j) for j in range(4)]
                a_im = [None] + [sm(A + 4 + j) for j in range(4)]
                tt(a_re[1], sm(mag), sm(cos))
                tt(a_im[1], sm(mag), sm(sin))
                link(pool.tensor_scalar(sm(decay_log), a_re[1], -1.0, None, ALU.add))
                tt(sm(t0), sm(decay_log), sm(lam_re))
                tt(sm(t1), a_im[1], sm(lam_im))
                tt(sm(fr), sm(t0), sm(t1), ALU.add)
                tt(sm(t0), a_im[1], sm(lam_re))
                tt(sm(t1), sm(decay_log), sm(lam_im))
                tt(sm(fi), sm(t0), sm(t1), ALU.subtract)
                tt(sm(F + 3), sm(fr), sm(t2))
                tt(sm(F + 7), sm(fi), sm(t2))
                for j in (2, 3, 4):
                    product(a_re[j], a_im[j], a_re[j - 1], a_im[j - 1], a_re[1], a_im[1], sm(t0), sm(t1))
                for tau in range(TAU - 1):
                    j = TAU - 1 - tau
                    product(sm(F + tau), sm(F + 4 + tau), a_re[j], a_im[j], sm(F + 3), sm(F + 7), sm(t0), sm(t1))
                for _ in range(2):
                    tt(sm(mag), sm(mag), sm(mag))

                def over(x, n):
                    return x.unsqueeze(2).broadcast_to([P, NQ, n])
                xy = [tmp[:, i, 0:NQ * H].rearrange("p (q h) -> p q h", h=H) for i in range(2)]

                def both(o, part, j, op):
                    for e in range(2):
                        r = slice(64 * e, 64 * e + 64)
                        tt(o[r, part, :, j, e, :], xy[0][r], xy[1][r], op)
                for tau in range(TAU):
                    f_re, f_im = over(sm(F + tau), H), over(sm(F + 4 + tau), H)
                    tt(xy[0], f_re, b_in[:, 0])
                    tt(xy[1], f_im, b_in[:, 1])
                    both(w_in_state, 0, tau, ALU.subtract)
                    tt(xy[0], f_re, b_in[:, 1])
                    tt(xy[1], f_im, b_in[:, 0])
                    both(w_in_state, 1, tau, ALU.add)
                for e in range(2):
                    r = slice(64 * e, 64 * e + 64)
                    for part in range(2):
                        link(pool.tensor_copy(w_state_out[r, part, :, 0, e, :], c_in[r, part]))
                for j in range(1, TAU + 1):
                    p_re, p_im = over(a_re[j], H), over(a_im[j], H)
                    tt(xy[0], c_in[:, 0], p_re)
                    tt(xy[1], c_in[:, 1], p_im)
                    both(w_state_out, 0, j, ALU.add)
                    tt(xy[0], c_in[:, 1], p_re)
                    tt(xy[1], c_in[:, 0], p_im)
                    both(w_state_out, 1, j, ALU.subtract)
                for i in range(2):
                    link(pool.memset(within[i][:, :, :], 0.0))
                pool.memset(minus_half[:, :], -0.5).then_inc(weights_ready, 1)
                e_re, e_im = sm(E), sm(E + 1)
                product(e_re, e_im, sm(cos), sm(sin), sm(cos), sm(sin), sm(t0), sm(t1))
                product(sm(fr), sm(fi), e_re, e_im, e_re, e_im, sm(t0), sm(t1))
                link(pool.memset(turn_cos[:, :, 0:1], 1.0))
                link(pool.memset(turn_sin[:, :, 0:1], 0.0))
                n, cur, new = 1, (sm(fr), sm(fi)), (e_re, e_im)
                while n < NC:
                    xn = [tmp[:, i, 0:NQ * n].rearrange("p (q c) -> p q c", c=n) for i in range(2)]
                    product(turn_cos[:, :, n:2 * n], turn_sin[:, :, n:2 * n], turn_cos[:, :, 0:n], turn_sin[:, :, 0:n],
                            over(cur[0], n), over(cur[1], n), *xn)
                    product(*new, *cur, *cur, sm(t0), sm(t1))
                    cur, new, n = new, cur, 2 * n
                ts(decay[:, :, :], over(sm(mag), NC), 1.0, 0.0)
                pool.memset(decay[:, :, 0:1], 0.0).then_inc(turns_ready, 1)

            def s5_mix():
                for g in range(NQ // QG):
                    cos, sin = (t[:, QG * g:QG * g + QG, :].rearrange("p q c -> p (q c)") for t in (turn_cos, turn_sin))
                    pool.wait_ge(scanned, 2 * g + 2)
                    pool.tensor_tensor(scratch[:, 0, :], b_n.rearrange("p a t -> p (a t)"), sin, ALU.mult).then_inc(imag_step, 1)
                    s_im = squares[:, 1].rearrange("p a t -> p (a t)")
                    if g:
                        pool.wait_ge(y_done, g)
                    pool.tensor_tensor(s_im, prod.rearrange("p a t -> p (a t)"), cos, ALU.mult).then_inc(imag_step, 1)
                    pool.wait_ge(imag_step, 2 * g + 2)
                    pool.tensor_tensor(s_im, s_im, scratch[:, 0, :], ALU.add).then_inc(state_im, 1)

            for st in stages:
                norm(st.v)
                if st.v == 0 and any(o.kind == "s5" for o in stages):
                    s5_parameters()
                if st.kind == "s5":
                    s5_mix()
                if st.kind == "attn":
                    attention()

        @block.scalar
        def _(act):
            act.dma_start(rows_in[:, 1, :], x[0, P:2 * P, :]).then_inc(rows_landed, 16)
            for i, src in enumerate(norms):
                act.dma_start(gain_rows[2 * i * KD:2 * (i + 1) * KD, :], src.rearrange("l (k p) -> (l k) p", p=P))\
                    .then_inc(gains_landed, 16)
            act.dma_start(gain_rows[8 * KD:9 * KD, :], final_norm.rearrange("(k p) -> k p", p=P)).then_inc(gains_landed, 16)
            act.dma_start(s5_rows[:, 0, :], s5_a_re[0].rearrange("(q e) p -> q (e p)", e=2)).then_inc(s5_landed, 16)
            act.dma_start(s5_rows[:, 1, :], s5_a_im[0].rearrange("(q e) p -> q (e p)", e=2)).then_inc(s5_landed, 16)
            act.dma_start(dt_rows[:, :], s5_log_dt[0].rearrange("(q e) -> q e", e=2)).then_inc(s5_landed, 16)
            act.dma_start(s5_rows[:, 3, 0:2 * H], s5_d[0].rearrange("(q c) -> q c", q=NQ)).then_inc(s5_landed, 16)
            for i, c in enumerate((s5_c_re, s5_c_im)):
                act.dma_start(c_rows[:, :, i], c[0].rearrange("(k g) h p -> (g h) k p", k=KD)).then_inc(c_landed, 16)
            for i, b in enumerate((s5_b_re, s5_b_im)):
                act.dma_start(b_in[:, i], b[0].rearrange("(q e) p h -> (e p) q h", e=2)).then_inc(b_landed, 16)

            def split_hi(n, slot, uses):
                act.wait_ge(raw_landed[slot], uses * 16)
                if not isinstance(n, int) or n >= RING:
                    act.wait_ge(pe_done, n - (RING - 1))
                act.activation(w_hi[:, slot, :], raw[:, slot, :], ACT.Copy).then_inc(hi_done, 1)

            def split(n):
                if n < n_chunks:
                    split_hi(n, n % RING, n // RING + 1)

            def prep(v, u, banks=range(NB)):
                for b in banks:
                    act.wait_ge(x_new, 4 * v + b + 1)
                    if u is not None:
                        for k in (2 * b, 2 * b + 1):
                            act.activation(op_hi[:, HALF[u], k, :], xT[:, k, :], ACT.Copy,
                                           scale=gain_col(stages[v], k)).then_inc(op_hi_done, 1)
                    if b >= 2 or v > 0:
                        act.wait_ge(squares_used, 4 * v + 2 * (b >= 2))
                    act.activation(squares[:, b % 2], xT[:, 2 * b:2 * b + 2, :], ACT.Square).then_inc(squared, 1)

            def ffn(st, nxt):
                n0, base = st.n0, NG * st.f

                def do_silu(g):
                    act.wait_ge(a_taken, base + g + 1)
                    if st.f or not isinstance(g, int) or g:
                        act.wait_ge(prod_done, base + g)
                    act.activation(silu[:, :, :], a_n[:, :, :], ACT.Silu).then_inc(silu_done, 1)

                def do_g_hi(g, half):
                    act.wait_ge(prod_done, base + g + 1)
                    act.activation(g_hi[:, half], prod[:, :, :], ACT.Copy).then_inc(g_hi_done, 1)
                split(n0 + 2)
                if nxt.kind == "s5":
                    s5_take()
                split(n0 + 3)
                split(n0 + 4)
                split(n0 + 5)
                do_silu(0)
                if nxt.kind == "ple":
                    p_high(nxt.q)
                if nxt.kind == "s5":
                    s5_phasors()

                def part(n, j, g):
                    m = n0 + j - 2
                    split_hi(n + j, m % RING, g * 2 + (m // RING + 1))
                    if nxt.kind == "s5" and isinstance(n, int):
                        s5_blocks(n + j - 3 - n0)

                def group(g):
                    n = g * 6 + (n0 - 2)
                    part(n, 2, g)
                    do_g_hi(g - 1, 0)
                    part(n, 3, g)
                    part(n, 4, g)
                    part(n, 5, g)
                    do_silu(g)
                    part(n, 6, g)
                    if not isinstance(g, int) or g < NG - 1:
                        part(n, 7, g)
                with act.Fori(1, NG - peeled(nxt)) as g:
                    group(g)
                for g in range(NG - peeled(nxt), NG):
                    group(g)
                n = n0 + 6 * (NG - 1) - 2
                do_g_hi(NG - 1, 1)
                part(n, 7, NG - 1)
                split(n + 8)
                prep(nxt.v, nxt.u if nxt.kind != "final" else None, [0, 1])
                split(n + 9)
                prep(nxt.v, nxt.u if nxt.kind != "final" else None, [2, 3])

            def p_high(q):
                act.wait_ge(p_turned, q + 1)
                act.activation(p_hi[:, :, :], misc[:, :].rearrange("p (k t) -> p k t", k=2), ACT.Copy).then_inc(p_hi_done, 1)

            def ple(st, nxt):
                split(st.n0 + 2)
                split(st.n0 + 3)
                for j in range(NB):
                    split(st.n0 + 4 + 2 * j)
                    if j < NB - 1:
                        split(st.n0 + 5 + 2 * j)
                    act.wait_ge(gate_taken, 4 * st.q + j + 1)
                    if st.e or j:
                        act.wait_ge(gated, st.e + j)
                    act.activation(silu[:, :, :], a_n[:, :, :], ACT.Sigmoid).then_inc(gate_ready, 1)
                    prep(nxt.v, nxt.u if nxt.kind != "final" else None, [j])
                split(st.n0 + 11)

            def s5_in():
                act.wait_ge(s5_landed, 16 * 4)
                act.activation(s5_rows[:, 2, :].rearrange("q (e p) -> q e p", e=2),
                               dt_rows[:, :].unsqueeze(2).broadcast_to([NQ, 2, S]), ACT.Copy).then_inc(rows_spread, 1)

            def s5_take():
                act.wait_ge(s5_turned, 1)
                act.activation(small[:, 2, :], misc[:, P + NQ * 2:P + NQ * 3], ACT.Exp).then_inc(small_ready, 1)
                act.activation(small[:, 0:2, :].rearrange("p i q -> p (i q)"), misc[:, P:P + 2 * NQ], ACT.Copy).then_inc(small_ready, 1)
                act.activation(small[0:2 * H, 3, :], misc[0:2 * H, P + NQ * 3:P + NQ * 4], ACT.Copy).then_inc(small_ready, 1)

            def s5_phasors():
                act.wait_ge(angles_ready, 1)
                act.activation(small[:, 6, :], small[:, 4, :], ACT.Exp).then_inc(phasors_ready, 1)
                act.activation(small[:, 8, :], small[:, 5, :], ACT.Sin).then_inc(phasors_ready, 1)
                act.activation(small[:, 7, :], small[:, 5, :], ACT.Abs).then_inc(rows_spread, 1)
                act.wait_ge(rows_spread, 2)
                act.activation(small[:, 7, :], small[:, 7, :], ACT.Sin, scale=-1.0, bias=half_pi[:, 0:1]).then_inc(phasors_ready, 1)

            def s5_blocks(c):
                i, second = block_at(c)
                if i is None or second:
                    return
                act.wait_ge(block_first, i + 1)
                o = within[i // 4][:, 4 * (i % 4):4 * (i % 4) + 4, :]
                for quad in (2, 3):
                    r = slice(32 * quad, 32 * quad + 32)
                    act.activation(o[r, :, 32 * quad:P], o[0:32, :, 0:P - 32 * quad], ACT.Copy).then_inc(block_taken, 1)
                act.wait_ge(turned_done, 2 * i + 1)
                act.activation(w_in_state[:, 0, 4 * i:4 * i + 4].rearrange("p q t e h -> p (q t e h)"), stat[:, :],
                               ACT.Copy).then_inc(turned_taken, 1)

            def s5(st, nxt):
                n0, zu = st.n0, st.u + 1
                scaled_u = scratch[:, 1, :].rearrange("p (k c t) -> p k c t", k=2, t=TAU)

                def place(j):
                    act.wait_ge(u_scaled, j + 1)
                    for quad in (2, 3):
                        for tau in range(TAU):
                            src = scaled_u[32 * quad:32 * quad + 32, :, :, tau]
                            dst = u_steps[32 * tau:32 * tau + 32, 8 * j:8 * j + 8, :].rearrange("p (k j) c -> p k j c", k=2)[:, :, quad, :]
                            act.activation(dst, src, ACT.Copy).then_inc(u_placed, 1)
                zf = square_sum

                def gelu(g):
                    act.wait_ge(y_done, g + 1)
                    if g:
                        act.wait_ge(op_lo_done, KD * zu + 2 * g)
                    y = y_bank[g].rearrange("p (k j c) -> p k j c", k=2, c=NC)
                    for quad in range(4):
                        for tau in range(TAU):
                            dst = zf[32 * quad:32 * quad + 32].rearrange("p k (c t) -> p k c t", t=TAU)[:, :, :, tau]
                            act.activation(dst, y[32 * tau:32 * tau + 32, :, quad, :], ACT.Gelu_apprx_tanh).then_inc(gelu_done, 1)
                    act.wait_ge(gelu_done, 16 * g + 16)
                    act.activation(z_ops[:, 0, g, 0:2, :], zf[:, :, :], ACT.Copy).then_inc(op_hi_done, 2)
                for i in range(24):
                    split(n0 + i + 2)
                    for kind, g in ACT_WORK.get(i, []):
                        {"place": place, "gelu": gelu}[kind](g)
                    if i >= 8:
                        which, j, half = GLU[i - 8]
                        if half and which == GATE:
                            act.wait_ge(pe_done, n0 + i + 1)
                            if st.e or j:
                                act.wait_ge(gated, st.e + j)
                            gate = glu_bank[GATE][j]
                            if j == NB - 1:
                                gate = gate.rearrange("p (k t) -> p k t", k=2)
                            act.activation(silu[:, :, :], gate[:, :, :], ACT.Sigmoid).then_inc(gate_ready, 1)
                        if half and which == OUT:
                            prep(nxt.v, nxt.u, [j])

            def attention(st, nxt):
                n0, o_set = st.n0, st.u + 1
                act.wait_ge(gated, st.e)
                act.preload_act_table_set("natural_log_exp_and_others")
                split(n0 + 2)
                split(n0 + 3)
                for j in range(NB):
                    split(n0 + 4 + 2 * j)
                    act.wait_ge(r_ready, st.v + 1)
                    act.wait_ge(pe_done, n0 + 2 * j + 2)
                    for tb in range(TB):
                        act.activation(val[:, tb, 256 * j:256 * j + 256], bank[j % 2][:, tb, :], ACT.Copy,
                                       scale=r_col[:, tb:tb + 1]).then_inc(bank_taken, 1)
                    split(n0 + 5 + 2 * j)
                for n in (n0 + 12, n0 + 13):
                    split(n)
                for s in range(STEPS):
                    h = s
                    if h < NH:
                        act.wait_ge(z_done, h + 1)
                        act.activation(z_abs[:, h % DEPTH], z_bank[h % DEPTH][:, 0:HW], ACT.Abs).then_inc(abs_done, 1)
                        act.wait_ge(abs_done, h + 1)
                        act.activation(z_exp[:, h % DEPTH], z_abs[:, h % DEPTH], ACT.Exp, scale=-1.0).then_inc(exp_done, 1)
                        act.wait_ge(exp_done, h + 1)
                        if h >= DEPTH:
                            act.wait_ge(drop_done, h - DEPTH + 1)
                        act.activation(z_log[:, h % DEPTH], z_exp[:, h % DEPTH], ACT.Ln, bias=1.0).then_inc(log_done, 1)
                    h = s - 2
                    if 0 <= h < NH:
                        act.wait_ge(exponent_done, h + 1)
                        if h >= DEPTH:
                            act.wait_ge(o_done, h - DEPTH + 1)
                        act.activation(att[:, h % DEPTH], z_bank[h % DEPTH][:, 0:HW], ACT.Exp).then_inc(att_done, 1)
                    if s < 16:
                        split(step_chunk(st, s) + 2)
                    h = s - 3
                    if 0 <= h and h % 2:
                        act.wait_ge(o_done, h + 1)
                        act.activation(op_hi[:, HALF[o_set], h // 2, :], acc[2 + h // 2 % 2][:, 0, :], ACT.Copy)\
                            .then_inc(op_hi_done, 1)
                split(n0 + 30)
                prep(nxt.v, nxt.u, [0])
                split(n0 + 31)
                prep(nxt.v, nxt.u, [1])
                split(n0 + 32)
                prep(nxt.v, nxt.u, [2])
                prep(nxt.v, nxt.u, [3])
                split(n0 + 33)

            act.wait_ge(gain_turned, 1)
            act.activation(gain[:, :], misc[:, 0:9 * KD], ACT.Copy).then_inc(gain_ready, 1)
            act.wait_ge(gain_ready, 1)
            prep(0, 0, [0])
            split(0)
            prep(0, 0, [1])
            split(1)
            prep(0, 0, [2, 3])
            if any(o.kind == "s5" for o in stages):
                s5_in()
            for st, nxt in zip(stages, stages[1:] + [None]):
                if st.kind[:3] == "ffn":
                    ffn(st, nxt)
                if st.kind == "s5":
                    s5(st, nxt)
                if st.kind == "ple":
                    ple(st, nxt)
                if st.kind == "attn":
                    attention(st, nxt)

        @block.vector
        def _(dve):
            def split_lo(n, slot):
                dve.wait_ge(hi_done, n + 1)
                dve.tensor_tensor(w_lo[:, slot, :], raw[:, slot, :], w_hi[:, slot, :].bitcast(F32), ALU.subtract)\
                    .then_inc(lo_done, 1)

            def split(n):
                if n < n_chunks:
                    split_lo(n, n % RING)

            def op_low(v, u, b):
                if u is None:
                    return
                for k in (2 * b, 2 * b + 1):
                    dve.wait_ge(op_hi_done, KD * u + k + 1)
                    dve.scalar_tensor_tensor(out=op_lo[:, HALF[u], k, :], in0=xT[:, k, :],
                                             scalar=gain_col(stages[v], k),
                                             in1=op_hi[:, HALF[u], k, :].bitcast(F32), op0=ALU.mult, op1=ALU.subtract)\
                        .then_inc(op_lo_done, 1)

            def stat_mean(v):
                dve.wait_ge(sum_col, v + 1)
                dve.tensor_scalar(mean_sq[:, :], stat[:, 0:TB], 1.0 / D, EPS, ALU.mult, ALU.add).then_inc(mean_ready, 1)

            def stat_diag(v):
                dve.wait_ge(r_ready, v + 1)
                for tb in range(TB):
                    dve.tensor_scalar(r_diag[:, tb, :], ident[:, :], r_col[:, tb:tb + 1], None, ALU.mult)\
                        .then_inc(diag_ready, 1)

            def stat_row(v):
                dve.wait_ge(r_spread, v + 1)
                dve.tensor_copy(r_row[:, :], stat[:, 256:256 + T]).then_inc(r_row_ready, 1)

            def residual_from_acc(v, u, f, n):
                dve.wait_ge(x_new, 4 * v)
                for b in range(NB):
                    dve.wait_ge(acc_done, NB * f + b + 1)
                    dve.scalar_tensor_tensor(out=xT[:, 2 * b:2 * b + 2, :], in0=acc[b][:, :, :], scalar=0.5,
                                             in1=xT[:, 2 * b:2 * b + 2, :], op0=ALU.mult, op1=ALU.add).then_inc(x_new, 1)
                    if 0 < b < NB - 1:
                        op_low(v, u, b - 1)
                split(n)
                op_low(v, u, NB - 2)
                op_low(v, u, NB - 1)

            def c_take():
                for b in range(2):
                    dve.wait_ge(c_turned, b + 1)
                    t = acc[b].rearrange("p a t -> p (a t)").rearrange("p (q e h) -> p q e h", e=2, h=H)
                    for i in range(2):
                        for e in range(2):
                            ins = dve.tensor_scalar(c_in[S * e:S * e + S, i, 16 * b:16 * b + 16, :], t[S * i:S * i + S, :, e, :],
                                                    1.0 - 2 * i, None, ALU.mult)
                    ins.then_inc(c_ready, 1)

            links = [0]

            def link(ins, n=1):
                links[0] += 1
                ins.then_inc(dve_step, 1)
                if n:
                    dve.wait_ge(dve_step, links[0])

            def s5_angles():
                lam_re, lam_im, dt, decay_log, angle, t0, t1, t2 = (small[:, i, :] for i in (0, 1, 2, 4, 5, 11, 12, 13))
                dve.wait_ge(small_ready, 3)
                link(dve.tensor_tensor(angle, lam_im, dt, ALU.mult), 0)
                link(dve.tensor_scalar(lam_re, lam_re, -1e-4, None, ALU.min))
                link(dve.tensor_scalar(t0, angle, 1.0 / (2 * 3.141592653589793), ROUND, ALU.mult, ALU.add), 0)
                link(dve.tensor_tensor(decay_log, lam_re, dt, ALU.mult))
                link(dve.tensor_scalar(t0, t0, -ROUND, None, ALU.add))
                for part in TURN:
                    link(dve.scalar_tensor_tensor(out=angle, in0=t0, scalar=-part, in1=angle, op0=ALU.mult, op1=ALU.add))
                dve.tensor_scalar(angle, angle, 3.1415925, -3.1415925, ALU.min, ALU.max).then_inc(angles_ready, 1)
                link(dve.tensor_tensor(t1, lam_re, lam_re, ALU.mult), 0)
                link(dve.tensor_tensor(t2, lam_im, lam_im, ALU.mult))
                link(dve.tensor_tensor(t1, t1, t2, ALU.add))
                dve.reciprocal(t2, t1).then_inc(angles_ready, 1)

            r_bc = r_row[:, :].unsqueeze(1).broadcast_to([P, 2, T])

            def ffn(st, nxt):
                n0, base, v = st.n0, NG * st.f, st.v

                def take_a(n, g):
                    dve.wait_ge(pe_done, n + 1)
                    if st.f or not isinstance(g, int) or g:
                        dve.wait_ge(silu_done, base + g)
                    dve.tensor_tensor(a_n[:, :, :], bank[0][:, :, :], r_bc, ALU.mult).then_inc(a_taken, 1)

                def take_b(n, g):
                    dve.wait_ge(pe_done, n + 1)
                    dve.tensor_tensor(b_n[:, :, :], bank[1][:, :, :], r_bc, ALU.mult).then_inc(b_taken, 1)
                    dve.wait_ge(silu_done, base + g + 1)
                    dve.wait_ge(b_taken, base + g + 1)
                    if st.f or not isinstance(g, int) or g:
                        dve.wait_ge(g_hi_done, base + g)
                    dve.tensor_tensor(prod[:, :, :], silu[:, :, :], b_n[:, :, :], ALU.mult).then_inc(prod_done, 1)

                def do_g_lo(g, half):
                    dve.wait_ge(g_hi_done, base + g + 1)
                    dve.tensor_tensor(g_lo[:, half], prod[:, :, :], g_hi[:, half].bitcast(F32), ALU.subtract)\
                        .then_inc(g_lo_done, 1)
                split(n0 + 2)
                if nxt.kind == "s5":
                    c_take()
                split(n0 + 3)
                split(n0 + 4)
                stat_mean(v)
                stat_diag(v)
                split(n0 + 5)
                stat_row(v)
                dve.wait_ge(r_row_ready, v + 1)
                take_a(n0 + 1, 0)
                if nxt.kind == "s5":
                    s5_angles()
                take_b(n0 + 3, 0)
                if nxt.kind == "ple":
                    dve.wait_ge(p_hi_done, nxt.q + 1)
                    dve.tensor_tensor(p_lo[:, :, :], misc[:, :].rearrange("p (k t) -> p k t", k=2), p_hi[:, :, :].bitcast(F32),
                                      ALU.subtract).then_inc(p_lo_done, 1)

                def part(n, j):
                    split_lo(n + j, (n0 + j - 2) % RING)
                    if nxt.kind == "s5" and isinstance(n, int):
                        s5_blocks(n + j - 3 - n0)

                def group(g):
                    n = g * 6 + (n0 - 2)
                    part(n, 2)
                    do_g_lo(g - 1, 0)
                    part(n, 3)
                    part(n, 4)
                    take_a(n + 1, g)
                    part(n, 5)
                    part(n, 6)
                    take_b(n + 3, g)
                    if not isinstance(g, int) or g < NG - 1:
                        part(n, 7)
                with dve.Fori(1, NG - peeled(nxt)) as g:
                    group(g)
                for g in range(NG - peeled(nxt), NG):
                    group(g)
                n = n0 + 6 * (NG - 1) - 2
                do_g_lo(NG - 1, 1)
                part(n, 7)
                split(n + 8)
                residual_from_acc(nxt.v, nxt.u if nxt.kind != "final" else None, st.f, n + 9)

            def ple(st, nxt):
                n0, v = st.n0, nxt.v
                u = nxt.u if nxt.kind != "final" else None
                split(n0 + 2)
                stat_mean(st.v)
                split(n0 + 3)
                stat_diag(st.v)
                stat_row(st.v)
                for j in range(NB):
                    split(n0 + 4 + 2 * j)
                    if j < NB - 1:
                        split(n0 + 5 + 2 * j)
                    dve.wait_ge(pe_done, n0 + 4 + 2 * j)
                    dve.wait_ge(r_row_ready, st.v + 1)
                    if st.e or j:
                        dve.wait_ge(gate_ready, st.e + j)
                    dve.tensor_tensor(a_n[:, :, :], bank[j % 2][:, :, :], r_bc, ALU.mult).then_inc(gate_taken, 1)
                    if j:
                        op_low(v, u, j - 1)
                    dve.wait_ge(gate_ready, st.e + j + 1)
                    dve.tensor_tensor(b_n[:, :, :], acc[j][:, :, :], silu[:, :, :], ALU.mult).then_inc(gated, 1)
                    dve.wait_ge(gated, st.e + j + 1)
                    dve.wait_ge(x_new, 4 * v)
                    xj = xT[:, 2 * j:2 * j + 2, :]
                    dve.tensor_tensor(xj, xj, b_n[:, :, :], ALU.add).then_inc(x_new, 1)
                op_low(v, u, NB - 1)
                split(n0 + 11)

            def s5_blocks(c):
                i, second = block_at(c)
                if i is None:
                    return
                if second:
                    dve.wait_ge(turned_done, 2 * i + 2)
                    dve.tensor_copy(w_in_state[:, 1, 4 * i:4 * i + 4].rearrange("p q t e h -> p (q t e h)"), stat[:, :])\
                        .then_inc(turned_taken, 1)
                    return
                o = within[i // 4][:, 4 * (i % 4):4 * (i % 4) + 4, :]
                kk = misc.rearrange("p (q c) -> p q c", q=4)
                dve.wait_ge(block_done, i + 1)
                dve.tensor_tensor(kk[0:32, :, 0:32], kk[0:32, :, 0:32], skip[:, 4 * i:4 * i + 4, :], ALU.add).then_inc(block_skip, 1)
                dve.wait_ge(block_skip, i + 1)
                dve.tensor_copy(o[0:32], kk[0:32]).then_inc(block_first, 1)
                dve.tensor_copy(o[32:64, :, 32:P], kk[0:32, :, 0:P - 32]).then_inc(block_taken, 2)

            def s5(st, nxt):
                n0, zu, v, u = st.n0, st.u + 1, nxt.v, nxt.u
                scaled_u = scratch[:, 1, :].rearrange("p (k c t) -> p k c t", k=2, t=TAU)

                def place(j):
                    dve.wait_ge(pe_done, n0 + 2 * j + 2)
                    if j:
                        dve.wait_ge(u_placed, 16 * j)
                    dve.tensor_tensor(scratch[:, 1, :].rearrange("p (k t) -> p k t", k=2), bank[j % 2][:, :, :], r_bc, ALU.mult)\
                        .then_inc(u_scaled, 1)
                    dve.wait_ge(u_scaled, j + 1)
                    for quad in (0, 1):
                        for tau in range(TAU):
                            src = scaled_u[32 * quad:32 * quad + 32, :, :, tau]
                            dst = u_steps[32 * tau:32 * tau + 32, 8 * j:8 * j + 8, :].rearrange("p (k j) c -> p k j c", k=2)[:, :, quad, :]
                            dve.tensor_copy(dst, src).then_inc(u_placed, 1)
                A, B, C, E = (t.rearrange("p a t -> p (a t)") for t in (a_n, b_n, silu, prod))
                s_re = squares[:, 0].rearrange("p a t -> p (a t)")
                zf = square_sum

                def z_low(g):
                    dve.wait_ge(op_hi_done, KD * zu + 2 * g + 2)
                    dve.tensor_tensor(z_ops[:, 1, g, 0:2, :], zf[:, :, :], z_ops[:, 0, g, 0:2, :].bitcast(F32), ALU.subtract)\
                        .then_inc(op_lo_done, 2)

                def tables(g):
                    return (t[:, QG * g:QG * g + QG, :].rearrange("p q c -> p (q c)") for t in (turn_cos, turn_sin, decay))

                def stats():
                    stat_mean(st.v)
                    stat_diag(st.v)
                    stat_row(st.v)
                    dve.wait_ge(r_row_ready, st.v + 1)

                def turn_back(g):
                    cos, sin, _ = tables(g)
                    dve.wait_ge(turns_ready, 1)
                    x_re, x_im = acc[3].rearrange("p a t -> p (a t)"), misc[:, :]
                    dve.wait_ge(s_in_done, g + 1)
                    if g:
                        dve.wait_ge(state_im, g)
                        dve.wait_ge(state_re, g)
                    link(dve.tensor_tensor(A, x_re, cos, ALU.mult), 0)
                    link(dve.tensor_tensor(B, x_im, sin, ALU.mult), 0)
                    link(dve.tensor_tensor(C, x_im, cos, ALU.mult), 0)
                    link(dve.tensor_tensor(E, x_re, sin, ALU.mult))
                    link(dve.tensor_tensor(A, A, B, ALU.add), 0)
                    dve.tensor_tensor(C, C, E, ALU.subtract).then_inc(x_back, 1)

                def scan(g):
                    cos, sin, fall = tables(g)
                    dve.wait_ge(dve_step, links[0])
                    dve.tensor_tensor_scan(B, fall, A, 0.0, ALU.mult, ALU.add).then_inc(scanned, 1)
                    dve.wait_ge(x_back, g + 1)
                    dve.tensor_tensor_scan(E, fall, C, 0.0, ALU.mult, ALU.add).then_inc(scanned, 1)
                    dve.wait_ge(scanned, 2 * g + 2)
                    link(dve.tensor_tensor(A, B, cos, ALU.mult), 0)
                    link(dve.tensor_tensor(C, E, sin, ALU.mult))
                    if g:
                        dve.wait_ge(y_done, g)
                    dve.tensor_tensor(s_re, A, C, ALU.subtract).then_inc(state_re, 1)

                for i in range(24):
                    split(n0 + i + 2)
                    for kind, *g in DVE_WORK.get(i, []):
                        {"stats": stats, "place": place, "back": turn_back, "scan": scan, "low": z_low}[kind](*g)
                    if i >= 8:
                        which, j, half = GLU[i - 8]
                        if half and which == OUT:
                            dve.wait_ge(pe_done, n0 + i + 1)
                            dve.wait_ge(gate_ready, st.e + j + 1)
                            y = glu_bank[OUT][j]
                            if j == NB - 1:
                                y = y.rearrange("p (k t) -> p k t", k=2)
                            dve.tensor_tensor(b_n[:, :, :], y[:, :, :], silu[:, :, :], ALU.mult).then_inc(gated, 1)
                            dve.wait_ge(gated, st.e + j + 1)
                            dve.wait_ge(x_new, 4 * v)
                            xj = xT[:, 2 * j:2 * j + 2, :]
                            dve.tensor_tensor(xj, xj, b_n[:, :, :], ALU.add).then_inc(x_new, 1)
                            op_low(v, u, j)

            def attention(st, nxt):
                n0, o_set = st.n0, st.u + 1

                def take_kq(j, which):
                    dve.wait_ge(pe_done, n0 + 10 + 4 * j + 2 * which)
                    dst = (kT, qT)[which][:, 2 * j:2 * j + 2, :]
                    if which:
                        op = dve.scalar_tensor_tensor(out=dst, in0=bank[1][:, :, :], scalar=SCALE, in1=r_bc,
                                                      op0=ALU.mult, op1=ALU.mult)
                    else:
                        op = dve.tensor_tensor(dst, bank[0][:, :, :], r_bc, ALU.mult)
                    op.then_inc(bank_taken, 2)

                def take_out(j):
                    xj = xT[:, 2 * j:2 * j + 2, :]
                    dve.wait_ge(x_new, 4 * nxt.v)
                    dve.tensor_tensor(xj, xj, out_bank[j][:, :, :], ALU.add).then_inc(x_new, 1)

                split(n0 + 2)
                split(n0 + 3)
                split(n0 + 4)
                stat_mean(st.v)
                stat_diag(st.v)
                split(n0 + 5)
                stat_row(st.v)
                for n in range(n0 + 6, n0 + 12):
                    split(n)
                dve.wait_ge(r_row_ready, st.v + 1)
                dve.wait_ge(bank_taken, 8)
                take_kq(0, 0)
                split(n0 + 12)
                split(n0 + 13)
                take_kq(0, 1)
                for s in range(STEPS):
                    if s in (2, 4, 6, 8, 10, 12):
                        take_kq((s - 1) // 4 + 1, (s - 1) // 2 % 2)
                    if s < 16:
                        split(step_chunk(st, s) + 2)
                    h = s
                    if h < NH:
                        dve.wait_ge(log_done, h + 1)
                        if h >= DEPTH:
                            dve.wait_ge(exponent_done, h - DEPTH + 1)
                        dve.scalar_tensor_tensor(out=drop[:, h % DEPTH], in0=z_bank[h % DEPTH][:, 0:HW], scalar=0.0,
                                                 in1=z_log[:, h % DEPTH], op0=ALU.max, op1=ALU.add).then_inc(drop_done, 1)
                    h = s - 3
                    if 0 <= h and h % 2:
                        dve.wait_ge(op_hi_done, KD * o_set + h // 2 + 1)
                        dve.tensor_tensor(op_lo[:, HALF[o_set], h // 2, :], acc[2 + h // 2 % 2][:, 0, :],
                                          op_hi[:, HALF[o_set], h // 2, :].bitcast(F32), ALU.subtract).then_inc(op_lo_done, 1)
                dve.wait_ge(pe_done, n0 + 28)
                take_out(0)
                split(n0 + 30)
                op_low(nxt.v, nxt.u, 0)
                dve.wait_ge(pe_done, n0 + 29)
                take_out(1)
                split(n0 + 31)
                op_low(nxt.v, nxt.u, 1)
                dve.wait_ge(pe_done, n0 + 30)
                take_out(2)
                split(n0 + 32)
                op_low(nxt.v, nxt.u, 2)
                dve.wait_ge(pe_done, n0 + 32)
                take_out(3)
                op_low(nxt.v, nxt.u, 3)
                split(n0 + 33)

            for b in range(NB):
                dve.wait_ge(x_turned, b + 1)
                dve.tensor_copy(xT[:, 2 * b:2 * b + 2, :], acc[b][:, :, :]).then_inc(x_new, 1)
            dve.wait_ge(gain_ready, 1)
            op_low(0, 0, 0)
            split(0)
            op_low(0, 0, 1)
            split(1)
            op_low(0, 0, 2)
            op_low(0, 0, 3)
            for st, nxt in zip(stages, stages[1:] + [None]):
                if st.kind[:3] == "ffn":
                    ffn(st, nxt)
                if st.kind == "s5":
                    s5(st, nxt)
                if st.kind == "ple":
                    ple(st, nxt)
                if st.kind == "attn":
                    attention(st, nxt)
                if st.kind == "final":
                    stat_mean(st.v)
                    dve.wait_ge(squared, 4 * st.v + 4)
                    dve.wait_ge(x_new, 4 * st.v + 4)
                    for k in range(KD):
                        dve.tensor_scalar(xT[:, k, :], xT[:, k, :], gain_col(st, k), None,
                                          ALU.mult).then_inc(scaled, 1)
                    dve.wait_ge(r_ready, st.v + 1)
                    for tb in range(TB):
                        for h in range(2):
                            dve.wait_ge(out_turned, 2 * tb + h + 1)
                            dve.tensor_scalar(rows_in[:, tb, h * 512:(h + 1) * 512], acc[2 * (tb % 2) + h][:, :, :]
                                              .rearrange("p a t -> p (a t)"), r_col[:, tb:tb + 1], None, ALU.mult)\
                                .then_inc(out_rows, 1)

        @block.tensor
        def _(pe):
            def products(o, wh, wl, xh, xl, start, stop):
                pe.matmul(o, wh, xh, start=start, stop=False, skip_group_check=True)
                pe.matmul(o, wl, xh, start=False, stop=False, skip_group_check=True)
                return pe.matmul(o, wh, xl, start=False, stop=stop, skip_group_check=True)

            def stat_sum(v):
                pe.wait_ge(sum_ready, v + 1)
                for tb in range(TB):
                    mm = pe.matmul(stat[:, tb:tb + 1], square_sum[:, 0, tb * P:(tb + 1) * P], ones[:, 0:1],
                                   start=True, stop=True)
                mm.then_inc(sum_col, 1)

            def stat_spread(v):
                for tb in range(TB):
                    pe.wait_ge(diag_ready, TB * v + tb + 1)
                    mm = pe.matmul(stat[:, 256 + tb * P:256 + (tb + 1) * P], ones[:, :], r_diag[:, tb, :],
                                   start=True, stop=True)
                mm.then_inc(r_spread, 1)

            def chunk_a(n, slot, half, o, u, ready=True, hooks={}, kks=range(4)):
                pe.wait_ge(lo_done, n + 1)
                for kk in kks:
                    k = 4 * half + kk
                    if not ready:
                        pe.wait_ge(op_lo_done, KD * u + k + 1)
                    for m in range(2):
                        wh, wl = (w[:, slot, (kk * 2 + m) * P:(kk * 2 + m + 1) * P] for w in (w_hi, w_lo))
                        mm = products(o[:, m, :], wh, wl, *operand(u, k), k == 0 and m == 0, k == KD - 1)
                    if kk == 3:
                        mm.then_inc(pe_done, 1)
                    if k in hooks:
                        hooks[k]()

            def open_acc():
                for b in range(NB):
                    pe.matmul(acc[b][:, 0, 0:2], zeros_b[:, :], zeros_b[:, 0:2], start=True, stop=True,
                              skip_group_check=True)

            def group(n, o, u, **kw):
                for half in range(2):
                    chunk_a(n + half, (n + half) % RING, half, o, u, **kw)

            def ple(st):
                n0, u = st.n0, st.u
                pe.wait_ge(p_lo_done, st.q + 1)
                for kt in range(2):
                    pe.wait_ge(lo_done, n0 + kt + 1)
                    for m in range(KD):
                        if kt == 0 and m % 2 == 0:
                            pe.wait_ge(x_new, 4 * st.v + m // 2 + 1)
                        wh, wl = (w[:, (n0 + kt) % RING, m * P:(m + 1) * P] for w in (w_hi, w_lo))
                        mm = products(acc[m // 2][:, m % 2, :], wh, wl, p_hi[:, kt, :], p_lo[:, kt, :],
                                      kt == 0 and m % 2 == 0, kt == 1)
                    mm.then_inc(pe_done, 1)
                    if kt == 0:
                        pass
                stat_sum(st.v)
                group(n0 + 2, bank[0], u, ready=False, hooks={3: lambda: stat_spread(st.v)})
                group(n0 + 4, bank[1], u)
                for j in (2, 3):
                    pe.wait_ge(gate_taken, 4 * st.q + j - 1)
                    group(n0 + 2 + 2 * j, bank[j % 2], u)

            def s5_turn():
                pe.wait_ge(s5_landed, 16 * 4)
                pe.wait_ge(rows_spread, 1)
                for i in range(3):
                    pe.transpose(misc[:, P + NQ * i:P + NQ * (i + 1)], s5_rows[:, i, :], ident[0:NQ, 0:NQ])
                pe.transpose(misc[0:2 * H, P + NQ * 3:P + NQ * 4], s5_rows[:, 3, 0:2 * H], ident[0:NQ, 0:NQ]).then_inc(s5_turned, 1)
                pe.wait_ge(c_landed, 16 * 2)
                for k in range(KD):
                    mm = pe.transpose(acc[k // 4].rearrange("p a t -> p (a t)")[:, P * (k % 4):P * (k % 4) + P],
                                      c_rows[:, k].rearrange("p i s -> p (i s)"), ident[:, :])
                    if k % 4 == 3:
                        mm.then_inc(c_turned, 1)

            def s5_blocks(c):
                i, second = block_at(c)
                if i is None:
                    return
                if i == 0:
                    pe.wait_ge(weights_ready, 1)
                if not second:
                    pe.wait_ge(block_taken, 4 * i)
                    pe.wait_ge(turned_taken, 2 * i)
                    for q in range(4):
                        for part in range(2):
                            lhs = w_in_state[:, part, 4 * i + q, TAU - 1, :, :].rearrange("p e h -> p (e h)")
                            rhs = w_state_out[:, part, 4 * i + q, 0:TAU].rearrange("p t e h -> p (t e h)")
                            mm = pe.matmul(misc[0:32, P * q:P * q + P], lhs, rhs, start=part == 0, stop=part == 1)
                    mm.then_inc(block_done, 1)
                pe.wait_ge(turned_taken, 2 * i + second)
                for q in range(4):
                    mm = pe.transpose(stat[:, P * q:P * q + P], w_in_state[:, second, 4 * i + q].rearrange("p t e h -> p (t e h)"),
                                      ident[:, :])
                mm.then_inc(turned_done, 1)

            def s5(st):
                n0, u = st.n0, st.u
                pe.wait_ge(block_taken, 32)
                pe.wait_ge(turned_taken, 16)

                def state_in(g, part):
                    if part == 0:
                        pe.wait_ge(u_placed, 16 * (g + 1))
                        if g:
                            pe.wait_ge(x_back, g)
                    o = (acc[3].rearrange("p a t -> p (a t)"), misc)[part]
                    for q in range(QG):
                        w = w_in_state[:, part, QG * g + q].rearrange("p t e h -> p (t e h)")
                        mm = pe.matmul(o[:, NC * q:NC * q + NC], w, u_steps[:, QG * g + q, :], start=True, stop=True)
                    if part:
                        mm.then_inc(s_in_done, 1)

                def step_out(g):
                    pe.wait_ge(r_row_ready, st.v + 1)
                    if g >= 2:
                        pe.wait_ge(gelu_done, 16 * g)
                    for q in range(QG):
                        qq = QG * g + q
                        pe.matmul(y_bank[g][:, NC * q:NC * q + NC], within[qq // 16][:, qq % 16, :], u_steps[:, qq, :],
                                  start=q == 0, stop=False, skip_group_check=True)

                def state_out(g, part):
                    pe.wait_ge((state_re, state_im)[part], g + 1)
                    states = squares[:, part].rearrange("p a t -> p (a t)")
                    for q in range(QG):
                        w = w_state_out[:, part, QG * g + q, 1:TAU + 1].rearrange("p t e h -> p (t e h)")
                        mm = pe.matmul(y_bank[g][:, NC * q + 1:NC * q + NC], w, states[:, NC * q:NC * q + NC - 1], start=False,
                                       stop=part == 1, skip_group_check=True)
                    if part:
                        mm.then_inc(y_done, 1)

                work = {"in": state_in, "step": step_out, "out": state_out}

                def between(i, k):
                    for kind, *which in BETWEEN.get((i, k), []):
                        work[kind](*which)

                def at(i):
                    h = 4 * (i % 2) if i < 8 else 4 * GLU[i - 8][2]
                    hooks = {h + k: lambda k=k: between(i, k) for k in range(4)}
                    if i == 1:
                        hooks = {h: lambda: stat_sum(st.v), h + 3: lambda: stat_spread(st.v)}
                    return hooks
                for i in range(24):
                    n = n0 + i
                    if i < 8:
                        if i >= 4 and i % 2 == 0:
                            pe.wait_ge(u_scaled, i // 2 - 1)
                        chunk_a(n, n % RING, i % 2, bank[i // 2 % 2], u, ready=i >= 2,
                                hooks=at(i))
                    else:
                        which, j, half = GLU[i - 8]
                        if which == GATE and j < 2 and half == 0:
                            pe.wait_ge(u_scaled, 3 + j)
                        if j >= 2 and half == 0:
                            pe.wait_ge(x_back, 4)
                        pe.wait_ge(op_lo_done, KD * (u + 1) + 4 * (half + 1))
                        o = glu_bank[which][j]
                        if j == NB - 1:
                            o = o.rearrange("p (k t) -> p k t", k=2)
                        chunk_a(n, n % RING, half, o, u + 1, hooks=at(i))

            def head_step(s):
                h = s
                if h < NH:
                    j, q0 = h // 2, DH * (h % 2)
                    zb = z_bank[h % DEPTH]
                    pe.wait_ge(bank_taken, 8 + 4 * (h // 4 + 1))
                    if h >= DEPTH:
                        pe.wait_ge(att_done, h - DEPTH + 1)
                    pe.matmul(zb[:, 0:T], kT[q0:q0 + DH, j, 0:P], qT[q0:q0 + DH, j, :], start=True, stop=True,
                              skip_group_check=True)
                    pe.matmul(zb[:, T:HW], kT[q0:q0 + DH, j, P:T], qT[q0:q0 + DH, j, P:T], start=False, stop=True,
                              skip_group_check=True).then_inc(z_done, 1)
                h = s - 2
                if 0 <= h < NH:
                    zb = z_bank[h % DEPTH]
                    pe.wait_ge(drop_masked, 2 * h + 2)
                    d = drop[:, h % DEPTH]

                    def add(o, a, b):
                        return pe.matmul(o, a, b, start=False, stop=True, skip_group_check=True)
                    add(zb[:, 0:T], minus_tri[:, :], d[:, 0:T])
                    add(zb[:, P:T], minus_ones[:, :], d[:, T:HW])
                    add(zb[:, T:HW], minus_tri[:, :], d[:, T:HW])
                    add(zb[:, 0:P], ident_b[:, :], masked_b[:, :])
                    add(zb[:, T:HW], ident_b[:, :], masked_b[:, :]).then_inc(exponent_done, 1)
                h = s - 3
                if 0 <= h:
                    j, q0 = h // 2, DH * (h % 2)
                    o = acc[2 + j % 2][q0:q0 + DH, 0, :]
                    pe.wait_ge(att_done, h + 1)
                    if j >= 2 and h % 2 == 0:
                        pe.wait_ge(op_lo_done, KD * o_set[0] + j - 1)
                    pe.matmul(o, val[:, 0, h * DH:(h + 1) * DH], att[:, h % DEPTH, 0:T], start=True, stop=True,
                              skip_group_check=True)
                    pe.matmul(o[:, P:T], val[:, 1, h * DH:(h + 1) * DH], att[:, h % DEPTH, T:HW], start=False, stop=True,
                              skip_group_check=True).then_inc(o_done, 1)

            o_set = [0]

            def attention(st):
                n0, u = st.n0, st.u
                o_set[0] = u + 1
                for j in range(NB):
                    if j >= 2:
                        pe.wait_ge(bank_taken, 2 * j - 2)
                    for half in range(2):
                        n = n0 + 2 * j + half
                        pe.wait_ge(lo_done, n + 1)
                        for kk in range(4):
                            k = 4 * half + kk
                            if j == 0:
                                pe.wait_ge(op_lo_done, KD * u + k + 1)
                            wh, wl = (w[:, n % RING, kk * 256:(kk + 1) * 256] for w in (w_hi, w_lo))
                            for tb in range(TB):
                                xh, xl = (o[:, HALF[u], k, tb * P:(tb + 1) * P] for o in (op_hi, op_lo))
                                start = k == 0 and tb == 0
                                pe.matmul(bank[j % 2][:, tb, :], xh, wh, start=start, stop=False, skip_group_check=True)
                                pe.matmul(bank[j % 2][:, tb, :], xh, wl, start=False, stop=False, skip_group_check=True)
                                mm = pe.matmul(bank[j % 2][:, tb, :], xl, wh, start=False, stop=k == KD - 1,
                                               skip_group_check=True)
                            if kk == 3:
                                mm.then_inc(pe_done, 1)
                            if j == 1 and k == 0:
                                stat_sum(st.v)
                            if j == 1 and k == 6:
                                stat_spread(st.v)
                pe.wait_ge(bank_taken, 6)
                group(n0 + 8, bank[0], u)
                pe.wait_ge(bank_taken, 8)
                group(n0 + 10, bank[1], u)
                for s in range(STEPS):
                    if s < 12:
                        if s % 2 == 0:
                            pe.wait_ge(bank_taken, 8 + 4 * (s // 4) + 2 + 2 * (s // 2 % 2))
                        n = n0 + 12 + s
                        chunk_a(n, n % RING, s % 2, bank[s // 2 % 2], u)
                    elif s < 18:
                        n = n0 + 12 + s
                        j, half = OUT_ORDER[s - 12]
                        if half == 0:
                            pe.wait_ge(bank_taken, (22, 24, 24)[j])
                        pe.wait_ge(op_lo_done, KD * (u + 1) + 4 + 2 * half)
                        chunk_a(n, n % RING, half, out_bank[j], u + 1, kks=range(4 - 2 * half))
                    head_step(s)
                for i, (j, half) in enumerate(OUT_ORDER[3:]):
                    n = n0 + 27 + i
                    if j == 3 and half == 0:
                        pe.wait_ge(att_done, NH)
                    chunk_a(n, n % RING, half, out_bank[j], u + 1, ready=False, kks=range(2 if i < 3 else 0, 4))

            def ffn(st, nxt):
                n0, base, v, u = st.n0, NG * st.f, st.v, st.u

                def up(n, s, which, **kw):
                    for half in range(2):
                        chunk_a(n + half, (s + half) % RING, half, bank[which], u, **kw)
                        behind(n + half)

                def down_tile(s, m, j, half):
                    wh, wl = (w[:, (s + j) % RING, m * P:(m + 1) * P] for w in (w_hi, w_lo))
                    return products(acc[m // 2][:, m % 2, :], wh, wl, g_hi[:, half, j, :], g_lo[:, half, j, :], False, False)

                def behind(n):
                    if nxt.kind == "s5" and isinstance(n, int):
                        s5_blocks(n - n0)

                def down(n, s, half):
                    for j in range(2):
                        pe.wait_ge(lo_done, n + j + 1)
                        for m in range(KD):
                            mm = down_tile(s, m, j, half)
                        mm.then_inc(pe_done, 1)
                        behind(n + j)
                if st.v:
                    pe.wait_ge(x_new, 4 * v)
                    pe.wait_ge(gate_taken, 4 * st.q)
                if st.e:
                    pe.wait_ge(gate_ready, st.e - 1)
                up(n0, n0, 0, ready=False, hooks={3: s5_turn} if nxt.kind == "s5" else {})
                pe.wait_ge(x_new, 4 * v + 4)
                if nxt.kind == "s5":
                    pe.wait_ge(c_ready, 2)
                open_acc()
                if nxt.kind == "ple":
                    pe.wait_ge(p_landed, 16 * (nxt.q + 1))
                    pe.wait_ge(gain_ready, 1)
                    for kt in range(2):
                        for tb in range(TB):
                            mm = pe.transpose(misc[:, kt * T + tb * P:kt * T + (tb + 1) * P],
                                              p_rows[:, tb, kt * P:(kt + 1) * P], ident[:, :])
                    mm.then_inc(p_turned, 1)
                if st.f:
                    pe.wait_ge(b_taken, base)
                if st.e:
                    pe.wait_ge(gate_ready, st.e)
                up(n0 + 2, n0 + 2, 1, hooks={0: lambda: stat_sum(v), 4: lambda: stat_spread(v)})

                def whole(g):
                    n, s = g * 6 + (n0 - 2), n0 + 4
                    pe.wait_ge(a_taken, g + base)
                    up(n, s, 0)
                    pe.wait_ge(b_taken, g + base)
                    up(n + 2, s + 2, 1)
                    pe.wait_ge(g_lo_done, g + base)
                    down(n + 4, s + 4, 0)
                with pe.Fori(1, NG - peeled(nxt)) as g:
                    whole(g)
                for g in range(NG - peeled(nxt), NG):
                    whole(g)
                n = n0 + 6 * (NG - 1) - 2
                pe.wait_ge(g_lo_done, base + NG)
                pe.wait_ge(lo_done, n + 8)
                for m in range(KD):
                    for j in range(2):
                        mm = down_tile(n + 6, m, j, 1)
                    if m % 2:
                        mm.then_inc(acc_done, 1)
                if nxt.kind == "s5":
                    pe.wait_ge(block_taken, 32)
                if nxt.kind == "ple":
                    pe.wait_ge(p_lo_done, nxt.q + 1)
                pe.matmul(misc[:, 0:2], zeros_b[:, :], zeros_b[:, 0:2], start=True, stop=True).then_inc(pe_done, 2)

            pe.wait_ge(consts_ready, 5)
            pe.wait_ge(rows_landed, 16 * TB)
            for k in range(KD):
                for tb in range(TB):
                    mm = pe.transpose(acc[k // 2][:, k % 2, tb * P:(tb + 1) * P], rows_in[:, tb, k * P:(k + 1) * P],
                                      ident[:, :])
                if k % 2:
                    mm.then_inc(x_turned, 1)
            pe.wait_ge(gains_landed, 16 * 5)
            R = 9 * KD
            pe.transpose(misc[:, 0:R], gain_rows[0:R, :], ident[0:R, 0:R]).then_inc(gain_turned, 1)
            pe.wait_ge(masks_made, 7)
            for st, nxt in zip(stages, stages[1:] + [None]):
                if st.kind[:3] == "ffn":
                    ffn(st, nxt)
                if st.kind == "s5":
                    s5(st)
                if st.kind == "ple":
                    ple(st)
                if st.kind == "attn":
                    attention(st)
                if st.kind == "final":
                    stat_sum(st.v)
                    for tb in range(TB):
                        for k in range(KD):
                            if tb == 0:
                                pe.wait_ge(scaled, k + 1)
                            mm = pe.transpose(acc[2 * (tb % 2) + k // 4][:, :, :].rearrange("p a t -> p (a t)")
                                              [:, (k % 4) * P:(k % 4 + 1) * P], xT[:, k, tb * P:(tb + 1) * P], ident[:, :])
                            if k % 4 == 3:
                                mm.then_inc(out_turned, 1)


_INS = ['x', 'p', 'ffn1_norm', 'ffn1_w1', 'ffn1_w3', 'ffn1_w2', 'mix_norm', 'ffn2_norm', 'ffn2_w1', 'ffn2_w3',
        'ffn2_w2', 'ple_norm', 'ple_proj', 'ple_gate', 's5_w_in', 's5_a_re', 's5_a_im', 's5_log_dt', 's5_b_re',
        's5_b_im', 's5_c_re', 's5_c_im', 's5_d', 's5_w_glu', 'sb_w_qkv', 'sb_w_o', 'final_norm']
_OUTS = [((1, 256, 1024), 'float32')]


def kernel(**inputs):
    import numpy as _np
    import concourse.bacc as _bacc
    from concourse import mybir as _mybir
    from concourse.bass_utils import run_bass_kernel_spmd as _run

    nc = _bacc.Bacc("TRN2", target_bir_lowering=False, num_devices=1)
    arrays, args = {}, []
    for name in _INS:
        a = _np.ascontiguousarray(inputs[name])
        arrays[f"in_{name}_dram"] = a
        args.append(nc.dram_tensor(f"in_{name}_dram", a.shape, _mybir.dt.from_np(a.dtype), kind="ExternalInput").ap())
    for i, (shape, dtype) in enumerate(_OUTS):
        dt = _mybir.dt.from_np(_np.dtype(dtype))
        args.append(nc.dram_tensor(f"out_{i}_dram", shape, dt, kind="ExternalOutput").ap())
    hybrid_trunk(nc, *args)
    r = _run(nc, [arrays], core_ids=[0])
    got = tuple(r.results[0][f"out_{i}_dram"] for i in range(len(_OUTS)))
    return got[0]
```

```python
from contextlib import ExitStack

import concourse.bass as bass
from concourse import mybir

F32 = mybir.dt.float32
F32R = mybir.dt.float32r
BF16 = mybir.dt.bfloat16
ALU = mybir.AluOpType
ACT = mybir.ActivationFunctionType

P = 128
EPS = 1e-6
HALF = [0, 0, 1, 0, 1, 0, 1, 0, 1, 0]
TURN = 6.28125, 0.0019354820251464844, -1.7484556e-07
ROUND = 12582912.0


class Stage:

    def __init__(self, kind, layer, index, first_chunk, operand, ffn, gates, ples):
        self.kind, self.layer = kind, layer
        self.v = index
        self.n0 = first_chunk
        self.u = operand
        self.f = ffn
        self.e = gates
        self.q = ples


CHUNKS = {"ffn1": 66, "ffn2": 66, "s5": 24, "attn": 32, "ple": 10, "final": 0}
SETS = {"ffn1": 1, "ffn2": 1, "s5": 2, "attn": 2, "ple": 1, "final": 0}
KINDS = [("ffn1", 0), ("s5", 0), ("ffn2", 0), ("ple", 0), ("ffn1", 1), ("attn", 1), ("ffn2", 1), ("ple", 1), ("final", 1)]


def plan(kinds):
    stages, n, u, f, e, q = [], 0, 0, 0, 0, 0
    for index, (kind, layer) in enumerate(kinds):
        stages.append(Stage(kind, layer, index, n, u, f, e, q))
        e, q = e + 4 * (kind in ("s5", "ple")), q + (kind == "ple")
        n, u, f = n + CHUNKS[kind], u + SETS[kind], f + (kind[:3] == "ffn")
    return stages, n


def hybrid_trunk(nc, x, p, ffn1_norm, ffn1_w1, ffn1_w3, ffn1_w2, mix_norm, ffn2_norm, ffn2_w1, ffn2_w3, ffn2_w2,
                 ple_norm, ple_proj, ple_gate, s5_w_in, s5_a_re, s5_a_im, s5_log_dt, s5_b_re, s5_b_im,
                 s5_c_re, s5_c_im, s5_d, s5_w_glu, sb_w_qkv, sb_w_o, final_norm, out, kinds=KINDS):
    _, T, D = x.shape
    DFF = ffn1_w1.shape[2]
    KD = D // P
    TB = T // P
    NG = DFF // 256
    NB = KD // 2
    RING = 3
    stages, n_chunks = plan(kinds)
    NH, DH = 16, 64
    SCALE = DH ** -0.5
    MASKED = -1e30
    H, S = s5_b_re.shape[3], s5_b_re.shape[2]
    NQ = D // (2 * H)
    TAU, NC = 4, T // 4
    QG = 8
    STEPS = NH + 3
    DEPTH = 3
    norms = [ffn1_norm, mix_norm, ffn2_norm, ple_norm]
    norm_of = {"ffn1": 0, "s5": 1, "attn": 1, "ffn2": 2, "ple": 3}
    ffn_weights = {"ffn1": (ffn1_w1, ffn1_w3, ffn1_w2), "ffn2": (ffn2_w1, ffn2_w3, ffn2_w2)}

    with ExitStack() as ctx:
        top = [-(-nc.sbuf_base // 32) * 32]
        spot = {}

        def sb(name, shape, dt=F32, at=None):
            size = 2 if dt == BF16 else 4
            for d in shape[1:]:
                size *= d
            if at is None:
                at = top[0]
                top[0] += -(-size // 32) * 32
            spot[name] = at
            return nc.alloc_sbuf_tensor_at(name, shape, dt, offset=at)

        def sem(name):
            return ctx.enter_context(nc.semaphore(name))

        raw = sb("raw", [P, RING, 1024])
        w_hi = sb("w_hi", [P, RING, 1024], F32R)
        w_lo = sb("w_lo", [P, RING, 1024], F32R)
        xT = sb("xT", [P, KD, T])
        op_hi = sb("op_hi", [P, 2, KD, T], F32R)
        op_lo = sb("op_lo", [P, 2, KD, T], F32R)
        squares = sb("squares", [P, 2, 2, T])
        square_sum = sb("square_sum", [P, 2, T])
        mean_sq = sb("mean_sq", [P, TB])
        r_col = sb("r_col", [P, TB])
        minus_half = sb("minus_half", [P, TB])
        r_diag = sb("r_diag", [P, TB, P])
        r_row = sb("r_row", [P, T])
        gain_rows = sb("gain_rows", [9 * KD, P])
        gain = sb("gain", [P, 9 * KD])
        a_n = sb("a_n", [P, 2, T])
        b_n = sb("b_n", [P, 2, T])
        silu = sb("silu", [P, 2, T])
        prod = sb("prod", [P, 2, T])
        g_hi = sb("g_hi", [P, 2, 2, T], F32R)
        g_lo = sb("g_lo", [P, 2, 2, T], F32R)
        rows_in = sb("rows_in", [P, TB, D], at=spot["g_hi"])
        p_rows = sb("p_rows", [P, TB, T])
        s5_rows = sb("s5_rows", [NQ, 4, P])
        skip = sb("skip", [2 * H, NQ, 2 * H], at=spot["p_rows"])
        p_hi = sb("p_hi", [P, 2, T], F32R)
        p_lo = sb("p_lo", [P, 2, T], F32R)
        minus_tri = sb("minus_tri", [P, P])
        minus_ones = sb("minus_ones", [P, P])
        ident_b = sb("ident_b", [P, P], BF16)
        masked_b = sb("masked_b", [P, P], BF16)
        ident = sb("ident", [P, P])
        ones = sb("ones", [P, P])
        half_pi = sb("half_pi", [P, 1])
        zeros_b = sb("zeros_b", [P, P], BF16)

        half_1 = spot["op_hi"] + KD * T * 4, spot["op_lo"] + KD * T * 4
        mixer = top[0]
        w_in_state = sb("w_in_state", [P, 2, NQ, TAU, 2, H])
        w_state_out = sb("w_state_out", [P, 2, NQ, TAU + 1, 2, H])
        z_ops = sb("z_ops", [P, 2, NB, 4, T], F32R, at=spot["w_in_state"])
        turn_cos = sb("turn_cos", [P, NQ, NC])
        turn_sin = sb("turn_sin", [P, NQ, NC])
        decay = sb("decay", [P, NQ, NC])
        within = [sb(f"within{i}", [P, NQ // 2, P], at=half_1[i]) for i in range(2)]
        x_scaled = sb("x_scaled", [P, KD, T], at=half_1[0])
        u_steps = sb("u_steps", [P, NQ, NC], at=spot["g_hi"])
        b_in = sb("b_in", [P, 2, NQ, H], at=half_1[0])
        c_in = sb("c_in", [P, 2, NQ, H], at=half_1[0] + 2 * NQ * H * 4)
        c_rows = sb("c_rows", [P, KD, 2, S], at=half_1[1])
        tmp = sb("tmp", [P, 2, NQ * 32], at=spot["decay"])
        small = sb("small", [P, 32, NQ], at=spot["p_hi"])
        scratch = sb("scratch", [P, 2, 512], at=spot["p_hi"])
        dt_rows = sb("dt_rows", [NQ, 2])

        kT = sb("kT", [P, KD, T], at=mixer)
        qT = sb("qT", [P, KD, T], at=mixer + 4 * KD * T)
        val = sb("val", [P, TB, D], at=mixer + 8 * KD * T)
        HW = T + P
        z_abs, z_exp, z_log, drop, att = (sb(name, [P, DEPTH, HW], at=mixer + 12 * KD * T + 4 * DEPTH * HW * i)
                                           for i, name in enumerate(("z_abs", "z_exp", "z_log", "drop", "att")))
        assert top[0] <= nc.sbuf_usable_end

        acc = [ctx.enter_context(nc.psum_tensor(f"acc{b}", [P, 2, T], F32)) for b in range(NB)]
        bank = [ctx.enter_context(nc.psum_tensor(f"bank{b}", [P, 2, T], F32)) for b in range(2)]
        stat = ctx.enter_context(nc.psum_tensor("stat", [P, 512], F32))
        misc = ctx.enter_context(nc.psum_tensor("misc", [P, 512], F32))

        raw_landed = [sem(f"raw_landed{s}") for s in range(RING)]
        hi_done, lo_done, pe_done = sem("hi_done"), sem("lo_done"), sem("pe_done")
        rows_landed = sem("rows_landed")
        gains_landed = sem("gains_landed")
        consts_ready = sem("consts_ready")
        ident_zeroed = sem("ident_zeroed")
        x_turned = sem("x_turned")
        p_landed = sem("p_landed")
        p_turned = sem("p_turned")
        p_hi_done, p_lo_done = sem("p_hi_done"), sem("p_lo_done")
        gate_taken, gate_ready, gated = sem("gate_taken"), sem("gate_ready"), sem("gated")
        masks_made = sem("masks_made")
        s5_landed, rows_spread = sem("s5_landed"), sem("rows_spread")
        s5_turned, small_ready = sem("s5_turned"), sem("small_ready")
        c_landed, b_landed = sem("c_landed"), sem("b_landed")
        c_turned, c_ready = sem("c_turned"), sem("c_ready")
        angles_ready, phasors_ready = sem("angles_ready"), sem("phasors_ready")
        pool_step = sem("pool_step")
        weights_ready = sem("weights_ready")
        turns_ready = sem("turns_ready")
        block_done, block_skip = sem("block_done"), sem("block_skip")
        block_first, block_taken = sem("block_first"), sem("block_taken")
        turned_done, turned_taken = sem("turned_done"), sem("turned_taken")
        u_scaled, u_placed = sem("u_scaled"), sem("u_placed")
        s_in_done, y_done = sem("s_in_done"), sem("y_done")
        dve_step = sem("dve_step")
        scanned, state_re, state_im = sem("scanned"), sem("state_re"), sem("state_im")
        imag_step = sem("imag_step")
        x_back = sem("x_back")
        gelu_done = sem("gelu_done")
        bank_taken = sem("bank_taken")
        z_done, abs_done, exp_done, log_done = sem("z_done"), sem("abs_done"), sem("exp_done"), sem("log_done")
        drop_done, drop_masked = sem("drop_done"), sem("drop_masked")
        exponent_done, att_done, o_done = sem("exponent_done"), sem("att_done"), sem("o_done")
        gain_turned = sem("gain_turned")
        gain_ready = sem("gain_ready")
        acc_done = sem("acc_done")
        x_new = sem("x_new")
        op_hi_done, op_lo_done = sem("op_hi_done"), sem("op_lo_done")
        squared = sem("squared")
        squares_used = sem("squares_used")
        sum_ready = sem("sum_ready")
        sum_col = sem("sum_col")
        mean_ready = sem("mean_ready")
        r_ready = sem("r_ready")
        diag_ready = sem("diag_ready")
        r_spread = sem("r_spread")
        r_row_ready = sem("r_row_ready")
        a_taken, b_taken = sem("a_taken"), sem("b_taken")
        silu_done, prod_done = sem("silu_done"), sem("prod_done")
        g_hi_done, g_lo_done = sem("g_hi_done"), sem("g_lo_done")
        out_turned = sem("out_turned")
        out_rows = [sem("out_rows0"), sem("out_rows1")]
        stored = sem("stored")
        scaled = sem("scaled")

        def gain_col(st, k):
            i = (8 if st.kind == "final" else 2 * norm_of[st.kind] + st.layer) * KD + k
            return gain[:, i:i + 1]

        def a_chunk(w, half, col):
            return w[half * 512:(half + 1) * 512, col].rearrange("(k p) c -> p k c", p=P)

        def slot_a(buf, n):
            return buf[:, n % RING, :].rearrange("p (k c) -> p k c", k=4)

        GATE, OUT = 0, 1
        GLU = [(w, j, half) for half in range(2) for j in range(NB) for w in (GATE, OUT) if (w, j) != (OUT, NB - 1)] + \
              [(OUT, NB - 1, half) for half in range(2)]
        glu_bank = [[bank[0], bank[1], acc[2], stat], [acc[0], acc[1], acc[3], misc]]
        BETWEEN = {(3, 2): [("in", 0, 0)], (3, 3): [("in", 0, 1)],
                   (4, 1): [("step", 0)], (4, 3): [("in", 1, 0)],
                   (5, 1): [("in", 1, 1)], (5, 3): [("out", 0, 0)],
                   (6, 1): [("out", 0, 1)], (6, 3): [("step", 1)],
                   (7, 1): [("out", 1, 0)], (7, 3): [("out", 1, 1), ("in", 2, 0), ("in", 2, 1), ("step", 2)],
                   (8, 1): [("in", 3, 0)], (8, 3): [("in", 3, 1)],
                   (9, 3): [("out", 2, 0)],
                   (10, 1): [("out", 2, 1)],
                   (11, 1): [("step", 3)], (11, 3): [("out", 3, 0)],
                   (12, 1): [("out", 3, 1)]}
        DVE_WORK = {1: [("mean",)], 2: [("row",), ("place", 0)], 3: [("place", 1), ("back", 0), ("scan", 0)],
                    5: [("back", 1), ("place", 2), ("scan", 1)], 6: [("low", 0)],
                    7: [("place", 3), ("low", 1), ("back", 2), ("scan", 2)], 8: [("back", 3)], 9: [("scan", 3)],
                    11: [("low", 2)], 13: [("low", 3)]}
        ACT_WORK = {2: [("place", 0)], 3: [("place", 1)], 5: [("place", 2)], 6: [("gelu", 0)],
                    7: [("place", 3), ("gelu", 1)], 10: [("gelu", 2)], 12: [("gelu", 3)]}

        def x_bank(g):
            return [acc[1].rearrange("p a t -> p (a t)"), acc[2].rearrange("p a t -> p (a t)")] if g == NB - 1 else \
                [acc[3].rearrange("p a t -> p (a t)"), misc[:, :]]

        y_bank = [stat, acc[0].rearrange("p a t -> p (a t)"), stat, misc]
        def c_half(b, i, e):
            t = acc[b].rearrange("p a t -> p (a t)").rearrange("p (q e h) -> p q e h", e=2, h=H)
            return c_in[S * e:S * e + S, i, 16 * b:16 * b + 16, :], t[S * i:S * i + S, :, e, :]

        z_set = [o.u + 1 for o in stages if o.kind == "s5"]

        def peeled(nxt):
            return 3 if nxt.kind == "s5" else 1

        def block_at(c):
            i = c - (CHUNKS["ffn1"] - 4 - NQ // 2 + 1)
            return (i // 2, i % 2) if 0 <= i < NQ // 2 else (None, None)

        def operand(u, k):
            if u in z_set:
                return [z_ops[:, i, k // 2, k % 2, :] for i in range(2)]
            return op_hi[:, HALF[u], k, :], op_lo[:, HALF[u], k, :]

        OUT_ORDER = [(0, 0), (1, 0), (2, 0), (0, 1), (1, 1), (2, 1), (3, 0), (3, 1)]
        out_bank = [bank[0], bank[1], stat.rearrange("p (k t) -> p k t", k=2), misc.rearrange("p (k t) -> p k t", k=2)]
        ple_bank = [bank[0], bank[1], misc.rearrange("p (k t) -> p k t", k=2), bank[1]]
        z_bank = [acc[0].rearrange("p a t -> p (a t)"), acc[1].rearrange("p a t -> p (a t)"), misc]

        def step_chunk(st, s):
            return st.n0 + 12 + s if s < 18 else None

        block = ctx.enter_context(nc.Block())

        @block.sync
        def _(sp):
            def load(n, slot, src, shape_k):
                if not isinstance(n, int) or n >= RING:
                    sp.wait_ge(lo_done, n - (RING - 1))
                dst = raw[:, slot, :]
                if shape_k:
                    dst = dst.rearrange("p (k c) -> p k c", k=4)
                sp.dma_start(dst, src).then_inc(raw_landed[slot], 16)

            def load_s5_parameters():
                sp.dma_start(s5_rows[:, 0, :], s5_a_re[0].rearrange("(q e) p -> q (e p)", e=2)).then_inc(s5_landed, 16)
                sp.dma_start(s5_rows[:, 1, :], s5_a_im[0].rearrange("(q e) p -> q (e p)", e=2)).then_inc(s5_landed, 16)
                sp.dma_start(dt_rows[:, :], s5_log_dt[0].rearrange("(q e) -> q e", e=2)).then_inc(s5_landed, 16)
                sp.dma_start(s5_rows[:, 3, 0:2 * H], s5_d[0].rearrange("(q c) -> q c", q=NQ)).then_inc(s5_landed, 16)
                for i, c in enumerate((s5_c_re, s5_c_im)):
                    sp.dma_start(c_rows[:, :, i], c[0].rearrange("(k g) h p -> (g h) k p", k=KD)).then_inc(c_landed, 16)
                for i, b in enumerate((s5_b_re, s5_b_im)):
                    sp.dma_start(b_in[:, i], b[0].rearrange("(q e) p h -> (e p) q h", e=2)).then_inc(b_landed, 16)

            def load_ffn(st):
                w1, w3, w2 = (w[st.layer] for w in ffn_weights[st.kind])

                def pair(w, n, s, g):
                    for half in range(2):
                        load(n + half, (s + half) % RING, a_chunk(w, half, bass.ds(g * 256, 256)), True)

                def down(n, s, g):
                    for j in range(2):
                        load(n + j, (s + j) % RING, w2[bass.ds(g * 256 + j * P, P), :], False)
                pair(w1, st.n0, st.n0, 0)
                load(st.n0 + 2, (st.n0 + 2) % RING, a_chunk(w3, 0, slice(0, 256)), True)
                if st.v == 0:
                    load_s5_parameters()
                load(st.n0 + 3, (st.n0 + 3) % RING, a_chunk(w3, 1, slice(0, 256)), True)
                with sp.Fori(1, NG) as g:
                    n, s = g * 6 + (st.n0 - 2), st.n0 + 4
                    pair(w1, n, s, g)
                    pair(w3, n + 2, s + 2, g)
                    down(n + 4, s + 4, g - 1)
                down(st.n0 + 6 * NG - 2, st.n0 + 6 * NG - 2, NG - 1)

            def load_group(n, w, col):
                for half in range(2):
                    load(n + half, (n + half) % RING, a_chunk(w, half, slice(col, col + 256)), True)

            def load_ple(st):
                for kt in range(2):
                    load(st.n0 + kt, (st.n0 + kt) % RING, ple_proj[st.layer, kt * P:(kt + 1) * P, :], False)
                for j in range(NB):
                    load_group(st.n0 + 2 + 2 * j, ple_gate[st.layer], 256 * j)

            def load_s5(st):
                for j in range(NB):
                    load_group(st.n0 + 2 * j, s5_w_in[0], 256 * j)
                for i, (which, j, half) in enumerate(GLU):
                    n, col = st.n0 + 8 + i, (D if which == GATE else 0) + 256 * j
                    load(n, n % RING, a_chunk(s5_w_glu[0], half, slice(col, col + 256)), True)

            def load_attn(st):
                w = sb_w_qkv[0]
                for j in range(NB):
                    load_group(st.n0 + 2 * j, w, 2 * D + 256 * j)
                for j in range(NB):
                    load_group(st.n0 + 8 + 4 * j, w, D + 256 * j)
                    load_group(st.n0 + 10 + 4 * j, w, 256 * j)
                for i, (j, half) in enumerate(OUT_ORDER):
                    n = st.n0 + 24 + i
                    load(n, n % RING, a_chunk(sb_w_o[0], half, slice(256 * j, 256 * j + 256)), True)

            for tb in range(TB):
                sp.dma_start(rows_in[:, tb, :], x[0, tb * P:(tb + 1) * P, :]).then_inc(rows_landed, 16)
            for st, nxt in zip(stages, stages[1:] + [None]):
                if nxt is not None and nxt.kind == "ple":
                    if any(o.kind == "s5" for o in stages):
                        sp.wait_ge(block_skip, 8)
                    if nxt.q:
                        sp.wait_ge(p_turned, nxt.q)
                    sp.dma_start(p_rows[:, :, :],
                                 p[nxt.layer, 0].rearrange("(b p) c -> p b c", p=P)).then_inc(p_landed, 16)
                if st.kind[:3] == "ffn":
                    load_ffn(st)
                if st.kind == "s5":
                    load_s5(st)
                if st.kind == "ple":
                    load_ple(st)
                if st.kind == "attn":
                    load_attn(st)
                if st.kind == "final":
                    for tb in range(TB):
                        for half in range(2):
                            cols = slice(half * D // 2, (half + 1) * D // 2)
                            sp.wait_ge(out_rows[half], 2 * (tb + 1))
                            sp.dma_start(out[0, tb * P:(tb + 1) * P, cols], rows_in[:, tb, cols]).then_inc(stored, 16)
                    sp.wait_ge(stored, 16 * 2 * TB)

        @block.gpsimd
        def _(pool):
            pool.memset(ident[:, :], 0.0).then_inc(ident_zeroed, 1)
            pool.memset(ones[:, :], 1.0).then_inc(consts_ready, 1)
            pool.memset(minus_half[:, :], -0.5).then_inc(consts_ready, 1)
            pool.memset(zeros_b[:, :], 0.0).then_inc(consts_ready, 1)
            pool.memset(half_pi[:, :], 1.5707963267948966).then_inc(consts_ready, 1)
            pool.wait_ge(ident_zeroed, 1)
            pool.affine_select(out=ident[:, :], in_=ident[:, :], compare_op=ALU.not_equal, fill=1.0, base=0,
                               pattern=[[-1, P]], channel_multiplier=1).then_inc(consts_ready, 1)

            def norm(v):
                last = 3 if stages[v].kind == "final" else 4
                sq = squares_used
                pool.wait_ge(squared, 4 * v + 2)
                if v:
                    pool.wait_ge(sum_col, v)
                pool.tensor_tensor(square_sum[:, :, :], squares[:, 0], squares[:, 1], ALU.add).then_inc(sq, 2)
                for b in range(2, last):
                    pool.wait_ge(sq, 4 * v + b)
                    pool.wait_ge(squared, 4 * v + b + 1)
                    pool.tensor_tensor(square_sum[:, :, :], square_sum[:, :, :], squares[:, b % 2], ALU.add)\
                        .then_inc(sq, 1)
                pool.wait_ge(sq, 4 * v + last)
                pool.tensor_tensor(square_sum[:, 0], square_sum[:, 0], square_sum[:, 1], ALU.add).then_inc(sum_ready, 1)
                pool.wait_ge(mean_ready, v + 1)
                pool.tensor_tensor(r_col[:, :], mean_sq[:, :], minus_half[:, :], ALU.pow).then_inc(r_ready, 1)
            pool.wait_ge(consts_ready, 5)
            pool.memset(minus_tri[:, :], -1.0).then_inc(masks_made, 1)
            pool.memset(minus_ones[:, :], -1.0).then_inc(masks_made, 1)
            pool.memset(ident_b[:, :], 0.0).then_inc(masks_made, 1)
            pool.memset(masked_b[:, :], 0.0).then_inc(masks_made, 1)
            pool.wait_ge(masks_made, 4)
            pool.affine_select(out=minus_tri[:, :], in_=minus_tri[:, :], compare_op=ALU.is_ge, fill=0.0, base=0,
                               pattern=[[-1, P]], channel_multiplier=1).then_inc(masks_made, 1)
            pool.affine_select(out=ident_b[:, :], in_=ident_b[:, :], compare_op=ALU.not_equal, fill=1.0, base=0,
                               pattern=[[-1, P]], channel_multiplier=1).then_inc(masks_made, 1)
            pool.affine_select(out=masked_b[:, :], in_=masked_b[:, :], compare_op=ALU.is_gt, fill=MASKED, base=0,
                               pattern=[[1, P]], channel_multiplier=-1).then_inc(masks_made, 1)

            def attention():
                for h in range(NH):
                    pool.wait_ge(drop_done, h + 1)
                    for c in (0, T):
                        d = drop[:, h % DEPTH, c:c + P]
                        pool.affine_select(out=d, in_=d, compare_op=ALU.is_gt, fill=0.0, base=0,
                                           pattern=[[1, P]], channel_multiplier=-1).then_inc(drop_masked, 1)

            links = [0]

            def link(ins):
                links[0] += 1
                ins.then_inc(pool_step, 1)
                pool.wait_ge(pool_step, links[0])

            def tt(o, a, b, op=ALU.mult):
                link(pool.tensor_tensor(o, a, b, op))

            def ts(o, a, m, b):
                link(pool.tensor_scalar(o, a, m, b, ALU.mult, ALU.add))

            def sm(i):
                return small[:, i, :]

            def s5_parameters():
                lam_re, lam_im, dt, skip_col, decay_log, angle, mag, cos, sin, fr, fi, t0, t1, t2 = range(14)
                A, F, E, M4 = 14, 22, 30, mag
                link(pool.memset(w_state_out[:, :, :, :, :, :], 0.0))
                pool.wait_ge(small_ready, 3)
                pool.wait_ge(angles_ready, 2)
                tt(skip[:, :, :], ident[0:32, 0:32].unsqueeze(1).broadcast_to([32, NQ, 32]),
                   sm(skip_col)[0:32].unsqueeze(2).broadcast_to([32, NQ, 32]))
                pool.wait_ge(phasors_ready, 3)
                pool.wait_ge(b_landed, 16 * 2)
                pool.wait_ge(c_ready, 2)

                def product(o_re, o_im, a_re, a_im, b_re, b_im, x, y):
                    tt(x, a_re, b_re)
                    tt(y, a_im, b_im)
                    tt(o_re, x, y, ALU.subtract)
                    tt(x, a_re, b_im)
                    tt(y, a_im, b_re)
                    tt(o_im, x, y, ALU.add)

                a_re = [None] + [sm(A + j) for j in range(4)]
                a_im = [None] + [sm(A + 4 + j) for j in range(4)]
                tt(a_re[1], sm(mag), sm(cos))
                tt(a_im[1], sm(mag), sm(sin))
                link(pool.tensor_scalar(sm(decay_log), a_re[1], -1.0, None, ALU.add))
                tt(sm(t0), sm(decay_log), sm(lam_re))
                tt(sm(t1), a_im[1], sm(lam_im))
                tt(sm(fr), sm(t0), sm(t1), ALU.add)
                tt(sm(t0), a_im[1], sm(lam_re))
                tt(sm(t1), sm(decay_log), sm(lam_im))
                tt(sm(fi), sm(t0), sm(t1), ALU.subtract)
                tt(sm(F + 3), sm(fr), sm(t2))
                tt(sm(F + 7), sm(fi), sm(t2))
                for j in (2, 3, 4):
                    product(a_re[j], a_im[j], a_re[j - 1], a_im[j - 1], a_re[1], a_im[1], sm(t0), sm(t1))
                for tau in range(TAU - 1):
                    j = TAU - 1 - tau
                    product(sm(F + tau), sm(F + 4 + tau), a_re[j], a_im[j], sm(F + 3), sm(F + 7), sm(t0), sm(t1))
                for _ in range(2):
                    tt(sm(mag), sm(mag), sm(mag))

                def over(x, n):
                    return x.unsqueeze(2).broadcast_to([P, NQ, n])
                xy = [tmp[:, i, 0:NQ * H].rearrange("p (q h) -> p q h", h=H) for i in range(2)]

                def both(o, part, j, op):
                    for e in range(2):
                        r = slice(64 * e, 64 * e + 64)
                        tt(o[r, part, :, j, e, :], xy[0][r], xy[1][r], op)
                for tau in range(TAU):
                    f_re, f_im = over(sm(F + tau), H), over(sm(F + 4 + tau), H)
                    tt(xy[0], f_re, b_in[:, 0])
                    tt(xy[1], f_im, b_in[:, 1])
                    both(w_in_state, 0, tau, ALU.subtract)
                    tt(xy[0], f_re, b_in[:, 1])
                    tt(xy[1], f_im, b_in[:, 0])
                    both(w_in_state, 1, tau, ALU.add)
                for e in range(2):
                    r = slice(64 * e, 64 * e + 64)
                    for part in range(2):
                        link(pool.tensor_copy(w_state_out[r, part, :, 0, e, :], c_in[r, part]))
                for j in range(1, TAU + 1):
                    p_re, p_im = over(a_re[j], H), over(a_im[j], H)
                    tt(xy[0], c_in[:, 0], p_re)
                    tt(xy[1], c_in[:, 1], p_im)
                    both(w_state_out, 0, j, ALU.add)
                    tt(xy[0], c_in[:, 1], p_re)
                    tt(xy[1], c_in[:, 0], p_im)
                    both(w_state_out, 1, j, ALU.subtract)
                link(pool.memset(within[0][:, :, :], 0.0))
                pool.memset(within[1][:, :, :], 0.0).then_inc(weights_ready, 1)
                e_re, e_im = sm(E), sm(E + 1)
                product(e_re, e_im, sm(cos), sm(sin), sm(cos), sm(sin), sm(t0), sm(t1))
                product(sm(fr), sm(fi), e_re, e_im, e_re, e_im, sm(t0), sm(t1))
                link(pool.memset(turn_cos[:, :, 0:1], 1.0))
                link(pool.memset(turn_sin[:, :, 0:1], 0.0))
                n, cur, new = 1, (sm(fr), sm(fi)), (e_re, e_im)
                while n < NC:
                    xn = [tmp[:, i, 0:NQ * n].rearrange("p (q c) -> p q c", c=n) for i in range(2)]
                    product(turn_cos[:, :, n:2 * n], turn_sin[:, :, n:2 * n], turn_cos[:, :, 0:n], turn_sin[:, :, 0:n],
                            over(cur[0], n), over(cur[1], n), *xn)
                    product(*new, *cur, *cur, sm(t0), sm(t1))
                    cur, new, n = new, cur, 2 * n
                ts(decay[:, :, :], over(sm(mag), NC), 1.0, 0.0)
                pool.memset(decay[:, :, 0:1], 0.0).then_inc(turns_ready, 1)

            def s5_mix():
                for g in range(NQ // QG):
                    cos, sin = (t[:, QG * g:QG * g + QG, :].rearrange("p q c -> p (q c)") for t in (turn_cos, turn_sin))
                    pool.wait_ge(scanned, 2 * g + 2)
                    pool.tensor_tensor(scratch[:, 0, :], b_n.rearrange("p a t -> p (a t)"), sin, ALU.mult)\
                        .then_inc(imag_step, 1)
                    s_im = squares[:, 1].rearrange("p a t -> p (a t)")
                    if g:
                        pool.wait_ge(y_done, g)
                    pool.tensor_tensor(s_im, prod.rearrange("p a t -> p (a t)"), cos, ALU.mult).then_inc(imag_step, 1)
                    pool.wait_ge(imag_step, 2 * g + 2)
                    pool.tensor_tensor(s_im, s_im, scratch[:, 0, :], ALU.add).then_inc(state_im, 1)

            link(pool.memset(w_in_state[:, :, :, :, :, :], 0.0))
            for st in stages:
                norm(st.v)
                if st.v == 0 and any(o.kind == "s5" for o in stages):
                    s5_parameters()
                if st.kind == "s5":
                    s5_mix()
                if st.kind == "attn":
                    attention()

        @block.scalar
        def _(act):
            for i, src in enumerate(norms):
                act.dma_start(gain_rows[2 * i * KD:2 * (i + 1) * KD, :], src.rearrange("l (k p) -> (l k) p", p=P))\
                    .then_inc(gains_landed, 16)
            act.dma_start(gain_rows[8 * KD:9 * KD, :], final_norm.rearrange("(k p) -> k p", p=P))\
                .then_inc(gains_landed, 16)

            def split_hi(n, slot, uses):
                act.wait_ge(raw_landed[slot], uses * 16)
                if not isinstance(n, int) or n >= RING:
                    act.wait_ge(pe_done, n - (RING - 1))
                act.activation(w_hi[:, slot, :], raw[:, slot, :], ACT.Copy).then_inc(hi_done, 1)

            def split(n):
                if n < n_chunks:
                    split_hi(n, n % RING, n // RING + 1)

            def prep(v, u, banks=range(NB)):
                for b in banks:
                    act.wait_ge(x_new, 4 * v + b + 1)
                    if u is not None:
                        for k in (2 * b, 2 * b + 1):
                            act.activation(op_hi[:, HALF[u], k, :], xT[:, k, :], ACT.Copy,
                                           scale=gain_col(stages[v], k)).then_inc(op_hi_done, 1)
                    if b >= 2 or v > 0:
                        act.wait_ge(squares_used, 4 * v + 2 * (b >= 2))
                    act.activation(squares[:, b % 2], xT[:, 2 * b:2 * b + 2, :], ACT.Square).then_inc(squared, 1)

            def ffn(st, nxt):
                n0, base = st.n0, NG * st.f

                def do_silu(g):
                    act.wait_ge(a_taken, base + g + 1)
                    if st.f or not isinstance(g, int) or g:
                        act.wait_ge(prod_done, base + g)
                    act.activation(silu[:, :, :], a_n[:, :, :], ACT.Silu).then_inc(silu_done, 1)

                def do_g_hi(g, half):
                    act.wait_ge(prod_done, base + g + 1)
                    act.activation(g_hi[:, half], prod[:, :, :], ACT.Copy).then_inc(g_hi_done, 1)
                if st.v == 0:
                    split(n0 + 2)
                if nxt.kind == "s5":
                    s5_take()
                split(n0 + 3)
                if nxt.kind == "s5":
                    c_take()
                split(n0 + 4)
                split(n0 + 5)
                if nxt.kind == "s5":
                    s5_phasors()
                do_silu(0)
                if nxt.kind == "ple":
                    p_high(nxt.q)

                def part(n, j, g):
                    m = n0 + j - 2
                    split_hi(n + j, m % RING, g * 2 + (m // RING + 1))
                    if nxt.kind == "s5" and isinstance(n, int):
                        s5_blocks(n + j - 3 - n0)

                def group(g):
                    n = g * 6 + (n0 - 2)
                    part(n, 2, g)
                    do_g_hi(g - 1, 0)
                    part(n, 3, g)
                    part(n, 4, g)
                    part(n, 5, g)
                    do_silu(g)
                    part(n, 6, g)
                    if not isinstance(g, int) or g < NG - 1:
                        part(n, 7, g)
                with act.Fori(1, NG - peeled(nxt)) as g:
                    group(g)
                for g in range(NG - peeled(nxt), NG):
                    group(g)
                n = n0 + 6 * (NG - 1) - 2
                do_g_hi(NG - 1, 1)
                part(n, 7, NG - 1)
                split(n + 8)
                prep(nxt.v, nxt.u if nxt.kind != "final" else None, [0, 1])
                split(n + 9)
                prep(nxt.v, nxt.u if nxt.kind != "final" else None, [2, 3])

            def p_high(q):
                act.wait_ge(p_turned, q + 1)
                act.activation(p_hi[:, :, :], misc[:, :].rearrange("p (k t) -> p k t", k=2), ACT.Copy)\
                    .then_inc(p_hi_done, 1)

            def ple(st, nxt):
                split(st.n0 + 2)
                split(st.n0 + 3)
                split(st.n0 + 4)
                split(st.n0 + 5)
                for j in range(NB):
                    act.wait_ge(gate_taken, 4 * st.q + j + 1)
                    if st.e or j:
                        act.wait_ge(gated, st.e + j)
                    act.activation(silu[:, :, :], a_n[:, :, :], ACT.Sigmoid).then_inc(gate_ready, 1)
                    if j < NB - 1:
                        split(st.n0 + 6 + 2 * j)
                        split(st.n0 + 7 + 2 * j)
                    else:
                        split(st.n0 + 12)
                    prep(nxt.v, nxt.u if nxt.kind != "final" else None, [j])

            def s5_in():
                act.wait_ge(s5_landed, 16 * 4)
                act.activation(s5_rows[:, 2, :].rearrange("q (e p) -> q e p", e=2),
                               dt_rows[:, :].unsqueeze(2).broadcast_to([NQ, 2, S]), ACT.Copy).then_inc(rows_spread, 1)

            def s5_take():
                act.wait_ge(s5_turned, 1)
                act.activation(small[:, 2, :], misc[:, P + NQ * 2:P + NQ * 3], ACT.Exp).then_inc(small_ready, 1)
                act.activation(small[:, 0:2, :].rearrange("p i q -> p (i q)"), misc[:, P:P + 2 * NQ], ACT.Copy)\
                    .then_inc(small_ready, 1)
                act.activation(small[0:2 * H, 3, :], misc[0:2 * H, P + NQ * 3:P + NQ * 4], ACT.Copy)\
                    .then_inc(small_ready, 1)

            def c_take():
                act.wait_ge(c_turned, 2)
                for i in range(2):
                    for e in range(2):
                        dst, src = c_half(1, i, e)
                        ins = act.activation(dst, src, ACT.Copy, scale=1.0 - 2 * i)
                ins.then_inc(c_ready, 1)

            def s5_phasors():
                act.wait_ge(angles_ready, 1)
                act.activation(small[:, 6, :], small[:, 4, :], ACT.Exp).then_inc(phasors_ready, 1)
                act.activation(small[:, 8, :], small[:, 5, :], ACT.Sin).then_inc(phasors_ready, 1)
                act.activation(small[:, 7, :], small[:, 5, :], ACT.Abs).then_inc(rows_spread, 1)
                act.wait_ge(rows_spread, 2)
                act.activation(small[:, 7, :], small[:, 7, :], ACT.Sin, scale=-1.0, bias=half_pi[:, 0:1])\
                    .then_inc(phasors_ready, 1)

            def s5_blocks(c):
                i, second = block_at(c)
                if i is None or second:
                    return
                act.wait_ge(block_first, i + 1)
                o = within[i // 4][:, 4 * (i % 4):4 * (i % 4) + 4, :]
                for quad in (2, 3):
                    r = slice(32 * quad, 32 * quad + 32)
                    act.activation(o[r, :, 32 * quad:P], o[0:32, :, 0:P - 32 * quad], ACT.Copy).then_inc(block_taken, 1)
                act.wait_ge(turned_done, 2 * i + 1)
                act.activation(w_in_state[:, 0, 4 * i:4 * i + 4].rearrange("p q t e h -> p (q t e h)"), stat[:, :],
                               ACT.Copy).then_inc(turned_taken, 1)

            def s5(st, nxt):
                n0, zu = st.n0, st.u + 1
                scaled_u = scratch[:, 1, :].rearrange("p (k c t) -> p k c t", k=2, t=TAU)

                def place(j):
                    act.wait_ge(u_scaled, j + 1)
                    for quad in (2, 3):
                        for tau in range(TAU):
                            src = scaled_u[32 * quad:32 * quad + 32, :, :, tau]
                            dst = u_steps[32 * tau:32 * tau + 32, 8 * j:8 * j + 8, :]
                            dst = dst.rearrange("p (k j) c -> p k j c", k=2)[:, :, quad, :]
                            act.activation(dst, src, ACT.Copy).then_inc(u_placed, 1)
                zf = square_sum

                def gelu(g):
                    act.wait_ge(y_done, g + 1)
                    if g:
                        act.wait_ge(op_lo_done, KD * zu + 2 * g)
                    y = y_bank[g].rearrange("p (k j c) -> p k j c", k=2, c=NC)
                    for quad in range(4):
                        for tau in range(TAU):
                            dst = zf[32 * quad:32 * quad + 32].rearrange("p k (c t) -> p k c t", t=TAU)[:, :, :, tau]
                            act.activation(dst, y[32 * tau:32 * tau + 32, :, quad, :], ACT.Gelu_apprx_tanh)\
                                .then_inc(gelu_done, 1)
                    act.wait_ge(gelu_done, 16 * g + 16)
                    act.activation(z_ops[:, 0, g, 0:2, :], zf[:, :, :], ACT.Copy).then_inc(op_hi_done, 2)
                for i in range(24):
                    split(n0 + i + 2)
                    if i > 8 and GLU[i - 9][0] == OUT and GLU[i - 9][2]:
                        prep(nxt.v, nxt.u, [GLU[i - 9][1]])
                    for kind, g in ACT_WORK.get(i, []):
                        {"place": place, "gelu": gelu}[kind](g)
                    if i >= 8:
                        which, j, half = GLU[i - 8]
                        if half and which == GATE:
                            act.wait_ge(pe_done, n0 + i + 1)
                            if st.e or j:
                                act.wait_ge(gated, st.e + j)
                            gate = glu_bank[GATE][j]
                            if j == NB - 1:
                                gate = gate.rearrange("p (k t) -> p k t", k=2)
                            act.activation(silu[:, :, :], gate[:, :, :], ACT.Sigmoid).then_inc(gate_ready, 1)
                split(n0 + 26)
                prep(nxt.v, nxt.u, [NB - 1])

            def attention(st, nxt):
                n0, o_set = st.n0, st.u + 1
                split(n0 + 2)
                split(n0 + 3)
                for j in range(NB):
                    split(n0 + 4 + 2 * j)
                    act.wait_ge(r_ready, st.v + 1)
                    act.wait_ge(pe_done, n0 + 2 * j + 2)
                    for tb in range(TB):
                        act.activation(val[:, tb, 256 * j:256 * j + 256], bank[j % 2][:, tb, :], ACT.Copy,
                                       scale=r_col[:, tb:tb + 1]).then_inc(bank_taken, 1)
                    split(n0 + 5 + 2 * j)
                act.preload_act_table_set("natural_log_exp_and_others")
                for n in (n0 + 12, n0 + 13):
                    split(n)
                for s in range(STEPS):
                    h = s
                    if h < NH:
                        act.wait_ge(z_done, h + 1)
                        act.activation(z_abs[:, h % DEPTH], z_bank[h % DEPTH][:, 0:HW], ACT.Abs).then_inc(abs_done, 1)
                        act.wait_ge(abs_done, h + 1)
                        act.activation(z_exp[:, h % DEPTH], z_abs[:, h % DEPTH], ACT.Exp, scale=-1.0)\
                            .then_inc(exp_done, 1)
                        act.wait_ge(exp_done, h + 1)
                        if h >= DEPTH:
                            act.wait_ge(drop_done, h - DEPTH + 1)
                        act.activation(z_log[:, h % DEPTH], z_exp[:, h % DEPTH], ACT.Ln, bias=1.0).then_inc(log_done, 1)
                    h = s - 2
                    if 0 <= h < NH:
                        act.wait_ge(exponent_done, h + 1)
                        if h >= DEPTH:
                            act.wait_ge(o_done, h - DEPTH + 1)
                        act.activation(att[:, h % DEPTH], z_bank[h % DEPTH][:, 0:HW], ACT.Exp).then_inc(att_done, 1)
                    h = s - 3
                    if 0 <= h and h % 2:
                        act.wait_ge(o_done, h + 1)
                        act.activation(op_hi[:, HALF[o_set], h // 2, :], acc[2 + h // 2 % 2][:, 0, :], ACT.Copy)\
                            .then_inc(op_hi_done, 1)
                    if s < 16:
                        split(step_chunk(st, s) + 2)
                split(n0 + 30)
                prep(nxt.v, nxt.u, [0])
                split(n0 + 31)
                prep(nxt.v, nxt.u, [1])
                split(n0 + 32)
                prep(nxt.v, nxt.u, [2])
                split(n0 + 33)
                split(n0 + 34)
                prep(nxt.v, nxt.u, [3])

            act.preload_act_table_set("exp_and_others")
            split(0)
            act.wait_ge(gain_turned, 1)
            act.activation(gain[:, :], misc[:, 0:9 * KD], ACT.Copy).then_inc(gain_ready, 1)
            act.wait_ge(gain_ready, 1)
            prep(0, 0, [0, 1])
            split(1)
            prep(0, 0, [2, 3])
            if any(o.kind == "s5" for o in stages):
                s5_in()
            for st, nxt in zip(stages, stages[1:] + [None]):
                if st.kind[:3] == "ffn":
                    ffn(st, nxt)
                if st.kind == "s5":
                    s5(st, nxt)
                if st.kind == "ple":
                    ple(st, nxt)
                if st.kind == "attn":
                    attention(st, nxt)
                if st.kind == "final":
                    act.wait_ge(r_ready, st.v + 1)
                    for tb in range(TB):
                        for j in range(NB // 2, NB):
                            act.wait_ge(out_turned, j + 1)
                            act.activation(rows_in[:, tb, 256 * j:256 * j + 256], acc[j][:, tb, :], ACT.Copy,
                                           scale=r_col[:, tb:tb + 1]).then_inc(out_rows[1], 1)

        @block.vector
        def _(dve):
            def split_lo(n, slot):
                dve.wait_ge(hi_done, n + 1)
                dve.tensor_tensor(w_lo[:, slot, :], raw[:, slot, :], w_hi[:, slot, :].bitcast(F32), ALU.subtract)\
                    .then_inc(lo_done, 1)

            def split(n):
                if n < n_chunks:
                    split_lo(n, n % RING)

            def op_low(v, u, b):
                if u is None:
                    return
                for k in (2 * b, 2 * b + 1):
                    dve.wait_ge(op_hi_done, KD * u + k + 1)
                    dve.scalar_tensor_tensor(out=op_lo[:, HALF[u], k, :], in0=xT[:, k, :],
                                             scalar=gain_col(stages[v], k),
                                             in1=op_hi[:, HALF[u], k, :].bitcast(F32), op0=ALU.mult, op1=ALU.subtract)\
                        .then_inc(op_lo_done, 1)

            def stat_mean(v):
                dve.wait_ge(sum_col, v + 1)
                dve.tensor_scalar(mean_sq[:, :], stat[:, 0:TB], 1.0 / D, EPS, ALU.mult, ALU.add).then_inc(mean_ready, 1)

            def stat_diag(v):
                dve.wait_ge(r_ready, v + 1)
                for tb in range(TB):
                    dve.tensor_scalar(r_diag[:, tb, :], ident[:, :], r_col[:, tb:tb + 1], None, ALU.mult)\
                        .then_inc(diag_ready, 1)

            def stat_row(v):
                dve.wait_ge(r_spread, v + 1)
                dve.tensor_copy(r_row[:, :], stat[:, 256:256 + T]).then_inc(r_row_ready, 1)

            def residual_from_acc(v, u, f, n):
                dve.wait_ge(x_new, 4 * v)
                for b in range(NB):
                    dve.wait_ge(acc_done, NB * f + b + 1)
                    dve.scalar_tensor_tensor(out=xT[:, 2 * b:2 * b + 2, :], in0=acc[b][:, :, :], scalar=0.5,
                                             in1=xT[:, 2 * b:2 * b + 2, :], op0=ALU.mult, op1=ALU.add)\
                                                 .then_inc(x_new, 1)
                    if 0 < b < NB - 1:
                        op_low(v, u, b - 1)
                split(n)
                op_low(v, u, NB - 2)
                op_low(v, u, NB - 1)

            def c_take():
                dve.wait_ge(c_turned, 1)
                for i in range(2):
                    for e in range(2):
                        dst, src = c_half(0, i, e)
                        ins = dve.tensor_scalar(dst, src, 1.0 - 2 * i, None, ALU.mult)
                ins.then_inc(c_ready, 1)

            links = [0]

            def link(ins, wait=True):
                links[0] += 1
                ins.then_inc(dve_step, 1)
                if wait:
                    dve.wait_ge(dve_step, links[0])

            def s5_angles():
                lam_re, lam_im, dt, decay_log, angle, t0, t1, t2 = (small[:, i, :] for i in (0, 1, 2, 4, 5, 11, 12, 13))
                dve.wait_ge(small_ready, 3)
                link(dve.tensor_tensor(angle, lam_im, dt, ALU.mult), wait=False)
                link(dve.tensor_scalar(lam_re, lam_re, -1e-4, None, ALU.min))
                link(dve.tensor_scalar(t0, angle, 1.0 / (2 * 3.141592653589793), ROUND, ALU.mult, ALU.add), wait=False)
                link(dve.tensor_tensor(decay_log, lam_re, dt, ALU.mult))
                link(dve.tensor_scalar(t0, t0, -ROUND, None, ALU.add))
                for part in TURN:
                    link(dve.scalar_tensor_tensor(out=angle, in0=t0, scalar=-part, in1=angle, op0=ALU.mult, op1=ALU.add))
                dve.tensor_scalar(angle, angle, 3.1415925, -3.1415925, ALU.min, ALU.max).then_inc(angles_ready, 1)
                link(dve.tensor_tensor(t1, lam_re, lam_re, ALU.mult), wait=False)
                link(dve.tensor_tensor(t2, lam_im, lam_im, ALU.mult))
                link(dve.tensor_tensor(t1, t1, t2, ALU.add))
                dve.reciprocal(t2, t1).then_inc(angles_ready, 1)

            r_bc = r_row[:, :].unsqueeze(1).broadcast_to([P, 2, T])

            def ffn(st, nxt):
                n0, base, v = st.n0, NG * st.f, st.v

                def take_a(n, g):
                    dve.wait_ge(pe_done, n + 1)
                    if st.f or not isinstance(g, int) or g:
                        dve.wait_ge(silu_done, base + g)
                    dve.tensor_tensor(a_n[:, :, :], bank[0][:, :, :], r_bc, ALU.mult).then_inc(a_taken, 1)

                def take_b(n, g):
                    dve.wait_ge(pe_done, n + 1)
                    dve.tensor_tensor(b_n[:, :, :], bank[1][:, :, :], r_bc, ALU.mult).then_inc(b_taken, 1)
                    dve.wait_ge(silu_done, base + g + 1)
                    dve.wait_ge(b_taken, base + g + 1)
                    if st.f or not isinstance(g, int) or g:
                        dve.wait_ge(g_hi_done, base + g)
                    dve.tensor_tensor(prod[:, :, :], silu[:, :, :], b_n[:, :, :], ALU.mult).then_inc(prod_done, 1)

                def do_g_lo(g, half):
                    dve.wait_ge(g_hi_done, base + g + 1)
                    dve.tensor_tensor(g_lo[:, half], prod[:, :, :], g_hi[:, half].bitcast(F32), ALU.subtract)\
                        .then_inc(g_lo_done, 1)
                if st.v == 0:
                    split(n0 + 2)
                split(n0 + 3)
                if nxt.kind == "s5":
                    c_take()
                split(n0 + 4)
                stat_mean(v)
                if nxt.kind == "s5":
                    s5_angles()
                stat_diag(v)
                split(n0 + 5)
                stat_row(v)
                dve.wait_ge(r_row_ready, v + 1)
                take_a(n0 + 1, 0)
                take_b(n0 + 3, 0)
                if nxt.kind == "ple":
                    dve.wait_ge(p_hi_done, nxt.q + 1)
                    dve.tensor_tensor(p_lo[:, :, :], misc[:, :].rearrange("p (k t) -> p k t", k=2), p_hi[:, :, :].bitcast(F32),
                                      ALU.subtract).then_inc(p_lo_done, 1)

                def part(n, j):
                    split_lo(n + j, (n0 + j - 2) % RING)
                    if nxt.kind == "s5" and isinstance(n, int):
                        s5_blocks(n + j - 3 - n0)

                def group(g):
                    n = g * 6 + (n0 - 2)
                    part(n, 2)
                    do_g_lo(g - 1, 0)
                    part(n, 3)
                    part(n, 4)
                    take_a(n + 1, g)
                    part(n, 5)
                    if isinstance(g, int) and g == NG - 1:
                        take_b(n + 3, g)
                        part(n, 6)
                    else:
                        part(n, 6)
                        take_b(n + 3, g)
                        part(n, 7)
                with dve.Fori(1, NG - peeled(nxt)) as g:
                    group(g)
                for g in range(NG - peeled(nxt), NG):
                    group(g)
                n = n0 + 6 * (NG - 1) - 2
                do_g_lo(NG - 1, 1)
                part(n, 7)
                split(n + 8)
                residual_from_acc(nxt.v, nxt.u if nxt.kind != "final" else None, st.f, n + 9)

            def ple(st, nxt):
                n0, v = st.n0, nxt.v
                u = nxt.u if nxt.kind != "final" else None
                split(n0 + 2)
                split(n0 + 3)
                stat_mean(st.v)
                stat_diag(st.v)
                stat_row(st.v)
                split(n0 + 4)
                split(n0 + 5)
                dve.wait_ge(r_row_ready, st.v + 1)
                for j in range(NB):
                    dve.wait_ge(pe_done, n0 + 4 + 2 * j)
                    if st.e or j:
                        dve.wait_ge(gate_ready, st.e + j)
                    dve.tensor_tensor(a_n[:, :, :], ple_bank[j][:, :, :], r_bc, ALU.mult).then_inc(gate_taken, 1)
                    if j:
                        op_low(v, u, j - 1)
                    dve.wait_ge(gate_ready, st.e + j + 1)
                    dve.tensor_tensor(b_n[:, :, :], acc[j][:, :, :], silu[:, :, :], ALU.mult).then_inc(gated, 1)
                    dve.wait_ge(gated, st.e + j + 1)
                    dve.wait_ge(x_new, 4 * v)
                    xj = xT[:, 2 * j:2 * j + 2, :]
                    dve.tensor_tensor(xj, xj, b_n[:, :, :], ALU.add).then_inc(x_new, 1)
                    if nxt.kind == "final":
                        dve.wait_ge(x_new, 4 * v + j + 1)
                        for k in (2 * j, 2 * j + 1):
                            dve.tensor_scalar(x_scaled[:, k, :], xT[:, k, :], gain_col(nxt, k), None, ALU.mult)\
                                .then_inc(scaled, 1)
                    if j < NB - 1:
                        split(n0 + 6 + 2 * j)
                        split(n0 + 7 + 2 * j)
                split(n0 + 12)
                op_low(v, u, NB - 1)

            def s5_blocks(c):
                i, second = block_at(c)
                if i is None:
                    return
                if second:
                    dve.wait_ge(turned_done, 2 * i + 2)
                    dve.tensor_copy(w_in_state[:, 1, 4 * i:4 * i + 4].rearrange("p q t e h -> p (q t e h)"), stat[:, :])\
                        .then_inc(turned_taken, 1)
                    return
                o = within[i // 4][:, 4 * (i % 4):4 * (i % 4) + 4, :]
                kk = misc.rearrange("p (q c) -> p q c", q=4)
                dve.wait_ge(block_done, i + 1)
                dve.tensor_tensor(kk[0:32, :, 0:32], kk[0:32, :, 0:32], skip[:, 4 * i:4 * i + 4, :], ALU.add)\
                    .then_inc(block_skip, 1)
                dve.wait_ge(block_skip, i + 1)
                dve.tensor_copy(o[0:32], kk[0:32]).then_inc(block_first, 1)
                dve.tensor_copy(o[32:64, :, 32:P], kk[0:32, :, 0:P - 32]).then_inc(block_taken, 2)

            def s5(st, nxt):
                n0, zu, v, u = st.n0, st.u + 1, nxt.v, nxt.u
                scaled_u = scratch[:, 1, :].rearrange("p (k c t) -> p k c t", k=2, t=TAU)

                def place(j):
                    dve.wait_ge(pe_done, n0 + 2 * j + 2)
                    if j:
                        dve.wait_ge(u_placed, 16 * j)
                    dve.tensor_tensor(scratch[:, 1, :].rearrange("p (k t) -> p k t", k=2), bank[j % 2][:, :, :], r_bc, ALU.mult)\
                        .then_inc(u_scaled, 1)
                    dve.wait_ge(u_scaled, j + 1)
                    for quad in (0, 1):
                        for tau in range(TAU):
                            src = scaled_u[32 * quad:32 * quad + 32, :, :, tau]
                            dst = u_steps[32 * tau:32 * tau + 32, 8 * j:8 * j + 8, :]
                            dst = dst.rearrange("p (k j) c -> p k j c", k=2)[:, :, quad, :]
                            dve.tensor_copy(dst, src).then_inc(u_placed, 1)
                A, B, C, E = (t.rearrange("p a t -> p (a t)") for t in (a_n, b_n, silu, prod))
                s_re = squares[:, 0].rearrange("p a t -> p (a t)")
                zf = square_sum

                def z_low(g):
                    dve.wait_ge(op_hi_done, KD * zu + 2 * g + 2)
                    dve.tensor_tensor(z_ops[:, 1, g, 0:2, :], zf[:, :, :], z_ops[:, 0, g, 0:2, :].bitcast(F32), ALU.subtract)\
                        .then_inc(op_lo_done, 2)

                def tables(g):
                    return (t[:, QG * g:QG * g + QG, :].rearrange("p q c -> p (q c)") for t in (turn_cos, turn_sin, decay))

                def mean():
                    stat_mean(st.v)
                    stat_diag(st.v)

                def row():
                    stat_row(st.v)
                    dve.wait_ge(r_row_ready, st.v + 1)

                def turn_back(g):
                    cos, sin, _ = tables(g)
                    dve.wait_ge(turns_ready, 1)
                    x_re, x_im = x_bank(g)
                    dve.wait_ge(s_in_done, g + 1)
                    if g:
                        dve.wait_ge(state_im, g)
                        dve.wait_ge(state_re, g)
                    link(dve.tensor_tensor(A, x_re, cos, ALU.mult), wait=False)
                    link(dve.tensor_tensor(B, x_im, sin, ALU.mult), wait=False)
                    link(dve.tensor_tensor(C, x_im, cos, ALU.mult), wait=False)
                    link(dve.tensor_tensor(E, x_re, sin, ALU.mult))
                    link(dve.tensor_tensor(A, A, B, ALU.add), wait=False)
                    dve.tensor_tensor(C, C, E, ALU.subtract).then_inc(x_back, 1)

                def scan(g):
                    cos, sin, fall = tables(g)
                    dve.wait_ge(dve_step, links[0])
                    dve.tensor_tensor_scan(B, fall, A, 0.0, ALU.mult, ALU.add).then_inc(scanned, 1)
                    dve.wait_ge(x_back, g + 1)
                    dve.tensor_tensor_scan(E, fall, C, 0.0, ALU.mult, ALU.add).then_inc(scanned, 1)
                    dve.wait_ge(scanned, 2 * g + 2)
                    link(dve.tensor_tensor(A, B, cos, ALU.mult), wait=False)
                    link(dve.tensor_tensor(C, E, sin, ALU.mult))
                    if g:
                        dve.wait_ge(y_done, g)
                    dve.tensor_tensor(s_re, A, C, ALU.subtract).then_inc(state_re, 1)

                for i in range(24):
                    split(n0 + i + 2)
                    if i > 8 and GLU[i - 9][0] == OUT and GLU[i - 9][2]:
                        op_low(v, u, GLU[i - 9][1])
                    for kind, *g in DVE_WORK.get(i, []):
                        {"mean": mean, "row": row, "place": place, "back": turn_back, "scan": scan, "low": z_low}[kind](*g)
                    if i >= 8:
                        which, j, half = GLU[i - 8]
                        if half and which == OUT:
                            dve.wait_ge(pe_done, n0 + i + 1)
                            dve.wait_ge(gate_ready, st.e + j + 1)
                            y = glu_bank[OUT][j]
                            if j == NB - 1:
                                y = y.rearrange("p (k t) -> p k t", k=2)
                            dve.tensor_tensor(b_n[:, :, :], y[:, :, :], silu[:, :, :], ALU.mult).then_inc(gated, 1)
                            dve.wait_ge(gated, st.e + j + 1)
                            dve.wait_ge(x_new, 4 * v)
                            xj = xT[:, 2 * j:2 * j + 2, :]
                            dve.tensor_tensor(xj, xj, b_n[:, :, :], ALU.add).then_inc(x_new, 1)
                split(n0 + 26)
                op_low(v, u, NB - 1)

            def attention(st, nxt):
                n0, o_set = st.n0, st.u + 1

                def take_kq(j, which):
                    dve.wait_ge(pe_done, n0 + 10 + 4 * j + 2 * which)
                    dst = (kT, qT)[which][:, 2 * j:2 * j + 2, :]
                    if which:
                        op = dve.scalar_tensor_tensor(out=dst, in0=bank[1][:, :, :], scalar=SCALE, in1=r_bc,
                                                      op0=ALU.mult, op1=ALU.mult)
                    else:
                        op = dve.tensor_tensor(dst, bank[0][:, :, :], r_bc, ALU.mult)
                    op.then_inc(bank_taken, 2)

                def take_out(j):
                    xj = xT[:, 2 * j:2 * j + 2, :]
                    dve.wait_ge(x_new, 4 * nxt.v)
                    dve.tensor_tensor(xj, xj, out_bank[j][:, :, :], ALU.add).then_inc(x_new, 1)

                split(n0 + 2)
                split(n0 + 3)
                split(n0 + 4)
                stat_mean(st.v)
                stat_diag(st.v)
                split(n0 + 5)
                stat_row(st.v)
                for n in range(n0 + 6, n0 + 12):
                    split(n)
                dve.wait_ge(r_row_ready, st.v + 1)
                dve.wait_ge(bank_taken, 8)
                take_kq(0, 0)
                split(n0 + 12)
                split(n0 + 13)
                take_kq(0, 1)
                for s in range(STEPS):
                    if s < 12 and s % 2:
                        take_kq(s // 4 + 1, s // 2 % 2)
                    h = s
                    if h < NH:
                        dve.wait_ge(log_done, h + 1)
                        if h >= DEPTH:
                            dve.wait_ge(exponent_done, h - DEPTH + 1)
                        dve.scalar_tensor_tensor(out=drop[:, h % DEPTH], in0=z_bank[h % DEPTH][:, 0:HW], scalar=0.0,
                                                 in1=z_log[:, h % DEPTH], op0=ALU.max, op1=ALU.add)\
                                                     .then_inc(drop_done, 1)
                    h = s - 3
                    if 0 <= h and h % 2:
                        dve.wait_ge(op_hi_done, KD * o_set + h // 2 + 1)
                        dve.tensor_tensor(op_lo[:, HALF[o_set], h // 2, :], acc[2 + h // 2 % 2][:, 0, :],
                                          op_hi[:, HALF[o_set], h // 2, :].bitcast(F32), ALU.subtract)\
                                              .then_inc(op_lo_done, 1)
                    if s < 16:
                        split(step_chunk(st, s) + 2)
                dve.wait_ge(pe_done, n0 + 28)
                take_out(0)
                split(n0 + 30)
                op_low(nxt.v, nxt.u, 0)
                dve.wait_ge(pe_done, n0 + 29)
                take_out(1)
                split(n0 + 31)
                op_low(nxt.v, nxt.u, 1)
                dve.wait_ge(pe_done, n0 + 30)
                take_out(2)
                split(n0 + 32)
                op_low(nxt.v, nxt.u, 2)
                split(n0 + 33)
                dve.wait_ge(pe_done, n0 + 32)
                take_out(3)
                split(n0 + 34)
                op_low(nxt.v, nxt.u, 3)

            for b in range(NB):
                dve.wait_ge(x_turned, b + 1)
                dve.tensor_copy(xT[:, 2 * b:2 * b + 2, :], acc[b][:, :, :]).then_inc(x_new, 1)
            split(0)
            dve.wait_ge(gain_ready, 1)
            op_low(0, 0, 0)
            op_low(0, 0, 1)
            split(1)
            op_low(0, 0, 2)
            op_low(0, 0, 3)
            for st, nxt in zip(stages, stages[1:] + [None]):
                if st.kind[:3] == "ffn":
                    ffn(st, nxt)
                if st.kind == "s5":
                    s5(st, nxt)
                if st.kind == "ple":
                    ple(st, nxt)
                if st.kind == "attn":
                    attention(st, nxt)
                if st.kind == "final":
                    stat_mean(st.v)
                    dve.wait_ge(r_ready, st.v + 1)
                    for tb in range(TB):
                        for j in range(NB // 2):
                            dve.wait_ge(out_turned, j + 1)
                            dve.tensor_scalar(rows_in[:, tb, 256 * j:256 * j + 256], acc[j][:, tb, :], r_col[:, tb:tb + 1],
                                              None, ALU.mult).then_inc(out_rows[0], 1)

        @block.tensor
        def _(pe):
            def products(o, wh, wl, xh, xl, start, stop):
                pe.matmul(o, wh, xh, start=start, stop=False, skip_group_check=True)
                pe.matmul(o, wl, xh, start=False, stop=False, skip_group_check=True)
                return pe.matmul(o, wh, xl, start=False, stop=stop, skip_group_check=True)

            def stat_sum(v):
                pe.wait_ge(sum_ready, v + 1)
                for tb in range(TB):
                    mm = pe.matmul(stat[:, tb:tb + 1], square_sum[:, 0, tb * P:(tb + 1) * P], ones[:, 0:1],
                                   start=True, stop=True)
                mm.then_inc(sum_col, 1)

            def last_sum(v):
                pe.wait_ge(sum_ready, v + 1)
                for i, tile in enumerate((square_sum[:, 0], squares[:, 1, 0], squares[:, 1, 1])):
                    if i == 1:
                        pe.wait_ge(squared, 4 * v + 4)
                    for tb in range(TB):
                        mm = pe.matmul(stat[:, tb:tb + 1], tile[:, tb * P:(tb + 1) * P], ones[:, 0:1],
                                       start=i == 0 and tb == 0, stop=i == 2, skip_group_check=True)
                mm.then_inc(sum_col, 1)

            def stat_spread(v):
                for tb in range(TB):
                    pe.wait_ge(diag_ready, TB * v + tb + 1)
                    mm = pe.matmul(stat[:, 256 + tb * P:256 + (tb + 1) * P], ones[:, :], r_diag[:, tb, :],
                                   start=True, stop=True)
                mm.then_inc(r_spread, 1)

            def chunk_a(n, slot, half, o, u, ready=True, hooks={}, kks=range(4)):
                pe.wait_ge(lo_done, n + 1)
                for kk in kks:
                    k = 4 * half + kk
                    if not ready:
                        pe.wait_ge(op_lo_done, KD * u + k + 1)
                    for m in range(2):
                        wh, wl = (w[:, slot, (kk * 2 + m) * P:(kk * 2 + m + 1) * P] for w in (w_hi, w_lo))
                        mm = products(o[:, m, :], wh, wl, *operand(u, k), k == 0 and m == 0, k == KD - 1)
                    if kk == 3:
                        mm.then_inc(pe_done, 1)
                    if k in hooks:
                        hooks[k]()

            def open_acc():
                for b in range(NB):
                    pe.matmul(acc[b][:, 0, 0:2], zeros_b[:, :], zeros_b[:, 0:2], start=True, stop=True,
                              skip_group_check=True)

            def group(n, o, u, **kw):
                for half in range(2):
                    chunk_a(n + half, (n + half) % RING, half, o, u, **kw)

            def ple(st):
                n0, u = st.n0, st.u
                pe.wait_ge(p_lo_done, st.q + 1)
                for kt in range(2):
                    pe.wait_ge(lo_done, n0 + kt + 1)
                    for m in range(KD):
                        if kt == 0 and m % 2 == 0:
                            pe.wait_ge(x_new, 4 * st.v + m // 2 + 1)
                        wh, wl = (w[:, (n0 + kt) % RING, m * P:(m + 1) * P] for w in (w_hi, w_lo))
                        mm = products(acc[m // 2][:, m % 2, :], wh, wl, p_hi[:, kt, :], p_lo[:, kt, :],
                                      kt == 0 and m % 2 == 0, kt == 1)
                    mm.then_inc(pe_done, 1)
                group(n0 + 2, ple_bank[0], u, ready=False, hooks={1: lambda: stat_sum(st.v), 3: lambda: stat_spread(st.v)})
                group(n0 + 4, ple_bank[1], u)
                group(n0 + 6, ple_bank[2], u)
                pe.wait_ge(gate_taken, 4 * st.q + 2)
                group(n0 + 8, ple_bank[3], u)

            def s5_turn():
                pe.wait_ge(s5_landed, 16 * 4)
                pe.wait_ge(rows_spread, 1)
                for i in range(3):
                    pe.transpose(misc[:, P + NQ * i:P + NQ * (i + 1)], s5_rows[:, i, :], ident[0:NQ, 0:NQ])
                pe.transpose(misc[0:2 * H, P + NQ * 3:P + NQ * 4], s5_rows[:, 3, 0:2 * H], ident[0:NQ, 0:NQ])\
                    .then_inc(s5_turned, 1)
                pe.wait_ge(c_landed, 16 * 2)
                for k in range(KD):
                    mm = pe.transpose(acc[k // 4].rearrange("p a t -> p (a t)")[:, P * (k % 4):P * (k % 4) + P],
                                      c_rows[:, k].rearrange("p i s -> p (i s)"), ident[:, :])
                    if k % 4 == 3:
                        mm.then_inc(c_turned, 1)

            def s5_blocks(c):
                i, second = block_at(c)
                if i is None:
                    return
                if i == 0:
                    pe.wait_ge(weights_ready, 1)
                if not second:
                    pe.wait_ge(block_taken, 4 * i)
                    pe.wait_ge(turned_taken, 2 * i)
                    for q in range(4):
                        for part in range(2):
                            lhs = w_in_state[:, part, 4 * i + q, TAU - 1, :, :].rearrange("p e h -> p (e h)")
                            rhs = w_state_out[:, part, 4 * i + q, 0:TAU].rearrange("p t e h -> p (t e h)")
                            mm = pe.matmul(misc[0:32, P * q:P * q + P], lhs, rhs, start=part == 0, stop=part == 1)
                    mm.then_inc(block_done, 1)
                pe.wait_ge(turned_taken, 2 * i + second)
                for q in range(4):
                    mm = pe.transpose(stat[:, P * q:P * q + P], w_in_state[:, second, 4 * i + q].rearrange("p t e h -> p (t e h)"),
                                      ident[:, :])
                mm.then_inc(turned_done, 1)

            def s5(st):
                n0, u = st.n0, st.u
                pe.wait_ge(block_taken, 32)
                pe.wait_ge(turned_taken, 16)

                def state_in(g, part):
                    if part == 0:
                        pe.wait_ge(u_placed, 16 * (g + 1))
                        if 0 < g < NB - 1:
                            pe.wait_ge(x_back, g)
                    o = x_bank(g)[part]
                    for q in range(QG):
                        w = w_in_state[:, part, QG * g + q].rearrange("p t e h -> p (t e h)")
                        mm = pe.matmul(o[:, NC * q:NC * q + NC], w, u_steps[:, QG * g + q, :], start=True, stop=True)
                    if part:
                        mm.then_inc(s_in_done, 1)

                def step_out(g):
                    pe.wait_ge(r_row_ready, st.v + 1)
                    if g == 2:
                        pe.wait_ge(gelu_done, 16)
                    if g == 3:
                        pe.wait_ge(x_back, 3)
                    for q in range(QG):
                        qq = QG * g + q
                        pe.matmul(y_bank[g][:, NC * q:NC * q + NC], within[qq // 16][:, qq % 16, :], u_steps[:, qq, :],
                                  start=q == 0, stop=False, skip_group_check=True)

                def state_out(g, part):
                    pe.wait_ge((state_re, state_im)[part], g + 1)
                    states = squares[:, part].rearrange("p a t -> p (a t)")
                    for q in range(QG):
                        w = w_state_out[:, part, QG * g + q, 1:TAU + 1].rearrange("p t e h -> p (t e h)")
                        mm = pe.matmul(y_bank[g][:, NC * q + 1:NC * q + NC], w, states[:, NC * q:NC * q + NC - 1], start=False,
                                       stop=part == 1, skip_group_check=True)
                    if part:
                        mm.then_inc(y_done, 1)

                work = {"in": state_in, "step": step_out, "out": state_out}

                def between(i, k):
                    for kind, *which in BETWEEN.get((i, k), []):
                        work[kind](*which)

                def at(i):
                    h = 4 * (i % 2) if i < 8 else 4 * GLU[i - 8][2]
                    hooks = {h + k: lambda k=k: between(i, k) for k in range(4)}
                    if i == 1:
                        hooks = {h + 3: lambda: stat_sum(st.v)}
                    if i == 2:
                        hooks = {h + 1: lambda: stat_spread(st.v)}
                    return hooks
                for i in range(24):
                    n = n0 + i
                    if i < 8:
                        if i >= 4 and i % 2 == 0:
                            pe.wait_ge(u_scaled, i // 2 - 1)
                        chunk_a(n, n % RING, i % 2, bank[i // 2 % 2], u, ready=i >= 2,
                                hooks=at(i))
                    else:
                        which, j, half = GLU[i - 8]
                        if which == GATE and j < 2 and half == 0:
                            pe.wait_ge(u_scaled, 3 + j)
                        if (which, j) in ((OUT, 1), (GATE, 2)) and half == 0:
                            pe.wait_ge(x_back, 4)
                        pe.wait_ge(op_lo_done, KD * (u + 1) + 4 * (half + 1))
                        o = glu_bank[which][j]
                        if j == NB - 1:
                            o = o.rearrange("p (k t) -> p k t", k=2)
                        chunk_a(n, n % RING, half, o, u + 1, hooks=at(i))

            def head_step(s):
                h = s
                if h < NH:
                    j, q0 = h // 2, DH * (h % 2)
                    zb = z_bank[h % DEPTH]
                    pe.wait_ge(bank_taken, 8 + 4 * (h // 4 + 1))
                    if h >= DEPTH:
                        pe.wait_ge(att_done, h - DEPTH + 1)
                    pe.matmul(zb[:, 0:T], kT[q0:q0 + DH, j, 0:P], qT[q0:q0 + DH, j, :], start=True, stop=True,
                              skip_group_check=True)
                    pe.matmul(zb[:, T:HW], kT[q0:q0 + DH, j, P:T], qT[q0:q0 + DH, j, P:T], start=False, stop=True,
                              skip_group_check=True).then_inc(z_done, 1)
                h = s - 2
                if 0 <= h < NH:
                    zb = z_bank[h % DEPTH]
                    pe.wait_ge(drop_masked, 2 * h + 2)
                    d = drop[:, h % DEPTH]

                    def add(o, a, b):
                        return pe.matmul(o, a, b, start=False, stop=True, skip_group_check=True)
                    add(zb[:, 0:T], minus_tri[:, :], d[:, 0:T])
                    add(zb[:, P:T], minus_ones[:, :], d[:, T:HW])
                    add(zb[:, T:HW], minus_tri[:, :], d[:, T:HW])
                    add(zb[:, 0:P], ident_b[:, :], masked_b[:, :])
                    add(zb[:, T:HW], ident_b[:, :], masked_b[:, :]).then_inc(exponent_done, 1)
                h = s - 3
                if 0 <= h:
                    j, q0 = h // 2, DH * (h % 2)
                    o = acc[2 + j % 2][q0:q0 + DH, 0, :]
                    pe.wait_ge(att_done, h + 1)
                    if j >= 2 and h % 2 == 0:
                        pe.wait_ge(op_lo_done, KD * o_set[0] + j - 1)
                    pe.matmul(o, val[:, 0, h * DH:(h + 1) * DH], att[:, h % DEPTH, 0:T], start=True, stop=True,
                              skip_group_check=True)
                    pe.matmul(o[:, P:T], val[:, 1, h * DH:(h + 1) * DH], att[:, h % DEPTH, T:HW], start=False, stop=True,
                              skip_group_check=True).then_inc(o_done, 1)

            o_set = [0]

            def attention(st):
                n0, u = st.n0, st.u
                o_set[0] = u + 1
                for j in range(NB):
                    if j >= 2:
                        pe.wait_ge(bank_taken, 2 * j - 2)
                    for half in range(2):
                        n = n0 + 2 * j + half
                        pe.wait_ge(lo_done, n + 1)
                        for kk in range(4):
                            k = 4 * half + kk
                            if j == 0:
                                pe.wait_ge(op_lo_done, KD * u + k + 1)
                            wh, wl = (w[:, n % RING, kk * 256:(kk + 1) * 256] for w in (w_hi, w_lo))
                            for tb in range(TB):
                                xh, xl = (o[:, HALF[u], k, tb * P:(tb + 1) * P] for o in (op_hi, op_lo))
                                start = k == 0 and tb == 0
                                pe.matmul(bank[j % 2][:, tb, :], xh, wh, start=start, stop=False, skip_group_check=True)
                                pe.matmul(bank[j % 2][:, tb, :], xh, wl, start=False, stop=False, skip_group_check=True)
                                mm = pe.matmul(bank[j % 2][:, tb, :], xl, wh, start=False, stop=k == KD - 1,
                                               skip_group_check=True)
                            if kk == 3:
                                mm.then_inc(pe_done, 1)
                            if j == 1 and k == 0:
                                stat_sum(st.v)
                            if j == 1 and k == 6:
                                stat_spread(st.v)
                pe.wait_ge(bank_taken, 6)
                group(n0 + 8, bank[0], u)
                pe.wait_ge(bank_taken, 8)
                group(n0 + 10, bank[1], u)
                for s in range(STEPS):
                    if s < 12:
                        if s % 2 == 0:
                            pe.wait_ge(bank_taken, 8 + 4 * (s // 4) + 2 + 2 * (s // 2 % 2))
                        n = n0 + 12 + s
                        chunk_a(n, n % RING, s % 2, bank[s // 2 % 2], u)
                    elif s < 18:
                        n = n0 + 12 + s
                        j, half = OUT_ORDER[s - 12]
                        if s == 15:
                            chunk_a(n - 1, (n - 1) % RING, 0, out_bank[2], u + 1, kks=range(2, 4))
                        if half == 0:
                            pe.wait_ge(bank_taken, (22, 24, 24)[j])
                        pe.wait_ge(op_lo_done, KD * (u + 1) + 4 + 2 * half)
                        chunk_a(n, n % RING, half, out_bank[j], u + 1, kks=range(2 if s >= 14 else 4))
                    head_step(s)
                for i, (j, half) in enumerate(OUT_ORDER[3:]):
                    n = n0 + 27 + i
                    if j == 3 and half == 0:
                        pe.wait_ge(att_done, NH)
                    chunk_a(n, n % RING, half, out_bank[j], u + 1, ready=False, kks=range(2 if i < 3 else 0, 4))

            def ffn(st, nxt):
                n0, base, v, u = st.n0, NG * st.f, st.v, st.u

                def up(n, s, which, **kw):
                    for half in range(2):
                        chunk_a(n + half, (s + half) % RING, half, bank[which], u, **kw)
                        behind(n + half)

                def down_tile(s, m, j, half):
                    wh, wl = (w[:, (s + j) % RING, m * P:(m + 1) * P] for w in (w_hi, w_lo))
                    return products(acc[m // 2][:, m % 2, :], wh, wl, g_hi[:, half, j, :], g_lo[:, half, j, :], False, False)

                def behind(n):
                    if nxt.kind == "s5" and isinstance(n, int):
                        s5_blocks(n - n0)

                def down(n, s, half):
                    for j in range(2):
                        pe.wait_ge(lo_done, n + j + 1)
                        for m in range(KD):
                            mm = down_tile(s, m, j, half)
                        mm.then_inc(pe_done, 1)
                        behind(n + j)
                if st.v:
                    pe.wait_ge(x_new, 4 * v)
                    if st.q:
                        pe.wait_ge(gate_taken, 4 * st.q - 3)
                if st.e:
                    pe.wait_ge(gate_ready, st.e - 3)
                up(n0, n0, 0, ready=False, hooks={3: s5_turn} if nxt.kind == "s5" else {})
                pe.wait_ge(x_new, 4 * v + 4)
                if nxt.kind == "ple":
                    pe.wait_ge(p_landed, 16 * (nxt.q + 1))
                    pe.wait_ge(gain_ready, 1)
                    for kt in range(2):
                        for tb in range(TB):
                            mm = pe.transpose(misc[:, kt * T + tb * P:kt * T + (tb + 1) * P],
                                              p_rows[:, tb, kt * P:(kt + 1) * P], ident[:, :])
                    mm.then_inc(p_turned, 1)
                if st.f:
                    pe.wait_ge(b_taken, base)
                if st.e:
                    pe.wait_ge(gate_ready, st.e - 2)
                    if st.q:
                        pe.wait_ge(gate_taken, 4 * st.q)
                up(n0 + 2, n0 + 2, 1, hooks={0: lambda: stat_sum(v), 6 if nxt.kind == "s5" else 4: lambda: stat_spread(v)})
                if nxt.kind == "s5":
                    pe.wait_ge(c_ready, 2)
                open_acc()

                def whole(g):
                    n, s = g * 6 + (n0 - 2), n0 + 4
                    pe.wait_ge(a_taken, g + base)
                    up(n, s, 0)
                    pe.wait_ge(b_taken, g + base)
                    up(n + 2, s + 2, 1)
                    pe.wait_ge(g_lo_done, g + base)
                    down(n + 4, s + 4, 0)
                with pe.Fori(1, NG - peeled(nxt)) as g:
                    whole(g)
                for g in range(NG - peeled(nxt), NG):
                    whole(g)
                n = n0 + 6 * (NG - 1) - 2
                pe.wait_ge(g_lo_done, base + NG)
                pe.wait_ge(lo_done, n + 8)
                for m in range(KD):
                    for j in range(2):
                        mm = down_tile(n + 6, m, j, 1)
                    if m % 2:
                        mm.then_inc(acc_done, 1)
                if nxt.kind == "s5":
                    pe.wait_ge(block_taken, 32)
                if nxt.kind == "ple":
                    pe.wait_ge(p_lo_done, nxt.q + 1)
                pe.matmul(misc[:, 0:2], zeros_b[:, :], zeros_b[:, 0:2], start=True, stop=True).then_inc(pe_done, 2)

            pe.wait_ge(consts_ready, 5)
            pe.wait_ge(rows_landed, 16 * TB)
            for k in range(KD):
                for tb in range(TB):
                    mm = pe.transpose(acc[k // 2][:, k % 2, tb * P:(tb + 1) * P], rows_in[:, tb, k * P:(k + 1) * P],
                                      ident[:, :])
                if k % 2:
                    mm.then_inc(x_turned, 1)
            pe.wait_ge(gains_landed, 16 * 5)
            R = 9 * KD
            pe.transpose(misc[:, 0:R], gain_rows[0:R, :], ident[0:R, 0:R]).then_inc(gain_turned, 1)
            pe.wait_ge(masks_made, 7)
            for st, nxt in zip(stages, stages[1:] + [None]):
                if st.kind[:3] == "ffn":
                    ffn(st, nxt)
                if st.kind == "s5":
                    s5(st)
                if st.kind == "ple":
                    ple(st)
                if st.kind == "attn":
                    attention(st)
                if st.kind == "final":
                    for j in range(NB):
                        if j == NB - 1:
                            last_sum(st.v)
                        pe.wait_ge(scaled, 2 * j + 2)
                        for tb in range(TB):
                            for k in range(2):
                                mm = pe.transpose(acc[j][:, tb, k * P:(k + 1) * P], x_scaled[:, 2 * j + k, tb * P:(tb + 1) * P],
                                                  ident[:, :])
                        mm.then_inc(out_turned, 1)


_INS = ['x', 'p', 'ffn1_norm', 'ffn1_w1', 'ffn1_w3', 'ffn1_w2', 'mix_norm', 'ffn2_norm', 'ffn2_w1', 'ffn2_w3',
        'ffn2_w2', 'ple_norm', 'ple_proj', 'ple_gate', 's5_w_in', 's5_a_re', 's5_a_im', 's5_log_dt', 's5_b_re',
        's5_b_im', 's5_c_re', 's5_c_im', 's5_d', 's5_w_glu', 'sb_w_qkv', 'sb_w_o', 'final_norm']
_OUTS = [((1, 256, 1024), 'float32')]


def kernel(**inputs):
    import numpy as _np
    import concourse.bacc as _bacc
    from concourse import mybir as _mybir
    from concourse.bass_utils import run_bass_kernel_spmd as _run

    nc = _bacc.Bacc("TRN2", target_bir_lowering=False, num_devices=1)
    arrays, args = {}, []
    for name in _INS:
        a = _np.ascontiguousarray(inputs[name])
        arrays[f"in_{name}_dram"] = a
        args.append(nc.dram_tensor(f"in_{name}_dram", a.shape, _mybir.dt.from_np(a.dtype), kind="ExternalInput").ap())
    for i, (shape, dtype) in enumerate(_OUTS):
        dt = _mybir.dt.from_np(_np.dtype(dtype))
        args.append(nc.dram_tensor(f"out_{i}_dram", shape, dt, kind="ExternalOutput").ap())
    hybrid_trunk(nc, *args)
    r = _run(nc, [arrays], core_ids=[0])
    got = tuple(r.results[0][f"out_{i}_dram"] for i in range(len(_OUTS)))
    return got[0]
```
